# Optimizing a Trainium2 kernel written in Bass

```python
import functools
import jax, jax.numpy as jnp
from jax import lax
import numpy as np

D_MODEL = 1024
BATCH = 1
SEQ = 512
DEPTH = 1
DEC_BATCH = 8
DEC_SEQ = 1
PAST_LEN = 2048
PAGE_SIZE = 128

HEAD_DIM = 64
HEADS_A = 8
DILATED_CONFIGS = ((128, 1), (512, 4), (2048, 16))
WINDOW_A = 2048
HEADS_B = 8
KV_HEADS_B = 2
GROUP_B = HEADS_B // KV_HEADS_B
WINDOW_B = 128
BLOCK = 128
ROPE_THETA = 10000.0
NORM_EPS = 1e-6
NEG_INF = -1e30
SCALE = HEAD_DIM ** -0.5

WIDTH_A = HEADS_A * HEAD_DIM
WIDTH_B = HEADS_B * HEAD_DIM
KV_WIDTH_B = KV_HEADS_B * HEAD_DIM
IN_WIDTHS = (WIDTH_A, WIDTH_A, WIDTH_A, WIDTH_B, KV_WIDTH_B, KV_WIDTH_B, D_MODEL, D_MODEL)
D_IN = sum(IN_WIDTHS)
SPLIT_POINTS = tuple(int(v) for v in np.cumsum(IN_WIDTHS)[:-1])

N_KEYS = 128
N_EXPERTS = N_KEYS * N_KEYS
PEER_HEADS = 8
PEER_TOPK = 16
PEER_HALF = 128
PEER_QUERY_DIM = 2 * PEER_HALF
PEER_CHUNK = 128

kernel_name = 'hybrid_dilated_swa_peer_step'

def rms_norm(x, g):
    xf = x.astype(jnp.float32)
    y = xf * lax.rsqrt(jnp.mean(xf * xf, axis=-1, keepdims=True) + NORM_EPS)
    return (y * g.astype(jnp.float32)).astype(x.dtype)

def rotary(x, pos):
    inv = ROPE_THETA ** (-jnp.arange(0, HEAD_DIM, 2, dtype=jnp.float32) / HEAD_DIM)
    ang = pos.astype(jnp.float32)[:, None] * inv[None, :]
    cos, sin = jnp.cos(ang)[:, None, :], jnp.sin(ang)[:, None, :]
    x1, x2 = jnp.split(x.astype(jnp.float32), 2, axis=-1)
    return jnp.concatenate([x1 * cos - x2 * sin, x2 * cos + x1 * sin], axis=-1).astype(x.dtype)

def masked_softmax(s, mask, sink):
    s = jnp.where(mask, s, NEG_INF)
    m = s.max(axis=-1)
    if sink is not None:
        m = jnp.maximum(m, sink)
    e = jnp.exp(s - m[..., None])
    denom = e.sum(axis=-1)
    if sink is not None:
        denom = denom + jnp.exp(sink - m)
    return e / denom[..., None], m + jnp.log(denom)

def band_attention(q, k, v, window, sink):
    n, L, kvh, g, dh = q.shape
    nb = -(-L // BLOCK)
    pad = nb * BLOCK - L
    qb = jnp.pad(q, ((0, 0), (0, pad), (0, 0), (0, 0), (0, 0))).reshape(n, nb, BLOCK, kvh, g, dh)
    kp = jnp.pad(k, ((0, 0), (BLOCK, pad), (0, 0), (0, 0))).reshape(n, nb + 1, BLOCK, kvh, dh)
    vp = jnp.pad(v, ((0, 0), (BLOCK, pad), (0, 0), (0, 0))).reshape(n, nb + 1, BLOCK, kvh, dh)
    kw = jnp.concatenate([kp[:, :-1], kp[:, 1:]], axis=2)
    vw = jnp.concatenate([vp[:, :-1], vp[:, 1:]], axis=2)
    s = jnp.einsum('nbqkgd,nbckd->nbkgqc', qb, kw, preferred_element_type=jnp.float32) * SCALE
    a = jnp.arange(BLOCK)[:, None]
    c = jnp.arange(2 * BLOCK)[None, :]
    off = BLOCK + a - c
    kpos = jnp.arange(nb)[:, None, None] * BLOCK + c[None] - BLOCK
    mask = ((off >= 0) & (off <= window))[None] & (kpos >= 0)
    p, lse = masked_softmax(s, mask[None, :, None, None], sink)
    o = jnp.einsum('nbkgqc,nbckd->nbqkgd', p.astype(vw.dtype), vw, preferred_element_type=jnp.float32)
    o = o.reshape(n, nb * BLOCK, kvh, g, dh)[:, :L].astype(q.dtype)
    lse = lse.transpose(0, 1, 4, 2, 3).reshape(n, nb * BLOCK, kvh, g)[:, :L]
    return o, lse

def gathered_attention(q, kc, vc, idx, sink):
    valid = idx >= 0
    safe = jnp.maximum(idx, 0)
    kg = jnp.take(kc, safe, axis=1)
    vg = jnp.take(vc, safe, axis=1)
    s = jnp.einsum('nskgd,nsjkd->nskgj', q, kg, preferred_element_type=jnp.float32) * SCALE
    p, lse = masked_softmax(s, valid[None, :, None, None, :], sink)
    o = jnp.einsum('nskgj,nsjkd->nskgd', p.astype(vg.dtype), vg, preferred_element_type=jnp.float32)
    return o.astype(q.dtype), lse

def to_strided(x, d):
    n, L = x.shape[:2]
    rest = x.shape[2:]
    return x.reshape(n, L // d, d, *rest).swapaxes(1, 2).reshape(n * d, L // d, *rest)

def from_strided(x, d):
    nd, Ld = x.shape[:2]
    rest = x.shape[2:]
    n = nd // d
    return x.reshape(n, d, Ld, *rest).swapaxes(1, 2).reshape(n, Ld * d, *rest)

def combine_by_denominator(outs, lses):
    w = jax.nn.softmax(jnp.stack(lses).astype(jnp.float32), axis=0)
    o = jnp.einsum('cnshg,cnshgd->nshgd', w, jnp.stack(outs).astype(jnp.float32))
    return o.astype(outs[0].dtype)

def prompt_mixers(qa, ka, va, qb, kb, vb, sink):
    s = qa.shape[1]
    outs, lses = [], []
    for window, dil in DILATED_CONFIGS:
        o, lse = band_attention(to_strided(qa, dil), to_strided(ka, dil), to_strided(va, dil),
                                window // dil, None)
        outs.append(from_strided(o, dil))
        lses.append(from_strided(lse, dil))
    oa = combine_by_denominator(outs, lses)
    ob, _ = band_attention(qb, kb, vb, WINDOW_B, sink[:, :, None])
    keep_a = min(WINDOW_A, s)
    keep_b = min(WINDOW_B, s)
    state = (ka[:, s - keep_a:], va[:, s - keep_a:], kb[:, s - keep_b:], vb[:, s - keep_b:])
    return oa, ob, state

def sample_mixers(qa, ka, va, qb, kb, vb, sink, ck_a, cv_a, ck_b, cv_b):
    s = qa.shape[1]
    kca = jnp.concatenate([ck_a, ka], axis=1)
    vca = jnp.concatenate([cv_a, va], axis=1)
    qi_a = ck_a.shape[1] + jnp.arange(s)
    outs, lses = [], []
    for window, dil in DILATED_CONFIGS:
        idx = qi_a[:, None] - dil * jnp.arange(window // dil + 1)[None, :]
        o, lse = gathered_attention(qa, kca, vca, idx, None)
        outs.append(o)
        lses.append(lse)
    oa = combine_by_denominator(outs, lses)
    kcb = jnp.concatenate([ck_b, kb], axis=1)
    vcb = jnp.concatenate([cv_b, vb], axis=1)
    qi_b = ck_b.shape[1] + jnp.arange(s)
    idx_b = qi_b[:, None] - jnp.arange(WINDOW_B + 1)[None, :]
    ob, _ = gathered_attention(qb, kcb, vcb, idx_b, sink)
    ma, mb = kca.shape[1], kcb.shape[1]
    keep_a = min(WINDOW_A, ma)
    keep_b = min(WINDOW_B, mb)
    state = (kca[:, ma - keep_a:], vca[:, ma - keep_a:], kcb[:, mb - keep_b:], vcb[:, mb - keep_b:])
    return oa, ob, state

def peer(xn, w_q, sub_keys, u_tab, v_tab):
    t = xn.shape[0]
    q = (xn @ w_q).reshape(t, PEER_HEADS, 2, PEER_HALF)
    s = jnp.einsum('thpc,pnc->thpn', q, sub_keys, preferred_element_type=jnp.float32)
    top_s, top_i = lax.top_k(s, PEER_TOPK)
    cand_s = (top_s[:, :, 0, :, None] + top_s[:, :, 1, None, :]).reshape(t, PEER_HEADS, PEER_TOPK ** 2)
    cand_e = (top_i[:, :, 0, :, None] * N_KEYS + top_i[:, :, 1, None, :]).reshape(t, PEER_HEADS, PEER_TOPK ** 2)
    best_s, best_j = lax.top_k(cand_s, PEER_TOPK)
    experts = jnp.take_along_axis(cand_e, best_j, axis=-1).reshape(t, PEER_HEADS * PEER_TOPK)
    gates = jax.nn.softmax(best_s, axis=-1).reshape(t, PEER_HEADS * PEER_TOPK)
    pad = (-t) % PEER_CHUNK
    nc = (t + pad) // PEER_CHUNK
    xp = jnp.pad(xn, ((0, pad), (0, 0))).reshape(nc, PEER_CHUNK, D_MODEL)
    ep = jnp.pad(experts, ((0, pad), (0, 0))).reshape(nc, PEER_CHUNK, PEER_HEADS * PEER_TOPK)
    gp = jnp.pad(gates, ((0, pad), (0, 0))).reshape(nc, PEER_CHUNK, PEER_HEADS * PEER_TOPK)

    def expert_block(args):
        xb, eb, gb = args
        u = jnp.take(u_tab, eb, axis=0)
        act = jax.nn.gelu(jnp.einsum('cd,ced->ce', xb, u, preferred_element_type=jnp.float32),
                          approximate=False)
        v = jnp.take(v_tab, eb, axis=0)
        out = jnp.einsum('ce,ced->cd', (gb * act).astype(v.dtype), v, preferred_element_type=jnp.float32)
        return out.astype(xb.dtype)

    out = lax.map(expert_block, (xp, ep, gp))
    return out.reshape(nc * PEER_CHUNK, D_MODEL)[:t]

def trunk_layer(x, pos, mix_fn, g_mix, w_in, w_a, w_b, w_o, g_ffn, w_pq, sub_keys, u_tab, v_tab):
    n, s, _ = x.shape
    xn = rms_norm(x, g_mix)
    z = xn @ w_in
    qa, ka, va, qb, kb, vb, ga, gb = jnp.split(z, SPLIT_POINTS, axis=-1)
    qa = rotary(qa.reshape(n, s, HEADS_A, HEAD_DIM), pos).reshape(n, s, HEADS_A, 1, HEAD_DIM)
    ka = rotary(ka.reshape(n, s, HEADS_A, HEAD_DIM), pos)
    va = va.reshape(n, s, HEADS_A, HEAD_DIM)
    qb = rotary(qb.reshape(n, s, HEADS_B, HEAD_DIM), pos).reshape(n, s, KV_HEADS_B, GROUP_B, HEAD_DIM)
    kb = rotary(kb.reshape(n, s, KV_HEADS_B, HEAD_DIM), pos)
    vb = vb.reshape(n, s, KV_HEADS_B, HEAD_DIM)
    oa, ob, state = mix_fn(qa, ka, va, qb, kb, vb)
    ya = oa.reshape(n, s, WIDTH_A) @ w_a
    yb = ob.reshape(n, s, WIDTH_B) @ w_b
    merged = jax.nn.sigmoid(ga) * ya + jax.nn.sigmoid(gb) * yb
    h = x + merged @ w_o
    hn = rms_norm(h, g_ffn)
    y = h + peer(hn.reshape(n * s, D_MODEL), w_pq, sub_keys, u_tab, v_tab).reshape(n, s, D_MODEL)
    return y, state

def setup_inputs(seed: int = 0) -> dict:
    key = jax.random.key(seed)
    ks = jax.random.split(key, 20)

    def nrm(k, shape, scale):
        return jax.random.normal(k, shape, jnp.float32) * scale

    win_a = min(WINDOW_A, PAST_LEN)
    win_b = min(WINDOW_B, PAST_LEN)
    return {
        'x_prompt': nrm(ks[0], (BATCH, SEQ, D_MODEL), 1.0),
        'x_sample': nrm(ks[1], (DEC_BATCH, DEC_SEQ, D_MODEL), 1.0),
        'cache_a_k': nrm(ks[2], (DEPTH, DEC_BATCH, win_a, HEADS_A, HEAD_DIM), 1.0),
        'cache_a_v': nrm(ks[3], (DEPTH, DEC_BATCH, win_a, HEADS_A, HEAD_DIM), 1.0),
        'cache_b_k': nrm(ks[4], (DEPTH, DEC_BATCH, win_b, KV_HEADS_B, HEAD_DIM), 1.0),
        'cache_b_v': nrm(ks[5], (DEPTH, DEC_BATCH, win_b, KV_HEADS_B, HEAD_DIM), 1.0),
        'norm_mix': 1.0 + nrm(ks[6], (DEPTH, D_MODEL), 0.1),
        'w_in': nrm(ks[7], (DEPTH, D_MODEL, D_IN), D_MODEL ** -0.5),
        'w_branch_a': nrm(ks[8], (DEPTH, WIDTH_A, D_MODEL), WIDTH_A ** -0.5),
        'w_branch_b': nrm(ks[9], (DEPTH, WIDTH_B, D_MODEL), WIDTH_B ** -0.5),
        'w_out': nrm(ks[10], (DEPTH, D_MODEL, D_MODEL), D_MODEL ** -0.5),
        'sink_b': nrm(ks[11], (DEPTH, HEADS_B), 0.5),
        'norm_ffn': 1.0 + nrm(ks[12], (DEPTH, D_MODEL), 0.1),
        'w_peer_q': nrm(ks[13], (DEPTH, D_MODEL, PEER_HEADS * PEER_QUERY_DIM), D_MODEL ** -0.5),
        'peer_sub_keys': nrm(ks[14], (DEPTH, 2, N_KEYS, PEER_HALF), PEER_HALF ** -0.5),
        'peer_u': nrm(ks[15], (DEPTH, N_EXPERTS, D_MODEL), D_MODEL ** -0.5),
        'peer_v': nrm(ks[16], (DEPTH, N_EXPERTS, D_MODEL), 0.5),
        'norm_final': 1.0 + nrm(ks[17], (D_MODEL,), 0.1),
    }

def reference(x_prompt, x_sample, cache_a_k, cache_a_v, cache_b_k, cache_b_v, norm_mix, w_in,
              w_branch_a, w_branch_b, w_out, sink_b, norm_ffn, w_peer_q, peer_sub_keys, peer_u,
              peer_v, norm_final):
    pos_p = jnp.arange(x_prompt.shape[1])
    pos_s = PAST_LEN + jnp.arange(x_sample.shape[1])
    hp, hs = x_prompt, x_sample
    new_p = ([], [], [], [])
    new_s = ([], [], [], [])
    for l in range(DEPTH):
        weights = (norm_mix[l], w_in[l], w_branch_a[l], w_branch_b[l], w_out[l], norm_ffn[l],
                   w_peer_q[l], peer_sub_keys[l], peer_u[l], peer_v[l])
        sink = sink_b[l].astype(jnp.float32).reshape(KV_HEADS_B, GROUP_B)
        hp, st_p = trunk_layer(hp, pos_p, functools.partial(prompt_mixers, sink=sink), *weights)
        hs, st_s = trunk_layer(hs, pos_s,
                               functools.partial(sample_mixers, sink=sink, ck_a=cache_a_k[l],
                                                 cv_a=cache_a_v[l], ck_b=cache_b_k[l],
                                                 cv_b=cache_b_v[l]),
                               *weights)
        for lst, arr in zip(new_p, st_p):
            lst.append(arr)
        for lst, arr in zip(new_s, st_s):
            lst.append(arr)
    y_prompt = rms_norm(hp, norm_final)
    y_sample = rms_norm(hs, norm_final)
    a_k_p, a_v_p, b_k_p, b_v_p = [jnp.stack(lst) for lst in new_p]
    a_k_s, a_v_s, b_k_s, b_v_s = [jnp.stack(lst) for lst in new_s]
    return (y_prompt, y_sample, a_k_p, a_v_p, b_k_p, b_v_p, a_k_s, a_v_s, b_k_s, b_v_s)


_drawn_inputs = setup_inputs


def setup_inputs(seed=0):
    import zlib

    import numpy as np

    out = dict(_drawn_inputs(seed))
    spreads = {}
    factors = {'sink_b': 7.301}
    for name, (base, spread) in spreads.items():
        noise = np.random.default_rng([zlib.crc32(name.encode()), seed]).standard_normal(out[name].shape)
        drawn = base * np.exp(spread * noise) if base else spread * noise
        out[name] = __import__('jax').numpy.asarray(drawn.astype(out[name].dtype))
    for name, factor in factors.items():
        out[name] = (out[name] * factor).astype(out[name].dtype)
    return out
```

```python
import numpy as np
import concourse.bass as bass
from concourse import mybir
from contextlib import ExitStack, contextmanager

P = 128
D = 1024
KO = D // P
SEQ, DEC, PAST = 512, 8, 2048
TILES = SEQ // P
SAMPLE = TILES
ALL = TILES + 1
HD, HA, HB, KVB = 64, 8, 8, 2
WA, WB, WK = HA * HD, HB * HD, KVB * HD
QA, KA, VA, QB, KB, VB = 0, WA, 2 * WA, 3 * WA, 3 * WA + WB, 3 * WA + WB + WK
ZW = 3 * WA + WB + 2 * WK
D_IN = ZW + 2 * D
SCALE = HD ** -0.5
NEG = -1e30
EPS = 1e-6
CHUNK = 512
NK, PH, TOPK = 128, 8, 16
SLOTS = PH * TOPK
LISTS = 2 * PH
RUNS = [(a, TOPK // (a + 1)) for a in range(TOPK // 2)]
CAND = sum(n for _, n in RUNS) + TOPK // 2
LOW = -3e38
FAR = 96
UR, VR = 4, 8
QUAD = 4
GROUPS = 8
PER_GROUP = SLOTS // GROUPS
QUADS = PER_GROUP // QUAD
PROMPT_SLOTS = TILES * SLOTS

PER_TILE = {
    "full4": 5, "full5": 5, "free4": 5, "free5": 5,
    "stat": 1, "std": 1, "rstd": 1, "hn": 1, "hn_kept": 1,
    "u_used": SLOTS, "v_used": SLOTS, "gelu": SLOTS // QUAD, "w": SLOTS // QUAD, "diag": SLOTS,
    "residual": 1, "acc_full": 1, "acc_free": 1, "ystat": 2, "ysum": 1, "ystd": 1, "yrstd": 1, "y_out": 16,
    "idx": SLOTS // QUAD, "gexp_in": 1, "gexp": 1, "chosen": 1, "y_ready": 1,
    "dve": 171,
    **{f"u_landed{j}": 16 * SLOTS // UR for j in range(UR)},
    **{f"v_landed{j}": 16 * SLOTS // VR for j in range(VR)},
}

class Ledger:

    def __init__(self):
        self.n, self.loops = {}, []

    def at(self, name):
        v = self.n.get(name, 0)
        for var, per in self.loops:
            if per.get(name, 0):
                v = var * per[name] + v
        return v

    def up(self, name, by=1):
        self.n[name] = self.n.get(name, 0) + by
        return self.at(name)

    @contextmanager
    def loop(self, eng, trips, per):
        start = dict(self.n)
        with eng.Fori(0, trips) as var:
            self.loops.append((var, per))
            yield var
            self.loops.pop()
        for name in self.n:
            turn = self.n[name] - start.get(name, 0)
            assert turn in (0, per.get(name, 0)), (name, turn, per.get(name, 0))
            if turn:
                self.n[name] = start.get(name, 0) + trips * turn


def hybrid_step_kernel(nc, x_p, x_s, cak, cav, cbk, cbv, g_mix, w_in, w_a, w_b, w_o, sink, g_ffn, w_pq, subk,
                       pu, pv, g_fin, masks_d, rope_d, sbias_d, ident_d, iota_d,
                       y_p, y_s, akp, avp, bkp, bvp, aks, avs, bks, bvs):
    f32, u32 = mybir.dt.float32, mybir.dt.uint32
    ALU, ACT, AX = mybir.AluOpType, mybir.ActivationFunctionType, mybir.AxisListType
    ds = bass.ds
    q_scratch = nc.dram_tensor("q_scratch", (DEC, WA + WB), f32).ap()
    hn_scratch = nc.dram_tensor("hn_scratch", (DEC, D), f32).ap()

    with ExitStack() as ctx:
        def sb(name, shape, dt=f32):
            return ctx.enter_context(nc.sbuf_tensor(name, shape, dt))

        KTW, KBTW = (WA // P) * SEQ, KVB * SEQ
        arena = sb("arena", [P, ALL * ZW + KTW + KBTW])
        Z = arena[:, 0:ALL * ZW].rearrange("p (t n) -> p t n", t=ALL)
        KT = arena[:, ALL * ZW:ALL * ZW + KTW].rearrange("p (c n) -> p c n", c=WA // P)
        KBT = arena[:, ALL * ZW + KTW:ALL * ZW + KTW + KBTW].rearrange("p (g n) -> p g n", g=KVB)
        GT = sb("GT", [P, ALL, 2 * D])
        WR = sb("WR", [P, 16 * D])
        XS = sb("XS", [P, KO * ALL * P])
        PP = sb("PP", [P, 2 * D])
        GF = sb("GF", [P, 2 * D])
        ident = sb("ident", [P, P])
        skT = sb("skT", [P, 2, NK])
        iota = sb("iota", [P, CAND])
        gmix = sb("gmix", [P, KO])
        nsink = sb("nsink", [P, HB])
        nsink_bh = sb("nsink_bh", [DEC * HB, 1])
        stats = sb("stats", [P, 96])
        e_all = sb("e_all", [P, ALL, SLOTS], u32)
        gate_all = sb("gate_all", [P, ALL, SLOTS])
        idxq = sb("idxq", [P, 4, QUAD], u32)
        dots = sb("dots", [P, 2, QUAD])
        gelus = sb("gelus", [P, 2, QUAD])
        wq = sb("wq", [P, 2, QUAD])

        GTf = GT[:, :, :].rearrange("p t n -> p (t n)")

        def row(t, lo, hi):
            return GTf[:, ds(t * (2 * D) + lo, hi - lo)]

        def slots(buf, t):
            return buf[:, :, :].rearrange("p t n -> p (t n)")[:, ds(t * SLOTS, SLOTS)]

        xT = XS[:, :].rearrange("p (k n) -> p k n", k=KO)
        ring = [WR[:, i * KO * CHUNK:(i + 1) * KO * CHUNK].rearrange("p (k n) -> p k n", k=KO) for i in range(2)]
        w_ab = WR[:, 8 * D:16 * D].rearrange("p (k n) -> p k n", k=8)
        w_out = WR[:, 0:8 * D].rearrange("p (k n) -> p k n", k=KO)
        w_q = WR[:, :].rearrange("p (k n) -> p k n", k=KO)
        NHR = 2 * HA + HB + KVB
        rot = XS[:, 0:NHR * HD]
        KD = XS[:, NHR * HD:NHR * HD + 4 * HD]
        o0 = NHR * HD + 4 * HD
        tmp1, tmp2 = XS[:, o0:o0 + D], XS[:, o0 + D:o0 + 2 * D]
        O = tmp1
        oT = tmp2.rearrange("p (k n) -> p k n", k=KO)
        qT = XS[:, o0 + 2 * D:o0 + 3 * D].rearrange("p (k n) -> p k n", k=KO)
        M = XS[:, 0:D]
        mT = qT
        Pr = PP[:, 0:D].rearrange("p (a n) -> p a n", a=2)
        PrT = PP[:, D:2 * D].rearrange("p (a n) -> p a n", a=2)
        maskA = GF[:, 0:4 * P]
        maskB = GF[:, 4 * P:6 * P]
        rope = GF[:, 768:768 + ALL * 2 * HD].rearrange("p (t c d) -> p t c d", t=ALL, c=2)
        sbias = GF[0:DEC * HB, 1408:2048]
        gffn, gfin = GF[:, 0:D], GF[:, D:2 * D]
        KVW = 3 * WA + 2 * WK
        kv = [arena[:, i * KVW:(i + 1) * KVW] for i in range(2)]
        s0 = 2 * KVW
        prod = arena[:, s0:s0 + 3 * WA]
        qbc = [arena[:, s0 + 3 * WA + i * D:s0 + 3 * WA + (i + 1) * D] for i in range(2)]
        s1 = s0 + 3 * WA + 2 * D
        sS = arena[:, s1:s1 + 5 * 64].rearrange("p (c n) -> p c n", c=5)
        sP = arena[0:64, s1 + 320:s1 + 320 + 640]
        sPT = arena[:, s1 + 960:s1 + 960 + 320].rearrange("p (c n) -> p c n", c=5)
        assert s1 + 1280 <= TILES * ZW
        qpT = XS[:, 0:2 * D].rearrange("p (l n) -> p l n", l=LISTS)
        Ssc = XS[:, 2 * D:4 * D].rearrange("p (l n) -> p l n", l=LISTS)
        hnT = XS[:, 4 * D:5 * D].rearrange("p (k n) -> p k n", k=KO)
        hnF = PP[:, 0:D]
        topv = PP[:, D:D + 256].rearrange("p (h c k) -> p h c k", h=PH, c=2)
        topi = PP[:, D + 256:D + 512].bitcast(u32).rearrange("p (h c k) -> p h c k", h=PH, c=2)
        best = PP[:, D + 512:D + 640].rearrange("p (h k) -> p h k", h=PH)
        bpos = PP[:, D + 640:D + 768].bitcast(u32).rearrange("p (h k) -> p h k", h=PH)
        bposf = PP[:, D + 768:D + 896].rearrange("p (h k) -> p h k", h=PH)
        eF = PP[:, D + 896:D + 1024]
        U = [arena[:, j * D:(j + 1) * D] for j in range(UR)]
        V = [arena[:, (UR + j) * D:(UR + j + 1) * D] for j in range(VR)]
        c0 = (UR + VR) * D
        diag = arena[:, c0:c0 + 8 * P].rearrange("p (j n) -> p j n", j=8)
        cs = arena[:, c0 + D:c0 + D + PH * CAND].rearrange("p (h c) -> p h c", h=PH)
        ce = arena[:, c0 + D + PH * CAND:c0 + D + 2 * PH * CAND].rearrange("p (h c) -> p h c", h=PH)
        gexp = arena[:, c0 + 1824:c0 + 1952].rearrange("p (h k) -> p h k", h=PH)
        topif = arena[:, c0 + 1824:c0 + 2080].rearrange("p (h c k) -> p h c k", h=PH, c=2)
        eqs = [XS[:, j * TOPK * CAND:(j + 1) * TOPK * CAND].rearrange("p (k c) -> p k c", k=TOPK) for j in range(4)]
        hbc = [XS[:, j * D:(j + 1) * D] for j in range(4)]
        ss, std, rstd = stats[:, 0:5], stats[:, 5:10], stats[:, 10:15]
        nm, den, rden, es = stats[:, 16:32], stats[:, 32:48], stats[:, 48:64], stats[:, 64:72]
        hss, hstd, hrstd = stats[:, 72:73], stats[:, 73:74], stats[:, 74:75]
        yss, ysum, ystd, yrstd = stats[:, 76:78], stats[:, 78:79], stats[:, 79:80], stats[:, 80:81]
        gsum = stats[:, 82:90]
        epsc = stats[:, 90:91]
        zero_col = sb("zero_col", [1, P])
        idxT = sb("idxT", [P, DEC], u32)
        gateT = sb("gateT", [P, DEC])
        sdots = sb("sdots", [P, 3, DEC])
        WM = sb("WM", [P, DEC, DEC])

        bank = [ctx.enter_context(nc.psum_tensor(f"bank{i}", [P, CHUNK], f32)) for i in range(8)]

        names = {}

        def sem(name):
            if name not in names:
                names[name] = ctx.enter_context(nc.semaphore(name))
            return names[name]

        full = [sem(f"full{i}") for i in range(8)]
        free = [sem(f"free{i}") for i in range(8)]
        for n in ("x_in", "const_in", "w_in0", "w_in1", "wab_in", "wout_in", "wq_in", "gf_in", "x_zero", "copies",
                  "stat", "std", "rstd", "xs", "rot", "stores", "probs", "pt", "pv", "onorm", "merged", "x_again",
                  "h", "dve", "kvzero", "q_out", "kv_in0", "kv_in1", "q_in0", "q_in1", "qk", "sP", "sE", "sW", "sO",
                  "sT", "hn", "hn_kept", "u_used", "v_used", "gelu", "w", "diag", "residual", "acc_full", "acc_free",
                  "ystat", "ysum", "ystd", "yrstd", "y_out", "idx", "gexp_in", "gexp", "chosen", "y_ready", "act",
                  "hn_out", "hb_in0", "hb_in1", "hb_in2", "hb_in3", "esink", "sd", "sg", "swm", "tT", "oT_zero", "eps"):
            sem(n)
        S = names
        u_landed = [sem(f"u_landed{j}") for j in range(UR)]
        v_landed = [sem(f"v_landed{j}") for j in range(VR)]

        block = ctx.enter_context(nc.Block())

        w_in_v = w_in.rearrange("(k p) n -> p k n", p=P)
        w_a_v = w_a.rearrange("(k p) n -> p k n", p=P)
        w_b_v = w_b.rearrange("(k p) n -> p k n", p=P)
        w_o_v = w_o.rearrange("(k p) n -> p k n", p=P)
        w_pq_v = w_pq.rearrange("(k p) n -> p k n", p=P)
        PAIR_AT = [0, 2 * CHUNK, ZW, ZW + 2 * CHUNK]
        XLOADS, CONSTS = 16 * ALL, 16 * 16

        MISC = 14
        KROWS = (PAST - P, PAST - CHUNK, 0)

        @block.sync
        def _(sp):
            L = Ledger()
            sp.wait_ge(S["x_zero"], 1)
            sp.dma_start(GT[0:DEC, SAMPLE, 0:D], x_s).then_inc(S["x_in"], 16)
            for t in range(TILES):
                sp.dma_start(GT[:, t, 0:D], x_p[t * P:(t + 1) * P, :]).then_inc(S["x_in"], 16)
            sp.dma_start(ident[:, :], ident_d).then_inc(S["const_in"], 16)
            sp.dma_start(gmix[:, :], g_mix.rearrange("(k p) -> p k", p=P), allow_slow_non_contiguous=True).then_inc(S["const_in"], 16)
            sp.dma_start(ring[1][:, :, 0:2 * WK], w_in_v[:, :, KB:KB + 2 * WK]).then_inc(S["w_in1"], 16)
            sp.dma_start(ring[0], w_in_v[:, :, 0:CHUNK]).then_inc(S["w_in0"], 16)
            sp.dma_start(GF[:, 0:768], masks_d).then_inc(S["const_in"], 16)
            sp.dma_start(GF[:, 768:1408], rope_d).then_inc(S["const_in"], 16)
            sp.dma_start(sbias, sbias_d).then_inc(S["const_in"], 16)
            sp.dma_start(iota[:, :], iota_d.partition_broadcast(P)).then_inc(S["const_in"], 16)
            sp.dma_start(nsink[:, :], sink.partition_broadcast(P)).then_inc(S["const_in"], 16)
            for b in range(DEC):
                sp.dma_start(nsink_bh[b * HB:(b + 1) * HB, :], sink.rearrange("(h o) -> h o", o=1)).then_inc(S["const_in"], 16)
            sp.dma_start(skT[:, :, :], subk.rearrange("c n d -> n c d")).then_inc(S["const_in"], 16)
            sp.dma_start(w_ab[:, 0:4, :], w_a_v).then_inc(S["wab_in"], 16)
            sp.dma_start(w_ab[:, 4:8, :], w_b_v).then_inc(S["wab_in"], 16)

            copies = [(c[b], o[b]) for b in range(DEC) for c, o in ((cak, aks), (cav, avs))]

            def copy_a():
                src, dst = copies.pop(0)
                n = (PAST - DEC_NEW) * WA // 64
                sp.dma_start(dst[0:PAST - 1, :].rearrange("s n -> (s n)").rearrange("(a n) -> a n", n=n),
                             src[1:PAST, :].rearrange("s n -> (s n)").rearrange("(a n) -> a n", n=n)).then_inc(S["copies"], 16)

            DEC_NEW = 1
            sp.dma_start(bks[:, 0:P - 1, :], cbk[:, 1:P, :]).then_inc(S["copies"], 16)
            sp.dma_start(bvs[:, 0:P - 1, :], cbv[:, 1:P, :]).then_inc(S["copies"], 16)
            for p in range(4):
                for c in range(2):
                    if p or c:
                        sp.wait_ge(full[6], 2 * p + c if c == 0 else 2 * p + 1)
                        sp.dma_start(ring[c], w_in_v[:, :, PAIR_AT[p] + c * CHUNK:PAIR_AT[p] + (c + 1) * CHUNK])\
                            .then_inc(S[f"w_in{c}"], 16)
                    copy_a()
            sp.wait_ge(full[6], 9)
            sp.dma_start(w_out, w_o_v).then_inc(S["wout_in"], 16)
            for t in range(TILES):
                copy_a()
                sp.wait_ge(S["rot"], t + 1)
                rows = slice(t * P, (t + 1) * P)
                sp.dma_start(akp[rows, :], rot[:, WA:2 * WA]).then_inc(S["stores"], 16)
                sp.dma_start(avp[rows, :], Z[:, t, VA:VA + WA]).then_inc(S["stores"], 16)
                if t == TILES - 1:
                    sp.dma_start(bkp, rot[:, 2 * WA + WB:2 * WA + WB + WK]).then_inc(S["stores"], 16)
                    sp.dma_start(bvp, Z[:, t, VB:VB + WK]).then_inc(S["stores"], 16)
                copy_a()
                sp.wait_ge(S["merged"], 2 * (t + 1))
                sp.dma_start(GT[:, t, D:2 * D], x_p[rows, :]).then_inc(S["x_again"], 16)

            sp.wait_ge(S["rot"], ALL)
            sp.dma_start(aks[:, PAST - 1, :], rot[0:DEC, WA:2 * WA]).then_inc(S["q_out"], 16)
            sp.dma_start(avs[:, PAST - 1, :], Z[0:DEC, SAMPLE, VA:VA + WA]).then_inc(S["q_out"], 16)
            sp.dma_start(bks[:, P - 1, :], rot[0:DEC, 2 * WA + WB:2 * WA + WB + WK]).then_inc(S["q_out"], 16)
            sp.dma_start(bvs[:, P - 1, :], Z[0:DEC, SAMPLE, VB:VB + WK]).then_inc(S["q_out"], 16)
            sp.dma_start(q_scratch[:, 0:WA], rot[0:DEC, 0:WA]).then_inc(S["q_out"], 16)
            sp.dma_start(q_scratch[:, WA:WA + WB], rot[0:DEC, 2 * WA:2 * WA + WB]).then_inc(S["q_out"], 16)
            sp.wait_ge(S["q_out"], 96)
            sp.wait_ge(S["kvzero"], 2)
            for i in range(2 * DEC):
                b, r = i % DEC, i % 2
                ca, cb, na, nb = (cak, cbk, aks, bks) if i < DEC else (cav, cbv, avs, bvs)
                if 2 <= i <= DEC + 1:
                    sp.wait_ge(S["qk"], i - 1)
                elif i > DEC + 1:
                    sp.wait_ge(S["sO"], i - DEC - 1)
                k = kv[r]
                sem_kv = S[f"kv_in{r}"]
                sp.dma_start(k[:, 0:WA], ca[b, PAST - P:PAST, :]).then_inc(sem_kv, 16)
                sp.dma_start(k[0:FAR, WA:2 * WA], ca[b, PAST - CHUNK:PAST - P:4, :]).then_inc(sem_kv, 16)
                sp.dma_start(k[FAR:FAR + 1, WA:2 * WA], na[b, PAST - 1:PAST, :]).then_inc(sem_kv, 16)
                sp.dma_start(k[0:FAR, 2 * WA:3 * WA], ca[b, 0:PAST - CHUNK:16, :]).then_inc(sem_kv, 16)
                sp.dma_start(k[:, 3 * WA:3 * WA + WK], cb[b, :, :]).then_inc(sem_kv, 16)
                sp.dma_start(k[0:1, 3 * WA + WK:KVW], nb[b, P - 1:P, :]).then_inc(sem_kv, 16)
                if i < DEC:
                    sp.dma_start(qbc[r], q_scratch[b, :].partition_broadcast(P)).then_inc(S[f"q_in{r}"], 16)
            sp.wait_ge(S["merged"], 2 * ALL)
            sp.dma_start(GT[0:DEC, SAMPLE, D:2 * D], x_s).then_inc(S["x_again"], 16)
            sp.wait_ge(S["h"], 2 * ALL)
            sp.dma_start(w_q, w_pq_v).then_inc(S["wq_in"], 16)
            sp.dma_start(gffn, g_ffn.partition_broadcast(P)).then_inc(S["gf_in"], 16)
            sp.dma_start(gfin, g_fin.partition_broadcast(P)).then_inc(S["gf_in"], 16)
            while copies:
                copy_a()
            with L.loop(sp, TILES - 1, PER_TILE) as t:
                sp.wait_ge(S["y_ready"], L.up("y_ready"))
                sp.dma_start(y_p[ds(t * P, P), :], GTf[:, ds(t * (2 * D) + D, D)]).then_inc(S["y_out"], 16)
            sp.wait_ge(S["hn_kept"], ALL)
            sp.dma_start(hn_scratch, GT[0:DEC, SAMPLE, 0:D]).then_inc(S["hn_out"], 16)
            sp.wait_ge(S["hn_out"], 16)
            sp.wait_ge(S["chosen"], ALL)
            for b in range(DEC):
                if b >= 4:
                    sp.wait_ge(S["u_used"], UR + PROMPT_SLOTS + b - 3)
                sp.dma_start(hbc[b % 4], hn_scratch[b, :].partition_broadcast(P)).then_inc(S[f"hb_in{b % 4}"], 16)
            sp.wait_ge(S["y_ready"], TILES)
            sp.dma_start(y_p[SEQ - P:SEQ, :], GT[:, TILES - 1, D:2 * D]).then_inc(S["y_out"], 16)
            sp.wait_ge(S["y_ready"], ALL)
            sp.dma_start(y_s, GT[0:DEC, SAMPLE, D:2 * D]).then_inc(S["y_out"], 16)
            sp.wait_ge(S["y_out"], 16 * ALL)
            sp.wait_ge(S["stores"], 16 * (2 * TILES + 2))
            sp.wait_ge(S["copies"], 16 * 18)

        @block.gpsimd
        def _(pool):
            L = Ledger()
            nc.gpsimd.memset(GT[:, SAMPLE, 0:D], 0.0).then_inc(S["x_zero"], 1)
            nc.gpsimd.memset(epsc, EPS).then_inc(S["eps"], 1)
            nc.gpsimd.memset(WM[:, :, :], 0.0).then_inc(S["eps"], 1)
            pool.wait_ge(S["h"], 2 * TILES)
            pool.wait_ge(S["stores"], 16 * (2 * TILES + 2))
            nc.gpsimd.memset(kv[0], 0.0).then_inc(S["kvzero"], 1)
            nc.gpsimd.memset(kv[1], 0.0).then_inc(S["kvzero"], 1)

            pool.wait_ge(S["h"], 2 * ALL)

            def gather(dst, table, idx, landed):
                nc.gpsimd.indirect_dma_start(dst, None, table, bass.IndirectOffsetOnAxis(ap=idx, axis=0))\
                    .then_inc(landed, 16)

            experts = e_all[:, :, :].rearrange("p t n -> p (t n)")
            with L.loop(pool, TILES, PER_TILE) as t:
                pool.wait_ge(S["chosen"], L.up("chosen"))
                for s in range(SLOTS):
                    if s % QUAD == 0:
                        q = s // QUAD % 4
                        nc.gpsimd.tensor_copy(idxq[:, q, :], experts[:, ds(t * SLOTS + s, QUAD)]).then_inc(S["idx"], 1)
                        pool.wait_ge(S["idx"], L.up("idx"))
                        pool.nop(nofuse=True)
                    pool.wait_ge(S["u_used"], L.up("u_used"))
                    pool.nop(nofuse=True)
                    gather(U[s % UR], pu, idxq[:, q, s % QUAD:s % QUAD + 1], u_landed[s % UR])
                    pool.wait_ge(S["v_used"], L.up("v_used"))
                    pool.nop(nofuse=True)
                    gather(V[s % VR], pv, idxq[:, q, s % QUAD:s % QUAD + 1], v_landed[s % VR])
            pool.wait_ge(S["tT"], 2)
            for b in range(DEC):
                pool.wait_ge(S["u_used"], L.up("u_used"))
                gather(U[b % UR], pu, idxT[:, b:b + 1], u_landed[b % UR])
                pool.wait_ge(S["v_used"], L.up("v_used"))
                gather(V[b], pv, idxT[:, b:b + 1], v_landed[b])

        @block.scalar
        def _(act):
            L = Ledger()
            act.wait_ge(S["x_in"], XLOADS)
            act.wait_ge(S["eps"], 1)
            for t in range(ALL):
                nc.scalar.activation(GT[:, t, D:2 * D], GT[:, t, 0:D], ACT.Square, accum_out=ss[:, t:t + 1])\
                    .then_inc(S["stat"], 1)
            act.wait_ge(S["stat"], ALL)
            nc.scalar.activation(std, ss, ACT.Sqrt, bias=epsc, scale=1.0 / D).then_inc(S["std"], 1)
            act.wait_ge(S["rstd"], 1)
            for t in range(ALL):
                nc.scalar.activation(GT[:, t, D:2 * D], GT[:, t, 0:D], ACT.Copy, scale=rstd[:, t:t + 1])\
                    .then_inc(S["xs"], 1)

            for m in range(ALL):
                act.wait_ge(full[2 + m], 1)
                nc.scalar.activation(Z[:, m, KB:KB + 2 * WK], bank[2 + m][:, 0:2 * WK], ACT.Copy).then_inc(free[2 + m], 1)
            zf = arena[:, 0:ALL * ZW]
            with act.Fori(0, 2) as p:
                for c in range(2):
                    for m in range(ALL):
                        act.wait_ge(full[2 + m], p * 2 + (c + 2))
                        nc.scalar.activation(zf[:, ds(p * (2 * CHUNK) + (m * ZW + c * CHUNK), CHUNK)], bank[2 + m][:, :],
                                             ACT.Copy).then_inc(free[2 + m], 1)
            gf = GT[:, :, :].rearrange("p t n -> p (t n)")
            with act.Fori(0, 2) as p:
                for c in range(2):
                    for m in range(ALL):
                        act.wait_ge(full[2 + m], p * 2 + (c + 6))
                        nc.scalar.activation(gf[:, ds(p * D + (m * 2 * D + c * CHUNK), CHUNK)], bank[2 + m][:, :],
                                             ACT.Sigmoid).then_inc(free[2 + m], 1)
            for m in range(ALL):
                L.n[f"full{2 + m}"] = 9
            misc = [0]

            def evac(dst, width=CHUNK):
                i = 4 + misc[0] % 2
                misc[0] += 1
                act.wait_ge(full[i], L.up(f"full{i}"))
                nc.scalar.activation(dst, bank[i][:, 0:width] if len(dst.shape) == 2 else
                                     bank[i][:, 0:width].rearrange("p (k n) -> p k n", n=P), ACT.Copy).then_inc(free[i], 1)

            def skip(n):
                for _ in range(n):
                    L.up(f"full{4 + misc[0] % 2}")
                    misc[0] += 1

            def mix():
                skip(4)
                evac(mT[:, 0:4, :])
                evac(mT[:, 4:8, :])
                skip(2)

            for t in range(TILES):
                cols = slice(t * P, (t + 1) * P)
                evac(qT[:, 0:4, :])
                evac(KT[:, :, cols])
                evac(qT[:, 4:8, :])
                evac(KBT[:, :, cols], 2 * P)
                for hd in range(HA + HB):
                    n = (t + 1) * P if hd < HA else min(t + 1, 2) * P
                    act.wait_ge(free[hd % 2], ALL + 8 * t + hd // 2 + 1)
                    nc.scalar.activation(Pr[:, hd % 2, 0:n], Pr[:, hd % 2, 0:n], ACT.Exp, bias=nm[:, hd:hd + 1], scale=-1.0,
                                         accum_out=den[:, hd:hd + 1]).then_inc(S["probs"], 1)
                act.wait_ge(S["esink"], 2 * t + 1)
                nc.scalar.activation(es, es, ACT.Exp).then_inc(S["esink"], 1)
                evac(oT[:, 0:4, :])
                evac(oT[:, 4:8, :])
                mix()

            act.wait_ge(S["sP"], 2)
            nc.scalar.activation(sP[:, 0:384], sP[:, 0:384], ACT.Exp, bias=nm[0:64, 0:1], scale=-1.0,
                                 accum_out=den[0:64, 0:1]).then_inc(S["sE"], 1)
            nc.scalar.activation(sP[:, 384:640], sP[:, 384:640], ACT.Exp, bias=nm[0:64, 1:2], scale=-1.0,
                                 accum_out=den[0:64, 1:2]).then_inc(S["sE"], 1)
            act.wait_ge(S["esink"], 2 * TILES + 1)
            nc.scalar.activation(es[0:64, 0:1], es[0:64, 0:1], ACT.Exp).then_inc(S["esink"], 1)
            skip(2)
            i = 4 + misc[0] % 2
            misc[0] += 1
            act.wait_ge(full[i], L.up(f"full{i}"))
            nc.scalar.activation(sPT, bank[i][:, 0:320].rearrange("p (c n) -> p c n", c=5), ACT.Copy).then_inc(free[i], 1)
            skip(1)
            mix()

            def choose(t, piece):
                if piece == 0:
                    h, hn = row(t, D, 2 * D), row(t, 0, D)
                    nc.scalar.activation(hnF, h, ACT.Square, accum_out=hss).then_inc(S["stat"], 1)
                    act.wait_ge(S["stat"], L.up("stat"))
                    nc.scalar.activation(hstd, hss, ACT.Sqrt, bias=epsc, scale=1.0 / D).then_inc(S["std"], 1)
                    act.wait_ge(S["hn"], L.up("hn"))
                    nc.scalar.activation(hn, hnF, ACT.Copy).then_inc(S["hn_kept"], 1)
                    evac(hnT[:, 0:4, :])
                    evac(hnT[:, 4:8, :])
                elif piece <= 4:
                    i = piece - 1
                    evac(qpT[:, 4 * i:4 * i + 4, :])
                    evac(Ssc[:, 4 * i:4 * i + 4, :])
                elif piece == 5:
                    act.wait_ge(S["gexp_in"], L.up("gexp_in"))
                    nc.scalar.activation(gexp, gexp, ACT.Exp).then_inc(S["gexp"], 1)

            L.n["stat"], L.n["hn"] = ALL, 0
            act.wait_ge(S["h"], 2 * ALL)
            L.n["v_used"] = VR
            for piece in range(GROUPS):
                choose(0, piece)

            L.n["u_used"] = UR
            L.n["v_used"] = VR

            with L.loop(act, TILES, PER_TILE) as t:
                for g in range(GROUPS):
                    for q in range(QUADS):
                        act.wait_ge(S["u_used"], L.up("u_used", QUAD))
                        nc.scalar.activation(gelus[:, q % 2, :], dots[:, q % 2, :], ACT.Gelu).then_inc(S["gelu"], 1)
                        act.wait_ge(S["w"], L.up("w"))
                        act.wait_ge(S["v_used"], L.up("v_used", QUAD) - 2 * QUAD)
                        for j in range(QUAD):
                            nc.scalar.activation(diag[:, QUAD * (q % 2) + j, :], ident[:, :], ACT.Copy,
                                                 scale=wq[:, q % 2, j:j + 1]).then_inc(S["diag"], 1)
                    choose(t + 1, g)
                act.wait_ge(S["acc_full"], L.up("acc_full"))
                for c in range(2):
                    nc.scalar.activation(PP[:, 0:CHUNK], bank[6 + c][:, :], ACT.Square, accum_out=yss[:, c:c + 1])\
                        .then_inc(S["ystat"], 1)
                    act.wait_ge(S["ystat"], L.up("ystat"))
                act.wait_ge(S["ysum"], L.up("ysum"))
                nc.scalar.activation(ystd, ysum, ACT.Sqrt, bias=epsc, scale=1.0 / D).then_inc(S["ystd"], 1)
            act.wait_ge(S["u_used"], UR + PROMPT_SLOTS + DEC)
            nc.scalar.activation(sdots[:, 1, :], sdots[:, 0, :], ACT.Gelu).then_inc(S["sg"], 1)
            act.wait_ge(S["acc_full"], L.up("acc_full"))
            for c in range(2):
                nc.scalar.activation(PP[0:DEC, 0:CHUNK], bank[6 + c][0:DEC, :], ACT.Square, accum_out=yss[0:DEC, c:c + 1])\
                    .then_inc(S["ystat"], 1)
                act.wait_ge(S["ystat"], L.up("ystat"))
            act.wait_ge(S["ysum"], L.up("ysum"))
            nc.scalar.activation(ystd[0:DEC, :], ysum[0:DEC, :], ACT.Sqrt, bias=epsc[0:DEC, :], scale=1.0 / D)\
                .then_inc(S["ystd"], 1)

        @block.tensor
        def _(pe):
            L = Ledger()

            def claim(i):
                n = L.at(f"free{i}")
                if not (isinstance(n, int) and n == 0):
                    pe.wait_ge(free[i], n)
                L.up(f"free{i}")

            pe.wait_ge(S["const_in"], CONSTS)
            misc = [0]

            def next_bank():
                i = 4 + misc[0] % 2
                misc[0] += 1
                claim(i)
                return i

            for m in range(ALL):
                pe.wait_ge(S["xs"], m + 1)
                for half in range(2):
                    claim(half)
                    for k in range(4):
                        kk = 4 * half + k
                        last = nc.tensor.transpose(bank[half][:, k * P:(k + 1) * P], GT[:, m, D + kk * P:D + (kk + 1) * P], ident[:, :])
                    last.then_inc(full[half], 1)
            pe.wait_ge(free[1], ALL)
            pe.wait_ge(free[0], ALL)
            pe.wait_ge(S["w_in1"], 16)
            for m in range(ALL):
                for k in range(KO):
                    last = nc.tensor.matmul(bank[2 + m][:, 0:2 * WK], xT[:, k, m * P:(m + 1) * P], ring[1][:, k, 0:2 * WK],
                                            start=(k == 0), stop=(k == KO - 1))
                last.then_inc(full[2 + m], 1)
            with pe.Fori(0, 4) as p:
                for c in range(2):
                    pe.wait_ge(S[f"w_in{c}"], p * 16 + (16 if c == 0 else 32))
                    for m in range(ALL):
                        pe.wait_ge(free[2 + m], p * 2 + (1 + c))
                        for k in range(KO):
                            last = nc.tensor.matmul(bank[2 + m][:, :], xT[:, k, m * P:(m + 1) * P], ring[c][:, k, :],
                                                    start=(k == 0), stop=(k == KO - 1))
                        last.then_inc(full[2 + m], 1)
            for m in range(ALL):
                L.n[f"free{2 + m}"] = 9

            def transposes(src, blocks):
                i = next_bank()
                for k in range(blocks):
                    last = nc.tensor.transpose(bank[i][:, k * P:(k + 1) * P], src[:, k * P:(k + 1) * P], ident[:, :])
                last.then_inc(full[i], 1)
                return i

            def mix(t):
                pe.wait_ge(S["wab_in"], 32)
                for n in range(2):
                    for br in range(2):
                        i = next_bank()
                        for k in range(4):
                            last = nc.tensor.matmul(bank[i][:, :], oT[:, 4 * br + k, :], w_ab[:, 4 * br + k, n * CHUNK:(n + 1) * CHUNK],
                                                    start=(k == 0), stop=(k == 3))
                        last.then_inc(full[i], 1)
                pe.wait_ge(S["merged"], 2 * t + 2)
                a = transposes(M[:, 0:CHUNK], 4)
                b = transposes(M[:, CHUNK:D], 4)
                pe.wait_ge(S["wout_in"], 16)
                pe.wait_ge(free[a], L.at(f"free{a}"))
                pe.wait_ge(free[b], L.at(f"free{b}"))
                for n in range(2):
                    i = next_bank()
                    for k in range(KO):
                        last = nc.tensor.matmul(bank[i][:, :], mT[:, k, :], w_out[:, k, n * CHUNK:(n + 1) * CHUNK],
                                                start=(k == 0), stop=(k == KO - 1))
                    last.then_inc(full[i], 1)

            for t in range(TILES):
                pe.wait_ge(S["rot"], t + 1)
                transposes(rot[:, 0:WA], 4)
                transposes(rot[:, WA:2 * WA], 4)
                a = transposes(rot[:, 2 * WA:2 * WA + WB], 4)
                b = transposes(KD, 2)
                pe.wait_ge(free[a], L.at(f"free{a}"))
                pe.wait_ge(free[b], L.at(f"free{b}"))

                def span(hd):
                    return (0, t + 1) if hd < HA else (max(t - 1, 0), t + 1)

                def score(hd):
                    lo, hi = span(hd)
                    h = hd % 8
                    r = slice(HD * (h % 2), HD * (h % 2) + HD)
                    claim(hd % 2)
                    keys = KT[r, h // 2, lo * P:hi * P] if hd < HA else KBT[r, h // 4, lo * P:hi * P]
                    nc.tensor.matmul(bank[hd % 2][:, 0:(hi - lo) * P], qT[r, (hd // 8) * 4 + h // 2, :], keys,
                                     start=True, stop=True).then_inc(full[hd % 2], 1)

                def turn(hd):
                    lo, hi = span(hd)
                    pe.wait_ge(S["probs"], t * 16 + hd + 1)
                    claim(2 + hd % 2)
                    for k in range(hi - lo):
                        last = nc.tensor.transpose(bank[2 + hd % 2][:, k * P:(k + 1) * P], Pr[:, hd % 2, k * P:(k + 1) * P], ident[:, :])
                    last.then_inc(full[2 + hd % 2], 1)

                def values(hd):
                    lo, hi = span(hd)
                    h = hd % 8
                    if h == 0:
                        claim(6 + hd // 8)
                    pe.wait_ge(free[2 + hd % 2], 9 * (2 + hd % 2 >= 2) + 8 * t + hd // 2 + 1)
                    at = VA + h * HD if hd < HA else VB + (h // 4) * HD
                    for k in range(hi - lo):
                        last = nc.tensor.matmul(bank[6 + hd // 8][:, h * HD:(h + 1) * HD], PrT[:, hd % 2, k * P:(k + 1) * P],
                                                Z[:, lo + k, at:at + HD], start=(k == 0), stop=(k == hi - lo - 1))
                    last.then_inc(S["pv"], 1)

                NH = HA + HB
                score(0)
                for hd in range(NH):
                    if hd + 1 < NH:
                        score(hd + 1)
                    turn(hd)
                    if hd:
                        values(hd - 1)
                values(NH - 1)
                pe.wait_ge(S["onorm"], 2 * t + 2)
                a = transposes(O[:, 0:CHUNK], 4)
                b = transposes(O[:, CHUNK:D], 4)
                pe.wait_ge(free[a], L.at(f"free{a}"))
                pe.wait_ge(free[b], L.at(f"free{b}"))
                mix(t)

            pe.wait_ge(S["qk"], DEC)
            for tiles in ((0, 3), (3, 5)):
                i = next_bank()
                for c in range(*tiles):
                    last = nc.tensor.transpose(bank[i][0:64, (c - tiles[0]) * P:(c - tiles[0] + 1) * P], sS[:, c, :], ident[:, :])
                last.then_inc(full[i], 1)
            pe.wait_ge(S["sW"], 2)
            i = next_bank()
            for c in range(5):
                last = nc.tensor.transpose(bank[i][:, c * 64:(c + 1) * 64], sP[:, c * P:(c + 1) * P], ident[0:64, 0:64])
            last.then_inc(full[i], 1)
            claim(6)
            claim(7)
            pe.wait_ge(free[i], L.at(f"free{i}"))
            for b in range(DEC):
                v = kv[b % 2]
                pe.wait_ge(S[f"kv_in{b % 2}"], 96 * (DEC // 2 + b // 2 + 1))
                for pair in range(4):
                    for c in range(3):
                        nc.tensor.matmul(bank[6][:, pair * 64 + b * 8:pair * 64 + b * 8 + 8], v[:, c * WA + pair * P:c * WA + (pair + 1) * P],
                                         sPT[:, c, b * 8:b * 8 + 8], start=(c == 0), stop=(c == 2))
                for c in range(2):
                    last = nc.tensor.matmul(bank[7][:, b * 8:b * 8 + 8], v[:, 3 * WA + c * WK:3 * WA + (c + 1) * WK],
                                            sPT[:, 3 + c, b * 8:b * 8 + 8], start=(c == 0), stop=(c == 1))
                last.then_inc(S["sO"], 1)
            i = next_bank()
            for c in range(2):
                last = nc.tensor.transpose(bank[i][:, c * P:(c + 1) * P], skT[:, c, :], ident[:, :])
            last.then_inc(full[i], 1)
            pe.wait_ge(S["sT"], 1)
            mix(SAMPLE)

            def choose(t, piece):
                if piece == 0:
                    pe.wait_ge(S["hn"], L.up("hn"))
                    transposes(hnF[:, 0:CHUNK], 4)
                    transposes(hnF[:, CHUNK:D], 4)
                    pe.wait_ge(free[4], L.at("free4"))
                    pe.wait_ge(free[5], L.at("free5"))
                elif piece <= 4:
                    i = next_bank()
                    for c in range(4):
                        col = (4 * (piece - 1) + c) * P
                        for k in range(KO):
                            last = nc.tensor.matmul(bank[i][:, c * P:(c + 1) * P], w_q[:, k, col:col + P], hnT[:, k, :],
                                                    start=(k == 0), stop=(k == KO - 1))
                    last.then_inc(full[i], 1)
                    pe.wait_ge(free[i], L.at(f"free{i}"))
                    i = next_bank()
                    for c in range(4):
                        last = nc.tensor.matmul(bank[i][:, c * P:(c + 1) * P], qpT[:, 4 * (piece - 1) + c, :], skT[:, c % 2, :],
                                                start=True, stop=True)
                    last.then_inc(full[i], 1)

            pe.wait_ge(S["wq_in"], 16)
            for piece in range(GROUPS):
                choose(0, piece)
            with L.loop(pe, TILES, PER_TILE) as t:
                pe.wait_ge(S["acc_free"], L.up("acc_free"))
                for c in range(2):
                    nc.tensor.matmul(bank[6 + c][:, :], ident[:, :],
                                     row(t, D + c * CHUNK, D + (c + 1) * CHUNK),
                                     start=True, stop=False, skip_group_check=True)
                for g in range(GROUPS):
                    for s in range(PER_GROUP):
                        j = s % VR
                        pe.wait_ge(v_landed[j], L.up(f"v_landed{j}", 16))
                        pe.wait_ge(S["diag"], L.up("diag"))
                        for c in range(2):
                            last = nc.tensor.matmul(bank[6 + c][:, :], diag[:, j, :], V[j][:, c * CHUNK:(c + 1) * CHUNK],
                                                    start=False, stop=False, skip_group_check=True)
                        last.then_inc(S["v_used"], 1)
                    choose(t + 1, g)
                for c in range(2):
                    last = nc.tensor.matmul(bank[6 + c][:, :], zero_col[0:1, :], gffn[0:1, 0:CHUNK],
                                            start=False, stop=True, skip_group_check=True)
                last.then_inc(S["acc_full"], 1)

            pe.wait_ge(S["chosen"], ALL)
            for src in (eF, gate_all[:, SAMPLE, :]):
                i = next_bank()
                nc.tensor.transpose(bank[i][:, 0:P], src, ident[:, :]).then_inc(full[i], 1)
            pe.wait_ge(S["acc_free"], L.up("acc_free"))
            for c in range(2):
                nc.tensor.matmul(bank[6 + c][0:DEC, :], ident[0:DEC, 0:DEC], GT[0:DEC, SAMPLE, D + c * CHUNK:D + (c + 1) * CHUNK],
                                 start=True, stop=False, skip_group_check=True)
            pe.wait_ge(S["swm"], 1)
            for b in range(DEC):
                pe.wait_ge(v_landed[b], L.up(f"v_landed{b}", 16))
                for c in range(2):
                    last = nc.tensor.matmul(bank[6 + c][0:DEC, :], WM[:, b, :], V[b][:, c * CHUNK:(c + 1) * CHUNK],
                                            start=False, stop=(b == DEC - 1), skip_group_check=True)
            last.then_inc(S["acc_full"], 1)

        @block.vector
        def _(dve):
            L = Ledger()

            def mark(ins):
                ins.then_inc(S["dve"], 1)
                L.up("dve")

            def settle():
                dve.wait_ge(S["dve"], L.at("dve"))
            V_ = nc.vector
            mark(V_.memset(zero_col[0:1, :], 0.0))
            dve.sem_inc(S["u_used"], UR)
            dve.sem_inc(S["v_used"], VR)
            dve.sem_inc(S["acc_free"], 1)
            dve.wait_ge(S["const_in"], CONSTS)
            mark(V_.tensor_scalar(nsink[:, :], nsink[:, :], -1.0, None, ALU.mult))
            mark(V_.tensor_scalar(nsink_bh[:, :], nsink_bh[:, :], -1.0, None, ALU.mult))
            dve.wait_ge(S["std"], 1)
            V_.reciprocal(rstd, std).then_inc(S["rstd"], 1)
            for m in range(ALL):
                for half in range(2):
                    dve.wait_ge(full[half], m + 1)
                    V_.tensor_tensor(xT[:, 4 * half:4 * half + 4, m * P:(m + 1) * P],
                                     bank[half][:, :].rearrange("p (k n) -> p k n", k=4),
                                     gmix[:, 4 * half:4 * half + 4].unsqueeze(2).to_broadcast([P, 4, P]), ALU.mult)\
                        .then_inc(free[half], 1)
            dve.wait_ge(full[6], 9)
            for m in range(ALL):
                dve.wait_ge(free[2 + m], 9)
            L.n["full4"] = L.n["full5"] = 9
            misc = [0]

            def skip(n):
                for _ in range(n):
                    L.up(f"full{4 + misc[0] % 2}")
                    misc[0] += 1

            def arrived():
                i = 4 + misc[0] % 2
                misc[0] += 1
                dve.wait_ge(full[i], L.up(f"full{i}"))
                return i

            def rotate(t, last):
                for src, dst, heads in ((QA, 0, 2 * HA), (QB, 2 * HA, HB + KVB)):
                    z = Z[:, t, src:src + heads * HD].rearrange("p (h d) -> p h d", d=HD)
                    a = tmp1[:, 0:heads * HD].rearrange("p (h d) -> p h d", d=HD)
                    b = tmp2[:, 0:heads * HD].rearrange("p (h d) -> p h d", d=HD)
                    out = rot[:, dst * HD:(dst + heads) * HD].rearrange("p (h d) -> p h d", d=HD)
                    H = HD // 2
                    settle()
                    mark(V_.tensor_tensor(a, z, rope[:, t, 0:1, :].to_broadcast([P, heads, HD]), ALU.mult))
                    mark(V_.tensor_tensor(b[:, :, 0:H], z[:, :, H:HD], rope[:, t, 1:2, 0:H].to_broadcast([P, heads, H]), ALU.mult))
                    mark(V_.tensor_tensor(b[:, :, H:HD], z[:, :, 0:H], rope[:, t, 1:2, H:HD].to_broadcast([P, heads, H]), ALU.mult))
                    settle()
                    mark(V_.tensor_tensor(out, a, b, ALU.add))
                settle()
                k = rot[:, (2 * HA + HB) * HD:NHR * HD].rearrange("p (g d) -> p g d", g=KVB)
                kd = KD.rearrange("p (g c d) -> p g c d", g=KVB, c=2)
                mark(V_.tensor_copy(kd[:, :, 0, :], k))
                V_.tensor_copy(kd[:, :, 1, :], k).then_inc(S["rot"], 1)

            def mix(t):
                for n in range(2):
                    c = slice(n * CHUNK, (n + 1) * CHUNK)
                    for br in range(2):
                        g = GT[:, t, br * D + n * CHUNK:br * D + (n + 1) * CHUNK]
                        i = arrived()
                        V_.tensor_tensor(g, g, bank[i][:, :], ALU.mult).then_inc(free[i], 1)
                    dve.wait_ge(free[5], L.at("full5"))
                    if n == 0 and t < TILES:
                        dve.wait_ge(S["stores"], 32 * (t + 1) + (32 if t == TILES - 1 else 0))
                    if n == 0 and t == SAMPLE:
                        dve.wait_ge(S["q_out"], 96)
                    V_.tensor_tensor(M[:, c], GT[:, t, c], GT[:, t, D + n * CHUNK:D + (n + 1) * CHUNK], ALU.add)\
                        .then_inc(S["merged"], 1)
                skip(2)
                dve.wait_ge(S["x_again"], 16 * (t + 1))
                for n in range(2):
                    i = arrived()
                    h = GT[:, t, D + n * CHUNK:D + (n + 1) * CHUNK]
                    V_.tensor_tensor(h, h, bank[i][:, :], ALU.add).then_inc(free[i], 1)
                dve.wait_ge(free[5], L.at("full5"))
                dve.wait_ge(free[4], L.at("full4"))
                dve.sem_inc(S["h"], 2)

            for t in range(TILES):
                if t:
                    dve.wait_ge(S["h"], 2 * t)
                rotate(t, t)
                skip(4)

                def scored(hd):
                    lo, hi = (0, t + 1) if hd < HA else (max(t - 1, 0), t + 1)
                    n = (hi - lo) * P
                    mask = maskA[:, 4 * P - n:4 * P] if hd < HA else maskB[:, 2 * P - n:2 * P]
                    dve.wait_ge(full[hd % 2], ALL + 8 * t + hd // 2 + 1)
                    if hd >= 2 or t:
                        dve.wait_ge(full[2 + hd % 2], 9 + 8 * t + hd // 2)
                    V_.tensor_tensor_reduce(out=Pr[:, hd % 2, 0:n], in0=bank[hd % 2][:, 0:n], in1=mask, scale=-SCALE,
                                            scalar=3e38 if hd < HA else nsink[:, hd - HA:hd - HA + 1],
                                            op0=ALU.add, op1=ALU.min, accum_out=nm[:, hd:hd + 1]).then_inc(free[hd % 2], 1)

                def turned(hd):
                    n = (t + 1) * P if hd < HA else min(t + 1, 2) * P
                    dve.wait_ge(full[2 + hd % 2], 9 + 8 * t + hd // 2 + 1)
                    if hd >= 2 or t:
                        dve.wait_ge(S["pv"], 16 * t + hd - 1)
                    V_.tensor_copy(PrT[:, hd % 2, 0:n], bank[2 + hd % 2][:, 0:n]).then_inc(free[2 + hd % 2], 1)

                def normalise(br):
                    hs = slice(8 * br, 8 * br + 8)
                    if br:
                        mark(V_.tensor_tensor(es, nm[:, 8:16], nsink[:, :], ALU.subtract))
                        settle()
                        dve.sem_inc(S["esink"], 1)
                        dve.wait_ge(S["esink"], 2 * t + 2)
                        mark(V_.tensor_tensor(den[:, 8:16], den[:, 8:16], es, ALU.add))
                        settle()
                    else:
                        dve.wait_ge(S["probs"], 16 * t + 8)
                    mark(V_.reciprocal(rden[:, hs], den[:, hs]))
                    settle()
                    dve.wait_ge(S["pv"], 16 * t + 8 * br + 8)
                    V_.tensor_tensor(O[:, br * CHUNK:(br + 1) * CHUNK].rearrange("p (h d) -> p h d", d=HD),
                                     bank[6 + br][:, :].rearrange("p (h d) -> p h d", d=HD),
                                     rden[:, hs].unsqueeze(2).to_broadcast([P, 8, HD]), ALU.mult).then_inc(S["onorm"], 1)
                    dve.wait_ge(S["onorm"], 2 * t + br + 1)
                    dve.sem_inc(free[6 + br], 1)

                scored(0)
                for hd in range(16):
                    if hd + 1 < 16:
                        scored(hd + 1)
                    turned(hd)
                    if hd == 9:
                        normalise(0)
                normalise(1)
                skip(2)
                mix(t)

            dve.wait_ge(S["h"], 2 * TILES)
            rotate(SAMPLE, None)
            for b in range(DEC):
                k, q = kv[b % 2], qbc[b % 2]
                dve.wait_ge(S[f"kv_in{b % 2}"], 96 * (b // 2 + 1))
                dve.wait_ge(S[f"q_in{b % 2}"], 16 * (b // 2 + 1))
                settle()
                mark(V_.tensor_tensor(prod.rearrange("p (c n) -> p c n", c=3), k[:, 0:3 * WA].rearrange("p (c n) -> p c n", c=3),
                                      q[:, 0:WA].unsqueeze(1).to_broadcast([P, 3, WA]), ALU.mult))
                settle()
                mark(V_.tensor_reduce(sS[:, 0:3, b * 8:b * 8 + 8], prod.rearrange("p (c h d) -> p c h d", c=3, d=HD), AX.X, ALU.add))
                settle()
                for c in range(2):
                    mark(V_.tensor_tensor(prod[:, c * WB:(c + 1) * WB].rearrange("p (g r d) -> p g r d", g=KVB, d=HD),
                                          k[:, 3 * WA + c * WK:3 * WA + (c + 1) * WK].rearrange("p (g d) -> p g d", g=KVB)
                                          .unsqueeze(2).to_broadcast([P, KVB, HB // KVB, HD]),
                                          q[:, WA:WA + WB].rearrange("p (g r d) -> p g r d", g=KVB, d=HD), ALU.mult))
                settle()
                V_.tensor_reduce(sS[:, 3:5, b * 8:b * 8 + 8], prod[:, 0:2 * WB].rearrange("p (c h d) -> p c h d", c=2, d=HD),
                                 AX.X, ALU.add).then_inc(S["qk"], 1)
                dve.wait_ge(S["qk"], b + 1)
            i = arrived()
            V_.tensor_tensor_reduce(out=sP[:, 0:384], in0=bank[i][0:64, 0:384], in1=sbias[:, 0:384], scale=-SCALE, scalar=3e38,
                                    op0=ALU.add, op1=ALU.min, accum_out=nm[0:64, 0:1]).then_inc(S["sP"], 1)
            j = arrived()
            V_.tensor_tensor_reduce(out=sP[:, 384:640], in0=bank[j][0:64, 0:256], in1=sbias[:, 384:640], scale=-SCALE,
                                    scalar=nsink_bh[:, 0:1], op0=ALU.add, op1=ALU.min, accum_out=nm[0:64, 1:2])\
                .then_inc(S["sP"], 1)
            dve.wait_ge(S["sP"], 2)
            dve.sem_inc(free[i], 1)
            dve.sem_inc(free[j], 1)
            mark(V_.tensor_tensor(es[0:64, 0:1], nm[0:64, 1:2], nsink_bh[:, :], ALU.subtract))
            settle()
            dve.sem_inc(S["esink"], 1)
            dve.wait_ge(S["esink"], 2 * TILES + 2)
            mark(V_.tensor_tensor(den[0:64, 1:2], den[0:64, 1:2], es[0:64, 0:1], ALU.add))
            settle()
            mark(V_.reciprocal(rden[0:64, 0:2], den[0:64, 0:2]))
            settle()
            V_.tensor_scalar(sP[:, 0:384], sP[:, 0:384], rden[0:64, 0:1], None, ALU.mult).then_inc(S["sW"], 1)
            V_.tensor_scalar(sP[:, 384:640], sP[:, 384:640], rden[0:64, 1:2], None, ALU.mult).then_inc(S["sW"], 1)
            skip(1)
            mark(V_.memset(tmp2, 0.0))
            settle()
            dve.wait_ge(S["sO"], DEC)
            for r in range(2):
                rows = slice(HD * r, HD * r + HD)
                src = bank[6][rows, 0:4 * 66].rearrange("p (c x) -> p c x", x=66)[:, :, r:r + 57:8]
                mark(V_.tensor_copy(oT[rows, 0:4, 0:DEC], src))
                for g in range(KVB):
                    src = bank[7][g * HD:(g + 1) * HD, 0:64].rearrange("p (b h) -> p h b", h=HB)[:, 4 * g + r:4 * g + r + 3:2, :]
                    mark(V_.tensor_copy(oT[rows, 4 + 2 * g:6 + 2 * g, 0:DEC], src))
            i = arrived()
            mark(V_.tensor_copy(skT[:, :, :], bank[i][:, 0:2 * P].rearrange("p (c n) -> p c n", c=2)))
            settle()
            dve.sem_inc(free[i], 1)
            dve.sem_inc(free[6], 1)
            dve.sem_inc(free[7], 1)
            dve.sem_inc(S["sT"], 1)
            mix(SAMPLE)

            def best16(lists):
                dve.nop(nofuse=True)
                for src, val, pos in lists:
                    mark(V_.max(val[:, 0:8], src))
                settle()
                dve.nop(nofuse=True)
                for src, val, pos in lists:
                    mark(V_.max_index(pos[:, 0:8], val[:, 0:8], src))
                settle()
                dve.nop(nofuse=True)
                for src, val, pos in lists:
                    mark(V_.match_replace(src, val[:, 0:8], src, LOW))
                settle()
                dve.nop(nofuse=True)
                for src, val, pos in lists:
                    mark(V_.max(val[:, 8:16], src))
                settle()
                dve.nop(nofuse=True)
                for src, val, pos in lists:
                    mark(V_.max_index(pos[:, 8:16], val[:, 8:16], src))
                settle()
                dve.nop(nofuse=True)

            def choose(t, piece):
                if piece == 0:
                    dve.wait_ge(S["std"], L.up("std"))
                    mark(V_.reciprocal(hrstd, hstd))
                    settle()
                    V_.scalar_tensor_tensor(hnF, row(t, D, 2 * D), hrstd, gffn, ALU.mult, ALU.mult).then_inc(S["hn"], 1)
                    skip(2)
                elif piece <= 4:
                    skip(2)
                    dve.wait_ge(free[5], L.at("full5"))
                    dve.wait_ge(free[4], L.at("full4"))
                    best16([(Ssc[:, l, :], topv[:, l // 2, l % 2, :], topi[:, l // 2, l % 2, :])
                            for l in range(4 * piece - 4, 4 * piece)])
                elif piece == 5:
                    mark(V_.tensor_copy(topif, topi))
                    settle()
                    mark(V_.tensor_scalar(topif[:, :, 0, :], topif[:, :, 0, :], float(NK), None, ALU.mult))
                    settle()
                    for top, out in ((topv, cs), (topif, ce)):
                        at = 0
                        for a, n in RUNS:
                            mark(V_.tensor_tensor(out[:, :, at:at + n], top[:, :, 0, a:a + 1].to_broadcast([P, PH, n]),
                                                  top[:, :, 1, 0:n], ALU.add))
                            at += n
                        mark(V_.tensor_tensor(out[:, :, at:CAND], top[:, :, 0, TOPK // 2:TOPK],
                                              top[:, :, 1, 0:1].to_broadcast([P, PH, TOPK // 2]), ALU.add))
                    settle()
                    best16([(cs[:, h, :], best[:, h, :], bpos[:, h, :]) for h in range(PH)])
                    mark(V_.tensor_copy(bposf, bpos))
                    V_.tensor_tensor(gexp, best, best[:, :, 0:1].to_broadcast([P, PH, TOPK]), ALU.subtract)\
                        .then_inc(S["gexp_in"], 1)
                    dve.wait_ge(S["gexp"], L.up("gexp"))
                    mark(V_.tensor_reduce(gsum, gexp, AX.X, ALU.add))
                    settle()
                    mark(V_.reciprocal(gsum, gsum))
                    settle()
                    out = slots(gate_all, t).rearrange("p (h k) -> p h k", h=PH)
                    mark(V_.tensor_tensor(out, gexp, gsum.unsqueeze(2).to_broadcast([P, PH, TOPK]), ALU.mult))
                    settle()
                else:
                    heads = [4 * (piece - 6) + j for j in range(4)]
                    for j, h in enumerate(heads):
                        mark(V_.tensor_tensor(eqs[j], iota[:, :].unsqueeze(1).to_broadcast([P, TOPK, CAND]),
                                              bposf[:, h, :].unsqueeze(2).to_broadcast([P, TOPK, CAND]), ALU.is_equal))
                    settle()
                    for j, h in enumerate(heads):
                        mark(V_.tensor_tensor(eqs[j], eqs[j], ce[:, h:h + 1, :].to_broadcast([P, TOPK, CAND]), ALU.mult))
                    settle()
                    for j, h in enumerate(heads):
                        mark(V_.tensor_reduce(eF[:, h * TOPK:(h + 1) * TOPK], eqs[j], AX.X, ALU.add))
                    settle()
                    if piece == 7:
                        V_.tensor_copy(slots(e_all, t), eF).then_inc(S["chosen"], 1)

            dve.wait_ge(S["gf_in"], 32)
            L.n["std"], L.n["rstd"] = 1, 1
            for piece in range(GROUPS):
                choose(0, piece)
            gates = gate_all[:, :, :].rearrange("p t n -> p (t n)")

            def finish(rows, out):
                dve.wait_ge(S["ystat"], L.up("ystat", 2))
                V_.tensor_tensor(ysum[0:rows, :], yss[0:rows, 0:1], yss[0:rows, 1:2], ALU.add).then_inc(S["ysum"], 1)
                dve.wait_ge(S["ystd"], L.up("ystd"))
                mark(V_.reciprocal(yrstd[0:rows, :], ystd[0:rows, :]))
                settle()
                for c in range(2):
                    ins = V_.scalar_tensor_tensor(out[c], bank[6 + c][0:rows, :], yrstd[0:rows, :],
                                                  gfin[0:rows, c * CHUNK:(c + 1) * CHUNK], ALU.mult, ALU.mult)
                    ins.then_inc(S["y_ready"], 1) if c else mark(ins)
                dve.wait_ge(S["y_ready"], L.up("y_ready"))
                dve.sem_inc(S["acc_free"], 1)

            with L.loop(dve, TILES, PER_TILE) as t:
                for g in range(GROUPS):
                    for q in range(QUADS):
                        for j in range(QUAD):
                            dve.wait_ge(u_landed[j], L.up(f"u_landed{j}", 16))
                            V_.scalar_tensor_tensor(U[j], U[j], 1.0, row(t, 0, D), ALU.mult, ALU.mult,
                                                    accum_out=dots[:, q % 2, j:j + 1]).then_inc(S["u_used"], 1)
                        dve.wait_ge(S["gelu"], L.up("gelu"))
                        V_.tensor_tensor(wq[:, q % 2, :], gelus[:, q % 2, :],
                                         gates[:, ds(t * SLOTS + g * PER_GROUP + q * QUAD, QUAD)], ALU.mult)\
                            .then_inc(S["w"], 1)
                    choose(t + 1, g)
                dve.wait_ge(S["acc_full"], L.up("acc_full"))
                finish(P, [row(t, D + c * CHUNK, D + (c + 1) * CHUNK) for c in range(2)])
            i = arrived()
            V_.tensor_copy(idxT[:, :], bank[i][:, 0:DEC]).then_inc(S["tT"], 1)
            j = arrived()
            V_.tensor_copy(gateT[:, :], bank[j][:, 0:DEC]).then_inc(S["tT"], 1)
            for b in range(DEC):
                dve.wait_ge(u_landed[b % UR], L.up(f"u_landed{b % UR}", 16))
                dve.wait_ge(S[f"hb_in{b % 4}"], 16 * (b // 4 + 1))
                V_.scalar_tensor_tensor(U[b % UR], U[b % UR], 1.0, hbc[b % 4], ALU.mult, ALU.mult,
                                        accum_out=sdots[:, 0, b:b + 1]).then_inc(S["u_used"], 1)
            dve.wait_ge(S["sg"], 1)
            dve.wait_ge(S["tT"], 2)
            V_.tensor_tensor(WM[:, :, :].rearrange("p a b -> p (a b)")[:, 0:64:9], sdots[:, 1, :], gateT[:, :], ALU.mult)\
                .then_inc(S["swm"], 1)
            dve.wait_ge(S["acc_full"], L.up("acc_full"))
            finish(DEC, [GT[0:DEC, SAMPLE, D + c * CHUNK:D + (c + 1) * CHUNK] for c in range(2)])


_INS = ['x_prompt', 'x_sample', 'cache_a_k', 'cache_a_v', 'cache_b_k', 'cache_b_v', 'norm_mix', 'w_in', 'w_branch_a',
        'w_branch_b', 'w_out', 'sink_b', 'norm_ffn', 'w_peer_q', 'peer_sub_keys', 'peer_u', 'peer_v', 'norm_final']
_OUTS = [(1, SEQ, D), (DEC, 1, D), (1, 1, SEQ, HA, HD), (1, 1, SEQ, HA, HD), (1, 1, P, KVB, HD), (1, 1, P, KVB, HD),
         (1, DEC, PAST, HA, HD), (1, DEC, PAST, HA, HD), (1, DEC, P, KVB, HD), (1, DEC, P, KVB, HD)]


def _tables():
    t, s = np.arange(P)[:, None], np.arange(P)[None, :]

    def count_a(off, near):
        n = (near & (off <= 128)).astype(int) + (off % 4 == 0) + (off % 16 == 0)
        return np.where(off >= 0, n, 0)

    def bias(n):
        return np.where(n > 0, np.log(np.maximum(n, 1)) / SCALE, NEG)

    a = [bias(count_a(t - s + P * d, True)) for d in (3, 2, 1, 0)]
    b = [bias(((t - s + P * d >= 0) & (t - s + P * d <= 128)).astype(int)) for d in (1, 0)]
    masks = np.concatenate(a + b, 1).astype(np.float32)
    inv = (10000.0 ** (-np.arange(0, HD, 2, dtype=np.float32) / HD)).astype(np.float32)
    pos = np.stack([np.arange(P) + P * i for i in range(TILES)] + [np.full(P, PAST)], 1).astype(np.float32)
    ang = (pos[:, :, None] * inv).astype(np.float32).astype(np.float64)
    c, sn = np.cos(ang), np.sin(ang)
    rope = np.stack([np.concatenate([c, c], -1), np.concatenate([-sn, sn], -1)], 2).astype(np.float32)
    near = np.arange(PAST - P, PAST)
    mid = np.arange(PAST - CHUNK, PAST - P, 4)
    n = np.zeros((3, P), int)
    n[0] = 1 + (near % 4 == 0) + (near % 16 == 0)
    n[1, :FAR] = 1 + (mid % 16 == 0)
    n[1, FAR] = 3
    n[2, :FAR] = 1
    m = np.zeros((2, P), int)
    m[0] = 1
    m[1, 0] = 1
    sb = np.concatenate([bias(n).reshape(-1), bias(m).reshape(-1)])
    sb = np.tile(sb.astype(np.float32), (DEC * HB, 1))
    return {"masks": masks, "rope": rope.reshape(P, -1), "sbias": sb, "ident": np.eye(P, dtype=np.float32),
            "iota": np.arange(CAND, dtype=np.float32)}


def kernel(**inputs):
    import concourse.bacc as _bacc
    from concourse import mybir as _mybir
    from concourse.bass_utils import run_bass_kernel_spmd as _run

    nc = _bacc.Bacc("TRN2", target_bir_lowering=False, num_devices=1)
    arrays, args = {}, []
    named = [(n, np.ascontiguousarray(inputs[n])) for n in _INS] + list(_tables().items())
    for name, a in named:
        arrays[f"in_{name}_dram"] = a
        args.append(nc.dram_tensor(f"in_{name}_dram", a.shape, _mybir.dt.from_np(a.dtype), kind="ExternalInput").ap())
    for i, shape in enumerate(_OUTS):
        args.append(nc.dram_tensor(f"out_{i}_dram", shape, _mybir.dt.float32, kind="ExternalOutput").ap())
    ways = ["o s d -> (o s) d", "b o d -> (b o) d"] + ["o b s h d -> (o b) s (h d)"] * 4
    ways += ["o d -> (o d)"] + ["o k n -> (o k) n"] * 4 + ["o h -> (o h)", "o d -> (o d)", "o k n -> (o k) n",
                                                        "o c n d -> (o c) n d", "o e d -> (o e) d", "o e d -> (o e) d"]
    ways += [None] * 6
    ways += ["o s d -> (o s) d", "b o d -> (b o) d"] + ["o b s h d -> (o b s) (h d)"] * 4 + ["o b s h d -> (o b) s (h d)"] * 4
    assert len(ways) == len(args)
    hybrid_step_kernel(nc, *[a if w is None else a.rearrange(w) for a, w in zip(args, ways)])
    r = _run(nc, [arrays], core_ids=[0])
    return tuple(r.results[0][f"out_{i}_dram"] for i in range(len(_OUTS)))
```

```python
import numpy as np
import concourse.bass as bass
from concourse import mybir
from contextlib import ExitStack, contextmanager

P = 128
D = 1024
KO = D // P
SEQ, DEC, PAST = 512, 8, 2048
TILES = SEQ // P
SAMPLE = TILES
ALL = TILES + 1
HD, HA, HB, KVB = 64, 8, 8, 2
WA, WB, WK = HA * HD, HB * HD, KVB * HD
QA, KA, VA, QB, KB, VB = 0, WA, 2 * WA, 3 * WA, 3 * WA + WB, 3 * WA + WB + WK
ZW = 3 * WA + WB + 2 * WK
D_IN = ZW + 2 * D
SCALE = HD ** -0.5
NEG = -1e30
EPS = 1e-6
CHUNK = 512
NK, PH, TOPK = 128, 8, 16
SLOTS = PH * TOPK
LISTS = 2 * PH
RUNS = [(a, TOPK // (a + 1)) for a in range(TOPK // 2)]
RUNS_AT = [(a, n, sum(m for _, m in RUNS[:a])) for a, n in RUNS]
CAND = sum(n for _, n in RUNS) + TOPK // 2
LOW = -3e38
FAR = 96
UR, VR = 4, 8
QUAD = 4
STEPS = SLOTS // QUAD
def HEAD(step, lag):
    h, rest = divmod(step - 3 - lag, 3)
    return h if rest == 0 and 0 <= h < PH else None
PROMPT_SLOTS = TILES * SLOTS

PER_TILE = {
    "full4": 9, "full5": 9, "free4": 9, "free5": 9,
    "stat": 1, "std": 1, "rstd": 1, "hn": 1, "hn_kept": 1,
    "u_used": SLOTS, "v_used": SLOTS, "gelu": SLOTS // QUAD, "w": SLOTS // QUAD, "diag": SLOTS,
    "residual": 1, "acc_full": 1, "acc_free": 1, "ystat": 2, "ysum": 1, "ystd": 1, "yrstd": 1, "y_out": 16,
    "idx": SLOTS // QUAD, "gexp_in": 1, "gexp": 1, "chosen": PH, "listed": PH, "gated": 1, "y_ready": 1,
    "dve": 309,
    **{f"u_landed{j}": 16 * SLOTS // UR for j in range(UR)},
    **{f"v_landed{j}": 16 * SLOTS // VR for j in range(VR)},
}

class Ledger:

    def __init__(self):
        self.n, self.loops = {}, []

    def at(self, name):
        v = self.n.get(name, 0)
        for var, per in self.loops:
            if per.get(name, 0):
                v = var * per[name] + v
        return v

    def up(self, name, by=1):
        self.n[name] = self.n.get(name, 0) + by
        return self.at(name)

    @contextmanager
    def loop(self, eng, trips, per):
        start = dict(self.n)
        with eng.Fori(0, trips) as var:
            self.loops.append((var, per))
            yield var
            self.loops.pop()
        for name in self.n:
            turn = self.n[name] - start.get(name, 0)
            assert turn in (0, per.get(name, 0)), (name, turn, per.get(name, 0))
            if turn:
                self.n[name] = start.get(name, 0) + trips * turn


def hybrid_step_kernel(nc, x_p, x_s, cak, cav, cbk, cbv, g_mix, w_in, w_a, w_b, w_o, sink, g_ffn, w_pq, subk,
                       pu, pv, g_fin, masks_d, rope_d, sbias_d, ident_d, iota_d,
                       y_p, y_s, akp, avp, bkp, bvp, aks, avs, bks, bvs):
    f32, u32 = mybir.dt.float32, mybir.dt.uint32
    ALU, ACT, AX = mybir.AluOpType, mybir.ActivationFunctionType, mybir.AxisListType
    ds = bass.ds
    q_scratch = nc.dram_tensor("q_scratch", (DEC, WA + WB), f32).ap()
    hn_scratch = nc.dram_tensor("hn_scratch", (DEC, D), f32).ap()

    with ExitStack() as ctx:
        def sb(name, shape, dt=f32):
            return ctx.enter_context(nc.sbuf_tensor(name, shape, dt))

        KTW, KBTW = (WA // P) * SEQ, KVB * SEQ
        arena = sb("arena", [P, ALL * ZW + KTW + KBTW])
        Z = arena[:, 0:ALL * ZW].rearrange("p (t n) -> p t n", t=ALL)
        KT = arena[:, ALL * ZW:ALL * ZW + KTW].rearrange("p (c n) -> p c n", c=WA // P)
        KBT = arena[:, ALL * ZW + KTW:ALL * ZW + KTW + KBTW].rearrange("p (g n) -> p g n", g=KVB)
        GT = sb("GT", [P, ALL, 2 * D])
        WR = sb("WR", [P, 16 * D])
        XS = sb("XS", [P, KO * ALL * P])
        PP = sb("PP", [P, 2 * D])
        GF = sb("GF", [P, 2 * D])
        ident = sb("ident", [P, P])
        skT = sb("skT", [P, 2, NK])
        iota = sb("iota", [P, CAND])
        gmix = sb("gmix", [P, KO])
        nsink = sb("nsink", [P, HB])
        nsink_bh = sb("nsink_bh", [DEC * HB, 1])
        stats = sb("stats", [P, 96])
        e_all = sb("e_all", [P, ALL, SLOTS], u32)
        gate_all = sb("gate_all", [P, ALL, SLOTS])
        idxq = sb("idxq", [P, 4, QUAD], u32)
        dots = sb("dots", [P, 2, QUAD])
        gelus = sb("gelus", [P, 2, QUAD])
        wq = sb("wq", [P, 2, QUAD])

        GTf = GT[:, :, :].rearrange("p t n -> p (t n)")

        def row(t, lo, hi):
            return GTf[:, ds(t * (2 * D) + lo, hi - lo)]

        def slots(buf, t):
            return buf[:, :, :].rearrange("p t n -> p (t n)")[:, ds(t * SLOTS, SLOTS)]

        xT = XS[:, :].rearrange("p (k n) -> p k n", k=KO)
        ring = [WR[:, i * KO * CHUNK:(i + 1) * KO * CHUNK].rearrange("p (k n) -> p k n", k=KO) for i in range(2)]
        w_ab = WR[:, 8 * D:16 * D].rearrange("p (k n) -> p k n", k=8)
        w_out = WR[:, 0:8 * D].rearrange("p (k n) -> p k n", k=KO)
        w_q = WR[:, :].rearrange("p (k n) -> p k n", k=KO)
        NHR = 2 * HA + HB + KVB
        rot = XS[:, 0:NHR * HD]
        KD = XS[:, NHR * HD:NHR * HD + 4 * HD]
        o0 = NHR * HD + 4 * HD
        tmp1, tmp2 = XS[:, o0:o0 + D], XS[:, o0 + D:o0 + 2 * D]
        O = tmp1
        oT = tmp2.rearrange("p (k n) -> p k n", k=KO)
        qT = XS[:, o0 + 2 * D:o0 + 3 * D].rearrange("p (k n) -> p k n", k=KO)
        M = XS[:, 0:D]
        mT = qT
        Pr = PP[:, 0:D].rearrange("p (a n) -> p a n", a=2)
        PrT = PP[:, D:2 * D].rearrange("p (a n) -> p a n", a=2)
        maskA = GF[:, 0:4 * P]
        maskB = GF[:, 4 * P:6 * P]
        rope = GF[:, 768:768 + ALL * 2 * HD].rearrange("p (t c d) -> p t c d", t=ALL, c=2)
        sbias = GF[0:DEC * HB, 1408:2048]
        gffn, gfin = GF[:, 0:D], GF[:, D:2 * D]
        KVW = 3 * WA + 2 * WK
        SA = WR[:, 8 * D:16 * D]
        kv = [SA[:, i * KVW:(i + 1) * KVW] for i in range(2)]
        s0 = 2 * KVW
        prod = SA[:, s0:s0 + 3 * WA]
        qbc = [SA[:, s0 + 3 * WA + i * D:s0 + 3 * WA + (i + 1) * D] for i in range(2)]
        s1 = s0 + 3 * WA + 2 * D
        sS = SA[:, s1:s1 + 5 * 64].rearrange("p (c n) -> p c n", c=5)
        sP = SA[0:64, s1 + 320:s1 + 320 + 640]
        sPT = SA[:, s0:s0 + 320].rearrange("p (c n) -> p c n", c=5)
        qpT = XS[:, 0:4 * P].rearrange("p (b c n) -> p b c n", b=2, c=2)
        Ssc = XS[:, 4 * P:8 * P].rearrange("p (b c n) -> p b c n", b=2, c=2)
        hnT = XS[:, 4 * D:5 * D].rearrange("p (k n) -> p k n", k=KO)
        hnF = PP[:, 0:D]
        topv = PP[:, D:D + 256].rearrange("p (h c k) -> p h c k", h=PH, c=2)
        topi = PP[:, D + 256:D + 512].bitcast(u32).rearrange("p (h c k) -> p h c k", h=PH, c=2)
        best = PP[:, D + 512:D + 640].rearrange("p (h k) -> p h k", h=PH)
        bpos = PP[:, D + 640:D + 768].bitcast(u32).rearrange("p (h k) -> p h k", h=PH)
        bposf = PP[:, D + 768:D + 896].rearrange("p (h k) -> p h k", h=PH)
        eF = PP[:, D + 896:D + 1024]
        U = [arena[:, j * D:(j + 1) * D] for j in range(UR)]
        V = [arena[:, (UR + j) * D:(UR + j + 1) * D] for j in range(VR)]
        c0 = (UR + VR) * D
        diag = arena[:, c0:c0 + 8 * P].rearrange("p (j n) -> p j n", j=8)
        cs = arena[:, c0 + D:c0 + D + PH * CAND].rearrange("p (h c) -> p h c", h=PH)
        ce = arena[:, c0 + D + PH * CAND:c0 + D + 2 * PH * CAND].rearrange("p (h c) -> p h c", h=PH)
        gexp = arena[:, c0 + 1824:c0 + 1952].rearrange("p (h k) -> p h k", h=PH)
        topif = arena[:, c0 + 1824:c0 + 2080].rearrange("p (h c k) -> p h c k", h=PH, c=2)
        eq = XS[:, D:D + TOPK * CAND].rearrange("p (k c) -> p k c", k=TOPK)
        hbc = [XS[:, j * D:(j + 1) * D] for j in range(4)]
        ss, std, rstd = stats[:, 0:5], stats[:, 5:10], stats[:, 10:15]
        nm, den, rden, es = stats[:, 16:32], stats[:, 32:48], stats[:, 48:64], stats[:, 64:72]
        hss, hstd, hrstd = stats[:, 72:73], stats[:, 73:74], stats[:, 74:75]
        yss, ysum, ystd, yrstd = stats[:, 76:78], stats[:, 78:79], stats[:, 79:80], stats[:, 80:81]
        gsum = stats[:, 82:90]
        epsc = stats[:, 90:91]
        zero_col = sb("zero_col", [1, P])
        oTs = sb("oTs", [P, KO, DEC])
        idxT = sb("idxT", [P, DEC], u32)
        gateT = sb("gateT", [P, DEC])
        sdots = sb("sdots", [P, 3, DEC])
        WM = sb("WM", [P, DEC, DEC])

        bank = [ctx.enter_context(nc.psum_tensor(f"bank{i}", [P, CHUNK], f32)) for i in range(8)]

        names = {}

        def sem(name):
            if name not in names:
                names[name] = ctx.enter_context(nc.semaphore(name))
            return names[name]

        full = [sem(f"full{i}") for i in range(8)]
        free = [sem(f"free{i}") for i in range(8)]
        for n in ("x_in", "const_in", "w_in0", "w_in1", "wab_in", "wout_in", "wq_in", "gf_in", "x_zero", "copies",
                  "stat", "std", "rstd", "xs", "rot", "stores", "probs", "pt", "pv", "onorm", "merged", "x_again",
                  "h", "dve", "kvzero", "q_out", "kv_in0", "kv_in1", "q_in0", "q_in1", "qk", "sP", "sE", "sW", "sO",
                  "sT", "hn", "hn_kept", "u_used", "v_used", "gelu", "w", "diag", "residual", "acc_full", "acc_free",
                  "ystat", "ysum", "ystd", "yrstd", "y_out", "idx", "gexp_in", "gexp", "chosen", "y_ready", "act",
                  "hn_out", "listed", "gated", "id_in", "rot_s", "hb_in0", "hb_in1", "hb_in2", "hb_in3", "esink", "sd", "sg", "swm", "tT", "oT_zero", "eps"):
            sem(n)
        S = names
        u_landed = [sem(f"u_landed{j}") for j in range(UR)]
        v_landed = [sem(f"v_landed{j}") for j in range(VR)]

        block = ctx.enter_context(nc.Block())

        w_in_v = w_in.rearrange("(k p) n -> p k n", p=P)
        w_a_v = w_a.rearrange("(k p) n -> p k n", p=P)
        w_b_v = w_b.rearrange("(k p) n -> p k n", p=P)
        w_o_v = w_o.rearrange("(k p) n -> p k n", p=P)
        w_pq_v = w_pq.rearrange("(k p) n -> p k n", p=P)
        PAIR_AT = [0, 2 * CHUNK, ZW, ZW + 2 * CHUNK]
        XLOADS, CONSTS = 16 * ALL, 16 * 14

        MISC = 14
        KROWS = (PAST - P, PAST - CHUNK, 0)

        @block.sync
        def _(sp):
            L = Ledger()
            for t in range(TILES):
                sp.dma_start(GT[:, t, 0:D], x_p[t * P:(t + 1) * P, :]).then_inc(S["x_in"], 16)
            sp.wait_ge(S["x_zero"], 1)
            sp.dma_start(GT[0:DEC, SAMPLE, 0:D], x_s).then_inc(S["x_in"], 16)
            sp.dma_start(ident[:, :], ident_d).then_inc(S["id_in"], 16)
            sp.dma_start(gmix[:, :], g_mix.rearrange("(k p) -> p k", p=P), allow_slow_non_contiguous=True).then_inc(S["id_in"], 16)
            sp.dma_start(ring[1][:, :, 0:2 * WK], w_in_v[:, :, KB:KB + 2 * WK]).then_inc(S["w_in1"], 16)
            sp.dma_start(ring[0], w_in_v[:, :, 0:CHUNK]).then_inc(S["w_in0"], 16)
            sp.dma_start(GF[:, 0:768], masks_d).then_inc(S["const_in"], 16)
            sp.dma_start(GF[:, 768:1408], rope_d).then_inc(S["const_in"], 16)
            sp.dma_start(sbias, sbias_d).then_inc(S["const_in"], 16)
            sp.dma_start(iota[:, :], iota_d.partition_broadcast(P)).then_inc(S["const_in"], 16)
            sp.dma_start(nsink[:, :], sink.partition_broadcast(P)).then_inc(S["const_in"], 16)
            for b in range(DEC):
                sp.dma_start(nsink_bh[b * HB:(b + 1) * HB, :], sink.rearrange("(h o) -> h o", o=1)).then_inc(S["const_in"], 16)
            sp.dma_start(skT[:, :, :], subk.rearrange("c n d -> n c d")).then_inc(S["const_in"], 16)

            copies = [(c[b], o[b]) for b in range(DEC) for c, o in ((cak, aks), (cav, avs))]

            def copy_a():
                src, dst = copies.pop(0)
                n = (PAST - DEC_NEW) * WA // 64
                sp.dma_start(dst[0:PAST - 1, :].rearrange("s n -> (s n)").rearrange("(a n) -> a n", n=n),
                             src[1:PAST, :].rearrange("s n -> (s n)").rearrange("(a n) -> a n", n=n)).then_inc(S["copies"], 16)

            DEC_NEW = 1
            sp.dma_start(bks[:, 0:P - 1, :], cbk[:, 1:P, :]).then_inc(S["copies"], 16)
            sp.dma_start(bvs[:, 0:P - 1, :], cbv[:, 1:P, :]).then_inc(S["copies"], 16)

            def chunk(p, c):
                if p or c:
                    sp.wait_ge(full[6], 2 * p + c)
                    sp.dma_start(ring[c], w_in_v[:, :, PAIR_AT[p] + c * CHUNK:PAIR_AT[p] + (c + 1) * CHUNK])\
                        .then_inc(S[f"w_in{c}"], 16)
                copy_a()

            for p in range(3):
                for c in range(2):
                    chunk(p, c)
            sp.wait_ge(S["rot_s"], 1)
            sp.dma_start(aks[:, PAST - 1, :], Z[0:DEC, SAMPLE, KA:KA + WA]).then_inc(S["q_out"], 16)
            sp.dma_start(avs[:, PAST - 1, :], Z[0:DEC, SAMPLE, VA:VA + WA]).then_inc(S["q_out"], 16)
            sp.dma_start(bks[:, P - 1, :], Z[0:DEC, SAMPLE, KB:KB + WK]).then_inc(S["q_out"], 16)
            sp.dma_start(bvs[:, P - 1, :], Z[0:DEC, SAMPLE, VB:VB + WK]).then_inc(S["q_out"], 16)
            sp.dma_start(q_scratch[:, 0:WA], Z[0:DEC, SAMPLE, QA:QA + WA]).then_inc(S["q_out"], 16)
            sp.dma_start(q_scratch[:, WA:WA + WB], Z[0:DEC, SAMPLE, QB:QB + WB]).then_inc(S["q_out"], 16)
            sp.wait_ge(S["q_out"], 96)
            sp.wait_ge(S["kvzero"], 2)
            for i in range(2 * DEC):
                if i in (3, 6):
                    chunk(3, i // 6)
                b, r = i % DEC, i % 2
                ca, cb, na, nb = (cak, cbk, aks, bks) if i < DEC else (cav, cbv, avs, bvs)
                if 2 <= i <= DEC + 1:
                    sp.wait_ge(S["qk"], i - 1)
                elif i > DEC + 1:
                    sp.wait_ge(S["sO"], i - DEC - 1)
                k = kv[r]
                sem_kv = S[f"kv_in{r}"]
                sp.dma_start(k[:, 0:WA], ca[b, PAST - P:PAST, :]).then_inc(sem_kv, 16)
                sp.dma_start(k[0:FAR, WA:2 * WA], ca[b, PAST - CHUNK:PAST - P:4, :]).then_inc(sem_kv, 16)
                sp.dma_start(k[FAR:FAR + 1, WA:2 * WA], na[b, PAST - 1:PAST, :]).then_inc(sem_kv, 16)
                sp.dma_start(k[0:FAR, 2 * WA:3 * WA], ca[b, 0:PAST - CHUNK:16, :]).then_inc(sem_kv, 16)
                sp.dma_start(k[:, 3 * WA:3 * WA + WK], cb[b, :, :]).then_inc(sem_kv, 16)
                sp.dma_start(k[0:1, 3 * WA + WK:KVW], nb[b, P - 1:P, :]).then_inc(sem_kv, 16)
                if i < DEC:
                    sp.dma_start(qbc[r], q_scratch[b, :].partition_broadcast(P)).then_inc(S[f"q_in{r}"], 16)
            sp.wait_ge(S["sO"], DEC)
            sp.dma_start(w_ab[:, 0:4, :], w_a_v).then_inc(S["wab_in"], 16)
            sp.dma_start(w_ab[:, 4:8, :], w_b_v).then_inc(S["wab_in"], 16)
            sp.wait_ge(full[6], 9)
            sp.dma_start(w_out, w_o_v).then_inc(S["wout_in"], 16)
            for t in range(TILES):
                copy_a()
                sp.wait_ge(S["rot"], t + 1)
                rows = slice(t * P, (t + 1) * P)
                sp.dma_start(akp[rows, :], rot[:, WA:2 * WA]).then_inc(S["stores"], 16)
                sp.dma_start(avp[rows, :], Z[:, t, VA:VA + WA]).then_inc(S["stores"], 16)
                if t == TILES - 1:
                    sp.dma_start(bkp, rot[:, 2 * WA + WB:2 * WA + WB + WK]).then_inc(S["stores"], 16)
                    sp.dma_start(bvp, Z[:, t, VB:VB + WK]).then_inc(S["stores"], 16)
                copy_a()
                sp.wait_ge(S["merged"], 2 * (t + 1))
                sp.dma_start(GT[:, t, D:2 * D], x_p[rows, :]).then_inc(S["x_again"], 16)

            sp.wait_ge(S["merged"], 2 * ALL)
            sp.dma_start(GT[0:DEC, SAMPLE, D:2 * D], x_s).then_inc(S["x_again"], 16)
            sp.wait_ge(S["h"], 2 * ALL)
            sp.dma_start(w_q, w_pq_v).then_inc(S["wq_in"], 16)
            sp.dma_start(gffn, g_ffn.partition_broadcast(P)).then_inc(S["gf_in"], 16)
            sp.dma_start(gfin, g_fin.partition_broadcast(P)).then_inc(S["gf_in"], 16)
            while copies:
                copy_a()
            with L.loop(sp, TILES - 1, PER_TILE) as t:
                sp.wait_ge(S["y_ready"], L.up("y_ready"))
                sp.dma_start(y_p[ds(t * P, P), :], GTf[:, ds(t * (2 * D) + D, D)]).then_inc(S["y_out"], 16)
            sp.wait_ge(S["hn_kept"], ALL)
            sp.dma_start(hn_scratch, GT[0:DEC, SAMPLE, 0:D]).then_inc(S["hn_out"], 16)
            sp.wait_ge(S["hn_out"], 16)
            sp.wait_ge(S["gated"], ALL)
            for b in range(DEC):
                if b >= 4:
                    sp.wait_ge(S["u_used"], UR + PROMPT_SLOTS + b - 3)
                sp.dma_start(hbc[b % 4], hn_scratch[b, :].partition_broadcast(P)).then_inc(S[f"hb_in{b % 4}"], 16)
            sp.wait_ge(S["y_ready"], TILES)
            sp.dma_start(y_p[SEQ - P:SEQ, :], GT[:, TILES - 1, D:2 * D]).then_inc(S["y_out"], 16)
            sp.wait_ge(S["y_ready"], ALL)
            sp.dma_start(y_s, GT[0:DEC, SAMPLE, D:2 * D]).then_inc(S["y_out"], 16)
            sp.wait_ge(S["y_out"], 16 * ALL)
            sp.wait_ge(S["stores"], 16 * (2 * TILES + 2))
            sp.wait_ge(S["copies"], 16 * 18)

        @block.gpsimd
        def _(pool):
            L = Ledger()
            nc.gpsimd.memset(GT[:, SAMPLE, 0:D], 0.0).then_inc(S["x_zero"], 1)
            nc.gpsimd.memset(epsc, EPS).then_inc(S["eps"], 1)
            nc.gpsimd.memset(WM[:, :, :], 0.0).then_inc(S["eps"], 1)
            nc.gpsimd.memset(kv[0], 0.0).then_inc(S["kvzero"], 1)
            nc.gpsimd.memset(kv[1], 0.0).then_inc(S["kvzero"], 1)

            pool.wait_ge(S["h"], 2 * ALL)

            def gather(dst, table, idx, landed):
                nc.gpsimd.indirect_dma_start(dst, None, table, bass.IndirectOffsetOnAxis(ap=idx, axis=0))\
                    .then_inc(landed, 16)

            experts = e_all[:, :, :].rearrange("p t n -> p (t n)")
            with L.loop(pool, TILES, PER_TILE) as t:
                for s in range(SLOTS):
                    if s % TOPK == 0:
                        pool.wait_ge(S["chosen"], L.up("chosen"))
                        pool.nop(nofuse=True)
                    if s % QUAD == 0:
                        q = s // QUAD % 4
                        nc.gpsimd.tensor_copy(idxq[:, q, :], experts[:, ds(t * SLOTS + s, QUAD)]).then_inc(S["idx"], 1)
                        pool.wait_ge(S["idx"], L.up("idx"))
                        pool.nop(nofuse=True)
                    pool.wait_ge(S["u_used"], L.up("u_used"))
                    pool.nop(nofuse=True)
                    gather(U[s % UR], pu, idxq[:, q, s % QUAD:s % QUAD + 1], u_landed[s % UR])
                    pool.wait_ge(S["v_used"], L.up("v_used"))
                    pool.nop(nofuse=True)
                    gather(V[s % VR], pv, idxq[:, q, s % QUAD:s % QUAD + 1], v_landed[s % VR])
            pool.wait_ge(S["tT"], 2)
            for b in range(DEC):
                pool.wait_ge(S["u_used"], L.up("u_used"))
                gather(U[b % UR], pu, idxT[:, b:b + 1], u_landed[b % UR])
                pool.wait_ge(S["v_used"], L.up("v_used"))
                gather(V[b], pv, idxT[:, b:b + 1], v_landed[b])

        @block.scalar
        def _(act):
            L = Ledger()
            act.wait_ge(S["x_in"], XLOADS)
            act.wait_ge(S["eps"], 1)
            for t in range(ALL):
                nc.scalar.activation(GT[:, t, D:2 * D], GT[:, t, 0:D], ACT.Square, accum_out=ss[:, t:t + 1])\
                    .then_inc(S["stat"], 1)
            act.wait_ge(S["stat"], ALL)
            nc.scalar.activation(std, ss, ACT.Sqrt, bias=epsc, scale=1.0 / D).then_inc(S["std"], 1)

            for m in range(ALL):
                act.wait_ge(full[2 + m], 1)
                nc.scalar.activation(Z[:, m, KB:KB + 2 * WK], bank[2 + m][:, 0:2 * WK], ACT.Copy).then_inc(free[2 + m], 1)
            zf = arena[:, 0:ALL * ZW]
            with act.Fori(0, 2) as p:
                for c in range(2):
                    for m in range(ALL):
                        act.wait_ge(full[2 + m], p * 2 + (c + 2))
                        nc.scalar.activation(zf[:, ds(p * (2 * CHUNK) + (m * ZW + c * CHUNK), CHUNK)], bank[2 + m][:, :],
                                             ACT.Copy).then_inc(free[2 + m], 1)
            gf = GT[:, :, :].rearrange("p t n -> p (t n)")
            with act.Fori(0, 2) as p:
                for c in range(2):
                    for m in range(ALL):
                        act.wait_ge(full[2 + m], p * 2 + (c + 6))
                        nc.scalar.activation(gf[:, ds(p * D + (m * 2 * D + c * CHUNK), CHUNK)], bank[2 + m][:, :],
                                             ACT.Sigmoid).then_inc(free[2 + m], 1)
            for m in range(ALL):
                L.n[f"full{2 + m}"] = 9
            misc = [0]

            def evac(dst, width=CHUNK):
                i = 4 + misc[0] % 2
                misc[0] += 1
                act.wait_ge(full[i], L.up(f"full{i}"))
                nc.scalar.activation(dst, bank[i][:, 0:width] if len(dst.shape) == 2 else
                                     bank[i][:, 0:width].rearrange("p (k n) -> p k n", n=P), ACT.Copy).then_inc(free[i], 1)

            def skip(n):
                for _ in range(n):
                    L.up(f"full{4 + misc[0] % 2}")
                    misc[0] += 1

            def mix():
                skip(4)
                evac(mT[:, 0:4, :])
                evac(mT[:, 4:8, :])
                skip(2)

            act.wait_ge(S["sP"], 2)
            nc.scalar.activation(sP[:, 0:384], sP[:, 0:384], ACT.Exp, bias=nm[0:64, 0:1], scale=-1.0,
                                 accum_out=den[0:64, 0:1]).then_inc(S["sE"], 1)
            nc.scalar.activation(sP[:, 384:640], sP[:, 384:640], ACT.Exp, bias=nm[0:64, 1:2], scale=-1.0,
                                 accum_out=den[0:64, 1:2]).then_inc(S["sE"], 1)
            act.wait_ge(S["esink"], 1)
            nc.scalar.activation(es[0:64, 0:1], es[0:64, 0:1], ACT.Exp).then_inc(S["esink"], 1)
            skip(2)
            i = 4 + misc[0] % 2
            misc[0] += 1
            act.wait_ge(full[i], L.up(f"full{i}"))
            nc.scalar.activation(sPT, bank[i][:, 0:320].rearrange("p (c n) -> p c n", c=5), ACT.Copy).then_inc(free[i], 1)
            skip(1)

            for t in range(TILES):
                cols = slice(t * P, (t + 1) * P)
                evac(qT[:, 0:4, :])
                evac(KT[:, :, cols])
                evac(qT[:, 4:8, :])
                evac(KBT[:, :, cols], 2 * P)
                for hd in range(HA + HB):
                    n = (t + 1) * P if hd < HA else min(t + 1, 2) * P
                    act.wait_ge(free[hd % 2], ALL + 8 * t + hd // 2 + 1)
                    nc.scalar.activation(Pr[:, hd % 2, 0:n], Pr[:, hd % 2, 0:n], ACT.Exp, bias=nm[:, hd:hd + 1], scale=-1.0,
                                         accum_out=den[:, hd:hd + 1]).then_inc(S["probs"], 1)
                act.wait_ge(S["esink"], 2 * t + 3)
                nc.scalar.activation(es, es, ACT.Exp).then_inc(S["esink"], 1)
                evac(oT[:, 0:4, :])
                evac(oT[:, 4:8, :])
                mix()
            mix()


            def choose(t, step):
                if step == 0:
                    nc.scalar.activation(hnF, row(t, D, 2 * D), ACT.Square, accum_out=hss).then_inc(S["stat"], 1)
                    act.wait_ge(S["stat"], L.up("stat"))
                    nc.scalar.activation(hstd, hss, ACT.Sqrt, bias=epsc, scale=1.0 / D).then_inc(S["std"], 1)
                if step == 1:
                    act.wait_ge(S["hn"], L.up("hn"))
                    nc.scalar.activation(row(t, 0, D), hnF, ACT.Copy).then_inc(S["hn_kept"], 1)
                if step == 2:
                    evac(hnT[:, 0:4, :])
                    evac(hnT[:, 4:8, :])
                if (h := HEAD(step, 2)) is not None:
                    evac(qpT[:, h % 2, :, :], 2 * P)
                if (h := HEAD(step, 4)) is not None:
                    n = L.at("listed")
                    if not (isinstance(n, int) and n < 2):
                        act.wait_ge(S["listed"], n - 1)
                    L.up("listed")
                    evac(Ssc[:, h % 2, :, :], 2 * P)
                if step == STEPS - 1:
                    act.wait_ge(S["gexp_in"], L.up("gexp_in"))
                    nc.scalar.activation(gexp, gexp, ACT.Exp).then_inc(S["gexp"], 1)

            L.n["stat"], L.n["hn"] = ALL, 0
            act.wait_ge(S["h"], 2 * ALL)
            L.n["v_used"] = VR
            for step in range(STEPS):
                choose(0, step)

            L.n["u_used"] = UR
            L.n["v_used"] = VR

            with L.loop(act, TILES, PER_TILE) as t:
                for q in range(STEPS):
                    act.wait_ge(S["u_used"], L.up("u_used", QUAD))
                    nc.scalar.activation(gelus[:, q % 2, :], dots[:, q % 2, :], ACT.Gelu).then_inc(S["gelu"], 1)
                    act.wait_ge(S["w"], L.up("w"))
                    act.wait_ge(S["v_used"], L.up("v_used", QUAD) - 2 * QUAD)
                    for j in range(QUAD):
                        nc.scalar.activation(diag[:, QUAD * (q % 2) + j, :], ident[:, :], ACT.Copy,
                                             scale=wq[:, q % 2, j:j + 1]).then_inc(S["diag"], 1)
                    choose(t + 1, q)
                act.wait_ge(S["acc_full"], L.up("acc_full"))
                for c in range(2):
                    nc.scalar.activation(PP[:, 0:CHUNK], bank[6 + c][:, :], ACT.Square, accum_out=yss[:, c:c + 1])\
                        .then_inc(S["ystat"], 1)
                    act.wait_ge(S["ystat"], L.up("ystat"))
                act.wait_ge(S["ysum"], L.up("ysum"))
                nc.scalar.activation(ystd, ysum, ACT.Sqrt, bias=epsc, scale=1.0 / D).then_inc(S["ystd"], 1)
            act.wait_ge(S["u_used"], UR + PROMPT_SLOTS + DEC)
            nc.scalar.activation(sdots[:, 1, :], sdots[:, 0, :], ACT.Gelu).then_inc(S["sg"], 1)
            act.wait_ge(S["acc_full"], L.up("acc_full"))
            for c in range(2):
                nc.scalar.activation(PP[0:DEC, 0:CHUNK], bank[6 + c][0:DEC, :], ACT.Square, accum_out=yss[0:DEC, c:c + 1])\
                    .then_inc(S["ystat"], 1)
                act.wait_ge(S["ystat"], L.up("ystat"))
            act.wait_ge(S["ysum"], L.up("ysum"))
            nc.scalar.activation(ystd[0:DEC, :], ysum[0:DEC, :], ACT.Sqrt, bias=epsc[0:DEC, :], scale=1.0 / D)\
                .then_inc(S["ystd"], 1)

        @block.tensor
        def _(pe):
            L = Ledger()

            def claim(i):
                n = L.at(f"free{i}")
                if not (isinstance(n, int) and n == 0):
                    pe.wait_ge(free[i], n)
                L.up(f"free{i}")

            pe.wait_ge(S["id_in"], 32)
            misc = [0]

            def next_bank():
                i = 4 + misc[0] % 2
                misc[0] += 1
                claim(i)
                return i

            def transpose_x(m):
                pe.wait_ge(S["xs"], m + 1)
                for half in range(2):
                    claim(half)
                    for k in range(4):
                        col = D + (4 * half + k) * P
                        last = nc.tensor.transpose(bank[half][:, k * P:(k + 1) * P], GT[:, m, col:col + P], ident[:, :])
                    last.then_inc(full[half], 1)

            transpose_x(0)
            for m in range(ALL):
                if m + 1 < ALL:
                    transpose_x(m + 1)
                pe.wait_ge(free[0], m + 1)
                pe.wait_ge(free[1], m + 1)
                pe.wait_ge(S["w_in1"], 16)
                for k in range(KO):
                    last = nc.tensor.matmul(bank[2 + m][:, 0:2 * WK], xT[:, k, m * P:(m + 1) * P], ring[1][:, k, 0:2 * WK],
                                            start=(k == 0), stop=(k == KO - 1))
                last.then_inc(full[2 + m], 1)
            with pe.Fori(0, 4) as p:
                for c in range(2):
                    pe.wait_ge(S[f"w_in{c}"], p * 16 + (16 if c == 0 else 32))
                    for m in range(ALL):
                        pe.wait_ge(free[2 + m], p * 2 + (1 + c))
                        for k in range(KO):
                            last = nc.tensor.matmul(bank[2 + m][:, :], xT[:, k, m * P:(m + 1) * P], ring[c][:, k, :],
                                                    start=(k == 0), stop=(k == KO - 1))
                        last.then_inc(full[2 + m], 1)
            for m in range(ALL):
                L.n[f"free{2 + m}"] = 9

            def transposes(src, blocks):
                i = next_bank()
                for k in range(blocks):
                    last = nc.tensor.transpose(bank[i][:, k * P:(k + 1) * P], src[:, k * P:(k + 1) * P], ident[:, :])
                last.then_inc(full[i], 1)
                return i

            def mix(t):
                pe.wait_ge(S["wab_in"], 32)
                if t == SAMPLE:
                    pe.wait_ge(S["sT"], 1)
                for n in range(2):
                    for br in range(2):
                        i = next_bank()
                        for k in range(4):
                            last = nc.tensor.matmul(bank[i][:, :], oT[:, 4 * br + k, :], w_ab[:, 4 * br + k, n * CHUNK:(n + 1) * CHUNK],
                                                    start=(k == 0), stop=(k == 3))
                        last.then_inc(full[i], 1)
                pe.wait_ge(S["merged"], 2 * t + 2)
                a = transposes(M[:, 0:CHUNK], 4)
                b = transposes(M[:, CHUNK:D], 4)
                pe.wait_ge(S["wout_in"], 16)
                pe.wait_ge(free[a], L.at(f"free{a}"))
                pe.wait_ge(free[b], L.at(f"free{b}"))
                for n in range(2):
                    i = next_bank()
                    for k in range(KO):
                        last = nc.tensor.matmul(bank[i][:, :], mT[:, k, :], w_out[:, k, n * CHUNK:(n + 1) * CHUNK],
                                                start=(k == 0), stop=(k == KO - 1))
                    last.then_inc(full[i], 1)

            pe.wait_ge(S["qk"], DEC)
            for tiles in ((0, 3), (3, 5)):
                i = next_bank()
                for c in range(*tiles):
                    last = nc.tensor.transpose(bank[i][0:64, (c - tiles[0]) * P:(c - tiles[0] + 1) * P], sS[:, c, :], ident[:, :])
                last.then_inc(full[i], 1)
            pe.wait_ge(S["sW"], 2)
            i = next_bank()
            for c in range(5):
                last = nc.tensor.transpose(bank[i][:, c * 64:(c + 1) * 64], sP[:, c * P:(c + 1) * P], ident[0:64, 0:64])
            last.then_inc(full[i], 1)
            claim(6)
            claim(7)
            pe.wait_ge(free[i], L.at(f"free{i}"))
            for b in range(DEC):
                v = kv[b % 2]
                pe.wait_ge(S[f"kv_in{b % 2}"], 96 * (DEC // 2 + b // 2 + 1))
                for pair in range(4):
                    for c in range(3):
                        nc.tensor.matmul(bank[6][:, pair * 64 + b * 8:pair * 64 + b * 8 + 8], v[:, c * WA + pair * P:c * WA + (pair + 1) * P],
                                         sPT[:, c, b * 8:b * 8 + 8], start=(c == 0), stop=(c == 2))
                for c in range(2):
                    last = nc.tensor.matmul(bank[7][:, b * 8:b * 8 + 8], v[:, 3 * WA + c * WK:3 * WA + (c + 1) * WK],
                                            sPT[:, 3 + c, b * 8:b * 8 + 8], start=(c == 0), stop=(c == 1))
                last.then_inc(S["sO"], 1)
            pe.wait_ge(S["const_in"], CONSTS)
            i = next_bank()
            for c in range(2):
                last = nc.tensor.transpose(bank[i][:, c * P:(c + 1) * P], skT[:, c, :], ident[:, :])
            last.then_inc(full[i], 1)

            for t in range(TILES):
                pe.wait_ge(S["rot"], t + 1)
                transposes(rot[:, 0:WA], 4)
                transposes(rot[:, WA:2 * WA], 4)
                a = transposes(rot[:, 2 * WA:2 * WA + WB], 4)
                b = transposes(KD, 2)
                pe.wait_ge(free[a], L.at(f"free{a}"))
                pe.wait_ge(free[b], L.at(f"free{b}"))

                def span(hd):
                    return (0, t + 1) if hd < HA else (max(t - 1, 0), t + 1)

                def score(hd):
                    lo, hi = span(hd)
                    h = hd % 8
                    r = slice(HD * (h % 2), HD * (h % 2) + HD)
                    claim(hd % 2)
                    keys = KT[r, h // 2, lo * P:hi * P] if hd < HA else KBT[r, h // 4, lo * P:hi * P]
                    nc.tensor.matmul(bank[hd % 2][:, 0:(hi - lo) * P], qT[r, (hd // 8) * 4 + h // 2, :], keys,
                                     start=True, stop=True).then_inc(full[hd % 2], 1)

                def turn(hd):
                    lo, hi = span(hd)
                    pe.wait_ge(S["probs"], t * 16 + hd + 1)
                    claim(2 + hd % 2)
                    for k in range(hi - lo):
                        last = nc.tensor.transpose(bank[2 + hd % 2][:, k * P:(k + 1) * P], Pr[:, hd % 2, k * P:(k + 1) * P], ident[:, :])
                    last.then_inc(full[2 + hd % 2], 1)

                def values(hd):
                    lo, hi = span(hd)
                    h = hd % 8
                    if h == 0:
                        claim(6 + hd // 8)
                    pe.wait_ge(free[2 + hd % 2], 9 * (2 + hd % 2 >= 2) + 8 * t + hd // 2 + 1)
                    at = VA + h * HD if hd < HA else VB + (h // 4) * HD
                    for k in range(hi - lo):
                        last = nc.tensor.matmul(bank[6 + hd // 8][:, h * HD:(h + 1) * HD], PrT[:, hd % 2, k * P:(k + 1) * P],
                                                Z[:, lo + k, at:at + HD], start=(k == 0), stop=(k == hi - lo - 1))
                    last.then_inc(S["pv"], 1)

                NH = HA + HB
                score(0)
                for hd in range(NH):
                    if hd + 1 < NH:
                        score(hd + 1)
                    turn(hd)
                    if hd:
                        values(hd - 1)
                values(NH - 1)
                pe.wait_ge(S["onorm"], 2 * t + 2)
                a = transposes(O[:, 0:CHUNK], 4)
                b = transposes(O[:, CHUNK:D], 4)
                pe.wait_ge(free[a], L.at(f"free{a}"))
                pe.wait_ge(free[b], L.at(f"free{b}"))
                mix(t)

            mix(SAMPLE)

            item = {}

            def choose(t, step):
                if step == 1:
                    pe.wait_ge(S["hn"], L.up("hn"))
                    transposes(hnF[:, 0:CHUNK], 4)
                    transposes(hnF[:, CHUNK:D], 4)
                if (h := HEAD(step, 3)) is not None:
                    pe.wait_ge(free[item["q"]], L.at(f"free{item['q']}"))
                    i = next_bank()
                    for c in range(2):
                        last = nc.tensor.matmul(bank[i][:, c * P:(c + 1) * P], qpT[:, h % 2, c, :], skT[:, c, :],
                                                start=True, stop=True)
                    last.then_inc(full[i], 1)
                for c in range(2):
                    if (h := HEAD(step, c)) is not None:
                        if h == 0 and c == 0:
                            pe.wait_ge(free[4], L.at("free4"))
                            pe.wait_ge(free[5], L.at("free5"))
                        if c == 0:
                            item["q"] = next_bank()
                        i = item["q"]
                        for k in range(KO):
                            last = nc.tensor.matmul(bank[i][:, c * P:(c + 1) * P], w_q[:, k, (2 * h + c) * P:(2 * h + c + 1) * P],
                                                    hnT[:, k, :], start=(k == 0), stop=(k == KO - 1))
                        if c:
                            last.then_inc(full[i], 1)

            pe.wait_ge(S["wq_in"], 16)
            for step in range(STEPS):
                choose(0, step)
            with L.loop(pe, TILES, PER_TILE) as t:
                pe.wait_ge(S["acc_free"], L.up("acc_free"))
                for c in range(2):
                    nc.tensor.matmul(bank[6 + c][:, :], ident[:, :],
                                     row(t, D + c * CHUNK, D + (c + 1) * CHUNK),
                                     start=True, stop=False, skip_group_check=True)
                for s in range(SLOTS):
                    j = s % VR
                    pe.wait_ge(v_landed[j], L.up(f"v_landed{j}", 16))
                    pe.wait_ge(S["diag"], L.up("diag"))
                    for c in range(2):
                        last = nc.tensor.matmul(bank[6 + c][:, :], diag[:, j, :], V[j][:, c * CHUNK:(c + 1) * CHUNK],
                                                start=False, stop=False, skip_group_check=True)
                    last.then_inc(S["v_used"], 1)
                    if s % QUAD == QUAD - 1:
                        choose(t + 1, s // QUAD)
                for c in range(2):
                    last = nc.tensor.matmul(bank[6 + c][:, :], zero_col[0:1, :], gffn[0:1, 0:CHUNK],
                                            start=False, stop=True, skip_group_check=True)
                last.then_inc(S["acc_full"], 1)

            pe.wait_ge(S["gated"], ALL)
            for src in (eF, gate_all[:, SAMPLE, :]):
                i = next_bank()
                nc.tensor.transpose(bank[i][:, 0:P], src, ident[:, :]).then_inc(full[i], 1)
            pe.wait_ge(S["acc_free"], L.up("acc_free"))
            for c in range(2):
                nc.tensor.matmul(bank[6 + c][0:DEC, :], ident[0:DEC, 0:DEC], GT[0:DEC, SAMPLE, D + c * CHUNK:D + (c + 1) * CHUNK],
                                 start=True, stop=False, skip_group_check=True)
            pe.wait_ge(S["swm"], 1)
            for b in range(DEC):
                pe.wait_ge(v_landed[b], L.up(f"v_landed{b}", 16))
                for c in range(2):
                    last = nc.tensor.matmul(bank[6 + c][0:DEC, :], WM[:, b, :], V[b][:, c * CHUNK:(c + 1) * CHUNK],
                                            start=False, stop=(b == DEC - 1), skip_group_check=True)
            last.then_inc(S["acc_full"], 1)

        @block.vector
        def _(dve):
            L = Ledger()

            def mark(ins):
                ins.then_inc(S["dve"], 1)
                L.up("dve")

            def settle():
                dve.wait_ge(S["dve"], L.at("dve"))
            V_ = nc.vector
            mark(V_.memset(zero_col[0:1, :], 0.0))
            dve.sem_inc(S["u_used"], UR)
            dve.sem_inc(S["v_used"], VR)
            dve.sem_inc(S["acc_free"], 1)
            dve.wait_ge(S["std"], 1)
            V_.reciprocal(rstd, std).then_inc(S["rstd"], 1)
            dve.wait_ge(S["rstd"], 1)
            for t in range(ALL):
                V_.tensor_scalar(GT[:, t, D:2 * D], GT[:, t, 0:D], rstd[:, t:t + 1], None, ALU.mult).then_inc(S["xs"], 1)
            dve.wait_ge(S["id_in"], 32)
            for m in range(ALL):
                for half in range(2):
                    dve.wait_ge(full[half], m + 1)
                    V_.tensor_tensor(xT[:, 4 * half:4 * half + 4, m * P:(m + 1) * P],
                                     bank[half][:, :].rearrange("p (k n) -> p k n", k=4),
                                     gmix[:, 4 * half:4 * half + 4].unsqueeze(2).to_broadcast([P, 4, P]), ALU.mult)\
                        .then_inc(free[half], 1)
            L.n["full4"] = L.n["full5"] = 9
            misc = [0]

            def skip(n):
                for _ in range(n):
                    L.up(f"full{4 + misc[0] % 2}")
                    misc[0] += 1

            def arrived():
                i = 4 + misc[0] % 2
                misc[0] += 1
                dve.wait_ge(full[i], L.up(f"full{i}"))
                return i

            def rotate(t):
                for src, dst, heads in ((QA, 0, 2 * HA), (QB, 2 * HA, HB + KVB)):
                    z = Z[:, t, src:src + heads * HD].rearrange("p (h d) -> p h d", d=HD)
                    first, second = (PP[:, 0:D], PP[:, D:2 * D]) if t == SAMPLE else (tmp1, tmp2)
                    a = first[:, 0:heads * HD].rearrange("p (h d) -> p h d", d=HD)
                    b = second[:, 0:heads * HD].rearrange("p (h d) -> p h d", d=HD)
                    out = z if t == SAMPLE else rot[:, dst * HD:(dst + heads) * HD].rearrange("p (h d) -> p h d", d=HD)
                    H = HD // 2
                    settle()
                    mark(V_.tensor_tensor(a, z, rope[:, t, 0:1, :].to_broadcast([P, heads, HD]), ALU.mult))
                    mark(V_.tensor_tensor(b[:, :, 0:H], z[:, :, H:HD], rope[:, t, 1:2, 0:H].to_broadcast([P, heads, H]), ALU.mult))
                    mark(V_.tensor_tensor(b[:, :, H:HD], z[:, :, 0:H], rope[:, t, 1:2, H:HD].to_broadcast([P, heads, H]), ALU.mult))
                    settle()
                    mark(V_.tensor_tensor(out, a, b, ALU.add))
                settle()
                if t == SAMPLE:
                    dve.sem_inc(S["rot_s"], 1)
                    return
                k = rot[:, (2 * HA + HB) * HD:NHR * HD].rearrange("p (g d) -> p g d", g=KVB)
                kd = KD.rearrange("p (g c d) -> p g c d", g=KVB, c=2)
                mark(V_.tensor_copy(kd[:, :, 0, :], k))
                V_.tensor_copy(kd[:, :, 1, :], k).then_inc(S["rot"], 1)

            def mix(t):
                for n in range(2):
                    c = slice(n * CHUNK, (n + 1) * CHUNK)
                    for br in range(2):
                        g = GT[:, t, br * D + n * CHUNK:br * D + (n + 1) * CHUNK]
                        i = arrived()
                        V_.tensor_tensor(g, g, bank[i][:, :], ALU.mult).then_inc(free[i], 1)
                    dve.wait_ge(free[5], L.at("full5"))
                    if n == 0 and t < TILES:
                        dve.wait_ge(S["stores"], 32 * (t + 1) + (32 if t == TILES - 1 else 0))
                    V_.tensor_tensor(M[:, c], GT[:, t, c], GT[:, t, D + n * CHUNK:D + (n + 1) * CHUNK], ALU.add)\
                        .then_inc(S["merged"], 1)
                skip(2)
                dve.wait_ge(S["x_again"], 16 * (t + 1))
                for n in range(2):
                    i = arrived()
                    h = GT[:, t, D + n * CHUNK:D + (n + 1) * CHUNK]
                    V_.tensor_tensor(h, h, bank[i][:, :], ALU.add).then_inc(free[i], 1)
                dve.wait_ge(free[5], L.at("full5"))
                dve.wait_ge(free[4], L.at("full4"))
                dve.sem_inc(S["h"], 2)

            dve.wait_ge(free[2 + SAMPLE], 5)
            dve.wait_ge(S["const_in"], CONSTS)
            mark(V_.tensor_scalar(nsink[:, :], nsink[:, :], -1.0, None, ALU.mult))
            mark(V_.tensor_scalar(nsink_bh[:, :], nsink_bh[:, :], -1.0, None, ALU.mult))
            rotate(SAMPLE)
            for b in range(DEC):
                k, q = kv[b % 2], qbc[b % 2]
                dve.wait_ge(S[f"kv_in{b % 2}"], 96 * (b // 2 + 1))
                dve.wait_ge(S[f"q_in{b % 2}"], 16 * (b // 2 + 1))
                settle()
                mark(V_.tensor_tensor(prod.rearrange("p (c n) -> p c n", c=3), k[:, 0:3 * WA].rearrange("p (c n) -> p c n", c=3),
                                      q[:, 0:WA].unsqueeze(1).to_broadcast([P, 3, WA]), ALU.mult))
                settle()
                mark(V_.tensor_reduce(sS[:, 0:3, b * 8:b * 8 + 8], prod.rearrange("p (c h d) -> p c h d", c=3, d=HD), AX.X, ALU.add))
                settle()
                for c in range(2):
                    mark(V_.tensor_tensor(prod[:, c * WB:(c + 1) * WB].rearrange("p (g r d) -> p g r d", g=KVB, d=HD),
                                          k[:, 3 * WA + c * WK:3 * WA + (c + 1) * WK].rearrange("p (g d) -> p g d", g=KVB)
                                          .unsqueeze(2).to_broadcast([P, KVB, HB // KVB, HD]),
                                          q[:, WA:WA + WB].rearrange("p (g r d) -> p g r d", g=KVB, d=HD), ALU.mult))
                settle()
                V_.tensor_reduce(sS[:, 3:5, b * 8:b * 8 + 8], prod[:, 0:2 * WB].rearrange("p (c h d) -> p c h d", c=2, d=HD),
                                 AX.X, ALU.add).then_inc(S["qk"], 1)
                dve.wait_ge(S["qk"], b + 1)
            i = arrived()
            V_.tensor_tensor_reduce(out=sP[:, 0:384], in0=bank[i][0:64, 0:384], in1=sbias[:, 0:384], scale=-SCALE, scalar=3e38,
                                    op0=ALU.add, op1=ALU.min, accum_out=nm[0:64, 0:1]).then_inc(S["sP"], 1)
            j = arrived()
            V_.tensor_tensor_reduce(out=sP[:, 384:640], in0=bank[j][0:64, 0:256], in1=sbias[:, 384:640], scale=-SCALE,
                                    scalar=nsink_bh[:, 0:1], op0=ALU.add, op1=ALU.min, accum_out=nm[0:64, 1:2])\
                .then_inc(S["sP"], 1)
            dve.wait_ge(S["sP"], 2)
            dve.sem_inc(free[i], 1)
            dve.sem_inc(free[j], 1)
            mark(V_.tensor_tensor(es[0:64, 0:1], nm[0:64, 1:2], nsink_bh[:, :], ALU.subtract))
            settle()
            dve.sem_inc(S["esink"], 1)
            dve.wait_ge(S["esink"], 2)
            mark(V_.tensor_tensor(den[0:64, 1:2], den[0:64, 1:2], es[0:64, 0:1], ALU.add))
            settle()
            mark(V_.reciprocal(rden[0:64, 0:2], den[0:64, 0:2]))
            settle()
            V_.tensor_scalar(sP[:, 0:384], sP[:, 0:384], rden[0:64, 0:1], None, ALU.mult).then_inc(S["sW"], 1)
            V_.tensor_scalar(sP[:, 384:640], sP[:, 384:640], rden[0:64, 1:2], None, ALU.mult).then_inc(S["sW"], 1)
            skip(1)
            dve.wait_ge(S["sO"], DEC)
            for r in range(2):
                rows = slice(HD * r, HD * r + HD)
                src = bank[6][rows, 0:4 * 66].rearrange("p (c x) -> p c x", x=66)[:, :, r:r + 57:8]
                mark(V_.tensor_copy(oTs[rows, 0:4, :], src))
                for g in range(KVB):
                    src = bank[7][g * HD:(g + 1) * HD, 0:64].rearrange("p (b h) -> p h b", h=HB)[:, 4 * g + r:4 * g + r + 3:2, :]
                    mark(V_.tensor_copy(oTs[rows, 4 + 2 * g:6 + 2 * g, :], src))
            i = arrived()
            mark(V_.tensor_copy(skT[:, :, :], bank[i][:, 0:2 * P].rearrange("p (c n) -> p c n", c=2)))
            settle()
            dve.sem_inc(free[i], 1)
            dve.sem_inc(free[6], 1)
            dve.sem_inc(free[7], 1)
            dve.wait_ge(full[6], 9)
            for m in range(ALL):
                dve.wait_ge(free[2 + m], 9)

            for t in range(TILES):
                if t:
                    dve.wait_ge(S["h"], 2 * t)
                rotate(t)
                skip(4)

                def scored(hd):
                    lo, hi = (0, t + 1) if hd < HA else (max(t - 1, 0), t + 1)
                    n = (hi - lo) * P
                    mask = maskA[:, 4 * P - n:4 * P] if hd < HA else maskB[:, 2 * P - n:2 * P]
                    dve.wait_ge(full[hd % 2], ALL + 8 * t + hd // 2 + 1)
                    if hd >= 2 or t:
                        dve.wait_ge(full[2 + hd % 2], 9 + 8 * t + hd // 2)
                    V_.tensor_tensor_reduce(out=Pr[:, hd % 2, 0:n], in0=bank[hd % 2][:, 0:n], in1=mask, scale=-SCALE,
                                            scalar=3e38 if hd < HA else nsink[:, hd - HA:hd - HA + 1],
                                            op0=ALU.add, op1=ALU.min, accum_out=nm[:, hd:hd + 1]).then_inc(free[hd % 2], 1)

                def turned(hd):
                    n = (t + 1) * P if hd < HA else min(t + 1, 2) * P
                    dve.wait_ge(full[2 + hd % 2], 9 + 8 * t + hd // 2 + 1)
                    if hd >= 2 or t:
                        dve.wait_ge(S["pv"], 16 * t + hd - 1)
                    V_.tensor_copy(PrT[:, hd % 2, 0:n], bank[2 + hd % 2][:, 0:n]).then_inc(free[2 + hd % 2], 1)

                def normalise(br):
                    hs = slice(8 * br, 8 * br + 8)
                    if br:
                        mark(V_.tensor_tensor(es, nm[:, 8:16], nsink[:, :], ALU.subtract))
                        settle()
                        dve.sem_inc(S["esink"], 1)
                        dve.wait_ge(S["esink"], 2 * t + 4)
                        mark(V_.tensor_tensor(den[:, 8:16], den[:, 8:16], es, ALU.add))
                        settle()
                    else:
                        dve.wait_ge(S["probs"], 16 * t + 8)
                    mark(V_.reciprocal(rden[:, hs], den[:, hs]))
                    settle()
                    dve.wait_ge(S["pv"], 16 * t + 8 * br + 8)
                    V_.tensor_tensor(O[:, br * CHUNK:(br + 1) * CHUNK].rearrange("p (h d) -> p h d", d=HD),
                                     bank[6 + br][:, :].rearrange("p (h d) -> p h d", d=HD),
                                     rden[:, hs].unsqueeze(2).to_broadcast([P, 8, HD]), ALU.mult).then_inc(S["onorm"], 1)
                    dve.wait_ge(S["onorm"], 2 * t + br + 1)
                    dve.sem_inc(free[6 + br], 1)

                scored(0)
                for hd in range(16):
                    if hd + 1 < 16:
                        scored(hd + 1)
                    turned(hd)
                    if hd == 9:
                        normalise(0)
                normalise(1)
                skip(2)
                mix(t)

            dve.wait_ge(S["h"], 2 * TILES)
            mark(V_.memset(tmp2, 0.0))
            settle()
            mark(V_.tensor_copy(oT[:, :, 0:DEC], oTs[:, :, :]))
            settle()
            dve.sem_inc(S["sT"], 1)
            mix(SAMPLE)

            def best16(lists):
                dve.nop(nofuse=True)
                for src, val, pos in lists:
                    mark(V_.max(val[:, 0:8], src))
                settle()
                dve.nop(nofuse=True)
                for src, val, pos in lists:
                    mark(V_.max_index(pos[:, 0:8], val[:, 0:8], src))
                settle()
                dve.nop(nofuse=True)
                for src, val, pos in lists:
                    mark(V_.match_replace(src, val[:, 0:8], src, LOW))
                settle()
                dve.nop(nofuse=True)
                for src, val, pos in lists:
                    mark(V_.max(val[:, 8:16], src))
                settle()
                dve.nop(nofuse=True)
                for src, val, pos in lists:
                    mark(V_.max_index(pos[:, 8:16], val[:, 8:16], src))
                settle()
                dve.nop(nofuse=True)

            def choose(t, step):
                if step == 0:
                    dve.wait_ge(S["std"], L.up("std"))
                    mark(V_.reciprocal(hrstd, hstd))
                    settle()
                    V_.scalar_tensor_tensor(hnF, row(t, D, 2 * D), hrstd, gffn, ALU.mult, ALU.mult).then_inc(S["hn"], 1)
                    skip(2)
                if (h := HEAD(step, 5)) is not None:
                    skip(2)
                    dve.wait_ge(free[5], L.at("full5"))
                    best16([(Ssc[:, h % 2, c, :], topv[:, h, c, :], topi[:, h, c, :]) for c in range(2)])
                    V_.tensor_copy(topif[:, h, :, :], topi[:, h, :, :]).then_inc(S["listed"], 1)
                    top = topv[:, h, :, :]
                    for a, n, at in RUNS_AT:
                        mark(V_.tensor_scalar(cs[:, h, at:at + n], top[:, 1, 0:n], top[:, 0, a:a + 1], None, ALU.add))
                    mark(V_.tensor_scalar(cs[:, h, CAND - TOPK // 2:CAND], top[:, 0, TOPK // 2:TOPK], top[:, 1, 0:1], None, ALU.add))
                    dve.wait_ge(S["listed"], L.up("listed"))
                    dve.nop(nofuse=True)
                    mark(V_.tensor_scalar(topif[:, h, 0, :], topif[:, h, 0, :], float(NK), None, ALU.mult))
                    settle()
                    top = topif[:, h, :, :]
                    for a, n, at in RUNS_AT:
                        mark(V_.tensor_scalar(ce[:, h, at:at + n], top[:, 1, 0:n], top[:, 0, a:a + 1], None, ALU.add))
                    mark(V_.tensor_scalar(ce[:, h, CAND - TOPK // 2:CAND], top[:, 0, TOPK // 2:TOPK], top[:, 1, 0:1], None, ALU.add))
                    settle()
                if (h := HEAD(step, 6)) is not None:
                    best16([(cs[:, h, :], best[:, h, :], bpos[:, h, :])])
                    mark(V_.tensor_copy(bposf[:, h, :], bpos[:, h, :]))
                    settle()
                    mark(V_.tensor_tensor(eq, iota[:, :].unsqueeze(1).to_broadcast([P, TOPK, CAND]),
                                          bposf[:, h, :].unsqueeze(2).to_broadcast([P, TOPK, CAND]), ALU.is_equal))
                    settle()
                    mark(V_.tensor_tensor(eq, eq, ce[:, h:h + 1, :].to_broadcast([P, TOPK, CAND]), ALU.mult))
                    settle()
                    mark(V_.tensor_reduce(eF[:, h * TOPK:(h + 1) * TOPK], eq, AX.X, ALU.add))
                    settle()
                    V_.tensor_copy(e_all[:, :, :].rearrange("p t n -> p (t n)")[:, ds(t * SLOTS + h * TOPK, TOPK)],
                                   eF[:, h * TOPK:(h + 1) * TOPK]).then_inc(S["chosen"], 1)
                if step == STEPS - 1:
                    V_.tensor_tensor(gexp, best, best[:, :, 0:1].to_broadcast([P, PH, TOPK]), ALU.subtract)\
                        .then_inc(S["gexp_in"], 1)
                    dve.wait_ge(S["gexp"], L.up("gexp"))
                    mark(V_.tensor_reduce(gsum, gexp, AX.X, ALU.add))
                    settle()
                    mark(V_.reciprocal(gsum, gsum))
                    settle()
                    out = slots(gate_all, t).rearrange("p (h k) -> p h k", h=PH)
                    V_.tensor_tensor(out, gexp, gsum.unsqueeze(2).to_broadcast([P, PH, TOPK]), ALU.mult).then_inc(S["gated"], 1)
                    dve.wait_ge(S["gated"], L.up("gated"))

            dve.wait_ge(S["gf_in"], 32)
            L.n["std"], L.n["rstd"] = 1, 1
            for step in range(STEPS):
                choose(0, step)
            gates = gate_all[:, :, :].rearrange("p t n -> p (t n)")

            def finish(rows, out):
                dve.wait_ge(S["ystat"], L.up("ystat", 2))
                V_.tensor_tensor(ysum[0:rows, :], yss[0:rows, 0:1], yss[0:rows, 1:2], ALU.add).then_inc(S["ysum"], 1)
                dve.wait_ge(S["ystd"], L.up("ystd"))
                mark(V_.reciprocal(yrstd[0:rows, :], ystd[0:rows, :]))
                settle()
                for c in range(2):
                    ins = V_.scalar_tensor_tensor(out[c], bank[6 + c][0:rows, :], yrstd[0:rows, :],
                                                  gfin[0:rows, c * CHUNK:(c + 1) * CHUNK], ALU.mult, ALU.mult)
                    ins.then_inc(S["y_ready"], 1) if c else mark(ins)
                dve.wait_ge(S["y_ready"], L.up("y_ready"))
                dve.sem_inc(S["acc_free"], 1)

            with L.loop(dve, TILES, PER_TILE) as t:
                for q in range(STEPS):
                    for j in range(QUAD):
                        dve.wait_ge(u_landed[j], L.up(f"u_landed{j}", 16))
                        V_.scalar_tensor_tensor(U[j], U[j], 1.0, row(t, 0, D), ALU.mult, ALU.mult,
                                                accum_out=dots[:, q % 2, j:j + 1]).then_inc(S["u_used"], 1)
                    dve.wait_ge(S["gelu"], L.up("gelu"))
                    V_.tensor_tensor(wq[:, q % 2, :], gelus[:, q % 2, :], gates[:, ds(t * SLOTS + q * QUAD, QUAD)], ALU.mult)\
                        .then_inc(S["w"], 1)
                    choose(t + 1, q)
                dve.wait_ge(S["acc_full"], L.up("acc_full"))
                finish(P, [row(t, D + c * CHUNK, D + (c + 1) * CHUNK) for c in range(2)])
            i = arrived()
            V_.tensor_copy(idxT[:, :], bank[i][:, 0:DEC]).then_inc(S["tT"], 1)
            j = arrived()
            V_.tensor_copy(gateT[:, :], bank[j][:, 0:DEC]).then_inc(S["tT"], 1)
            for b in range(DEC):
                dve.wait_ge(u_landed[b % UR], L.up(f"u_landed{b % UR}", 16))
                dve.wait_ge(S[f"hb_in{b % 4}"], 16 * (b // 4 + 1))
                V_.scalar_tensor_tensor(U[b % UR], U[b % UR], 1.0, hbc[b % 4], ALU.mult, ALU.mult,
                                        accum_out=sdots[:, 0, b:b + 1]).then_inc(S["u_used"], 1)
            dve.wait_ge(S["sg"], 1)
            dve.wait_ge(S["tT"], 2)
            V_.tensor_tensor(WM[:, :, :].rearrange("p a b -> p (a b)")[:, 0:64:9], sdots[:, 1, :], gateT[:, :], ALU.mult)\
                .then_inc(S["swm"], 1)
            dve.wait_ge(S["acc_full"], L.up("acc_full"))
            finish(DEC, [GT[0:DEC, SAMPLE, D + c * CHUNK:D + (c + 1) * CHUNK] for c in range(2)])


_INS = ['x_prompt', 'x_sample', 'cache_a_k', 'cache_a_v', 'cache_b_k', 'cache_b_v', 'norm_mix', 'w_in', 'w_branch_a',
        'w_branch_b', 'w_out', 'sink_b', 'norm_ffn', 'w_peer_q', 'peer_sub_keys', 'peer_u', 'peer_v', 'norm_final']
_OUTS = [(1, SEQ, D), (DEC, 1, D), (1, 1, SEQ, HA, HD), (1, 1, SEQ, HA, HD), (1, 1, P, KVB, HD), (1, 1, P, KVB, HD),
         (1, DEC, PAST, HA, HD), (1, DEC, PAST, HA, HD), (1, DEC, P, KVB, HD), (1, DEC, P, KVB, HD)]


def _tables():
    t, s = np.arange(P)[:, None], np.arange(P)[None, :]

    def count_a(off, near):
        n = (near & (off <= 128)).astype(int) + (off % 4 == 0) + (off % 16 == 0)
        return np.where(off >= 0, n, 0)

    def bias(n):
        return np.where(n > 0, np.log(np.maximum(n, 1)) / SCALE, NEG)

    a = [bias(count_a(t - s + P * d, True)) for d in (3, 2, 1, 0)]
    b = [bias(((t - s + P * d >= 0) & (t - s + P * d <= 128)).astype(int)) for d in (1, 0)]
    masks = np.concatenate(a + b, 1).astype(np.float32)
    inv = (10000.0 ** (-np.arange(0, HD, 2, dtype=np.float32) / HD)).astype(np.float32)
    pos = np.stack([np.arange(P) + P * i for i in range(TILES)] + [np.full(P, PAST)], 1).astype(np.float32)
    ang = (pos[:, :, None] * inv).astype(np.float32).astype(np.float64)
    c, sn = np.cos(ang), np.sin(ang)
    rope = np.stack([np.concatenate([c, c], -1), np.concatenate([-sn, sn], -1)], 2).astype(np.float32)
    near = np.arange(PAST - P, PAST)
    mid = np.arange(PAST - CHUNK, PAST - P, 4)
    n = np.zeros((3, P), int)
    n[0] = 1 + (near % 4 == 0) + (near % 16 == 0)
    n[1, :FAR] = 1 + (mid % 16 == 0)
    n[1, FAR] = 3
    n[2, :FAR] = 1
    m = np.zeros((2, P), int)
    m[0] = 1
    m[1, 0] = 1
    sb = np.concatenate([bias(n).reshape(-1), bias(m).reshape(-1)])
    sb = np.tile(sb.astype(np.float32), (DEC * HB, 1))
    return {"masks": masks, "rope": rope.reshape(P, -1), "sbias": sb, "ident": np.eye(P, dtype=np.float32),
            "iota": np.arange(CAND, dtype=np.float32)}


def kernel(**inputs):
    import concourse.bacc as _bacc
    from concourse import mybir as _mybir
    from concourse.bass_utils import run_bass_kernel_spmd as _run

    nc = _bacc.Bacc("TRN2", target_bir_lowering=False, num_devices=1)
    arrays, args = {}, []
    named = [(n, np.ascontiguousarray(inputs[n])) for n in _INS] + list(_tables().items())
    for name, a in named:
        arrays[f"in_{name}_dram"] = a
        args.append(nc.dram_tensor(f"in_{name}_dram", a.shape, _mybir.dt.from_np(a.dtype), kind="ExternalInput").ap())
    for i, shape in enumerate(_OUTS):
        args.append(nc.dram_tensor(f"out_{i}_dram", shape, _mybir.dt.float32, kind="ExternalOutput").ap())
    ways = ["o s d -> (o s) d", "b o d -> (b o) d"] + ["o b s h d -> (o b) s (h d)"] * 4
    ways += ["o d -> (o d)"] + ["o k n -> (o k) n"] * 4 + ["o h -> (o h)", "o d -> (o d)", "o k n -> (o k) n",
                                                        "o c n d -> (o c) n d", "o e d -> (o e) d", "o e d -> (o e) d"]
    ways += [None] * 6
    ways += ["o s d -> (o s) d", "b o d -> (b o) d"] + ["o b s h d -> (o b s) (h d)"] * 4 + ["o b s h d -> (o b) s (h d)"] * 4
    assert len(ways) == len(args)
    hybrid_step_kernel(nc, *[a if w is None else a.rearrange(w) for a, w in zip(args, ways)])
    r = _run(nc, [arrays], core_ids=[0])
    return tuple(r.results[0][f"out_{i}_dram"] for i in range(len(_OUTS)))
```

```python
import numpy as np
import concourse.bass as bass
from concourse import mybir
from contextlib import ExitStack, contextmanager

P = 128
D = 1024
KO = D // P
SEQ, DEC, PAST = 512, 8, 2048
TILES = SEQ // P
SAMPLE = TILES
ALL = TILES + 1
HD, HA, HB, KVB = 64, 8, 8, 2
WA, WB, WK = HA * HD, HB * HD, KVB * HD
QA, KA, VA, QB, KB, VB = 0, WA, 2 * WA, 3 * WA, 3 * WA + WB, 3 * WA + WB + WK
ZW = 3 * WA + WB + 2 * WK
D_IN = ZW + 2 * D
SCALE = HD ** -0.5
NEG = -1e30
EPS = 1e-6
CHUNK = 512
NK, PH, TOPK = 128, 8, 16
SLOTS = PH * TOPK
LISTS = 2 * PH
RECTS = [(0, 1, 16), (1, 1, 8), (2, 2, 5), (4, 4, 3), (8, 8, 1)]
assert all(any(a0 <= a < a0 + na and b < nb for a0, na, nb in RECTS)
           for a in range(TOPK) for b in range(TOPK) if (a + 1) * (b + 1) <= TOPK)
RECTS_AT = [(a, na, nb, sum(m * n for _, m, n in RECTS[:i])) for i, (a, na, nb) in enumerate(RECTS)]
CAND = sum(m * n for _, m, n in RECTS)
LOW = -3e38
FAR = 96
UR, VR = 4, 8
QUAD = 4
STEPS = SLOTS // QUAD
def HEAD(step, lag):
    h, rest = divmod(step - 3 - lag, 3)
    return h if rest == 0 and 0 <= h < PH else None
PROMPT_SLOTS = TILES * SLOTS

PER_TILE = {
    "full4": 9, "full5": 9, "free4": 9, "free5": 9,
    "stat": 1, "std": 1, "rstd": 1, "hn": 1, "hn_kept": 1,
    "u_used": SLOTS, "v_used": SLOTS, "gelu": SLOTS // QUAD, "w": SLOTS // QUAD, "diag": SLOTS,
    "residual": 1, "acc_full": 1, "acc_free": 1, "ystat": 2, "ysum": 1, "ystd": 1, "yrstd": 1, "y_out": 16,
    "idx": SLOTS // QUAD, "gexp_in": 1, "gexp": 1, "chosen": PH, "listed": PH, "gated": 1, "y_ready": 1,
    "dve": 245,
    **{f"u_landed{j}": 16 * SLOTS // UR for j in range(UR)},
    **{f"v_landed{j}": 16 * SLOTS // VR for j in range(VR)},
}

class Ledger:

    def __init__(self):
        self.n, self.loops = {}, []

    def at(self, name):
        v = self.n.get(name, 0)
        for var, per in self.loops:
            if per.get(name, 0):
                v = var * per[name] + v
        return v

    def up(self, name, by=1):
        self.n[name] = self.n.get(name, 0) + by
        return self.at(name)

    @contextmanager
    def loop(self, eng, trips, per):
        start = dict(self.n)
        with eng.Fori(0, trips) as var:
            self.loops.append((var, per))
            yield var
            self.loops.pop()
        for name in self.n:
            turn = self.n[name] - start.get(name, 0)
            assert turn in (0, per.get(name, 0)), (name, turn, per.get(name, 0))
            if turn:
                self.n[name] = start.get(name, 0) + trips * turn


def hybrid_step_kernel(nc, x_p, x_s, cak, cav, cbk, cbv, g_mix, w_in, w_a, w_b, w_o, sink, g_ffn, w_pq, subk,
                       pu, pv, g_fin, masks_d, rope_d, sbias_d, ident_d, iota_d,
                       y_p, y_s, akp, avp, bkp, bvp, aks, avs, bks, bvs):
    f32, u32 = mybir.dt.float32, mybir.dt.uint32
    ALU, ACT, AX = mybir.AluOpType, mybir.ActivationFunctionType, mybir.AxisListType
    ds = bass.ds
    q_scratch = nc.dram_tensor("q_scratch", (DEC, WA + WB), f32).ap()
    hn_scratch = nc.dram_tensor("hn_scratch", (DEC, D), f32).ap()

    with ExitStack() as ctx:
        def sb(name, shape, dt=f32):
            return ctx.enter_context(nc.sbuf_tensor(name, shape, dt))

        KTW, KBTW = (WA // P) * SEQ, KVB * SEQ
        arena = sb("arena", [P, ALL * ZW + KTW + KBTW])
        Z = arena[:, 0:ALL * ZW].rearrange("p (t n) -> p t n", t=ALL)
        KT = arena[:, ALL * ZW:ALL * ZW + KTW].rearrange("p (c n) -> p c n", c=WA // P)
        KBT = arena[:, ALL * ZW + KTW:ALL * ZW + KTW + KBTW].rearrange("p (g n) -> p g n", g=KVB)
        GT = sb("GT", [P, ALL, 2 * D])
        WR = sb("WR", [P, 16 * D])
        XS = sb("XS", [P, KO * ALL * P])
        PP = sb("PP", [P, 2 * D])
        GF = sb("GF", [P, 2 * D])
        ident = sb("ident", [P, P])
        skT = sb("skT", [P, 2, NK])
        iota = sb("iota", [P, CAND])
        gmix = sb("gmix", [P, KO])
        nsink = sb("nsink", [P, HB])
        nsink_bh = sb("nsink_bh", [DEC * HB, 1])
        stats = sb("stats", [P, 96])
        e_all = sb("e_all", [P, ALL, SLOTS], u32)
        gate_all = sb("gate_all", [P, ALL, SLOTS])
        idxq = sb("idxq", [P, 4, QUAD], u32)
        dots = sb("dots", [P, 2, QUAD])
        gelus = sb("gelus", [P, 2, QUAD])
        wq = sb("wq", [P, 2, QUAD])

        GTf = GT[:, :, :].rearrange("p t n -> p (t n)")

        def row(t, lo, hi):
            return GTf[:, ds(t * (2 * D) + lo, hi - lo)]

        def slots(buf, t):
            return buf[:, :, :].rearrange("p t n -> p (t n)")[:, ds(t * SLOTS, SLOTS)]

        xT = XS[:, :].rearrange("p (k n) -> p k n", k=KO)
        ring = [WR[:, i * KO * CHUNK:(i + 1) * KO * CHUNK].rearrange("p (k n) -> p k n", k=KO) for i in range(2)]
        w_ab = WR[:, 8 * D:16 * D].rearrange("p (k n) -> p k n", k=8)
        w_out = WR[:, 0:8 * D].rearrange("p (k n) -> p k n", k=KO)
        w_q = WR[:, :].rearrange("p (k n) -> p k n", k=KO)
        KD = XS[:, 0:TILES * 4 * HD].rearrange("p (t g c d) -> p t g c d", t=TILES, g=KVB, c=2)
        O = XS[:, 2 * D:3 * D]
        qT = XS[:, 3 * D:4 * D].rearrange("p (k n) -> p k n", k=KO)
        oT = [Z[:, t, 0:D].rearrange("p (k n) -> p k n", k=KO) for t in range(TILES)]
        mT = O.rearrange("p (k n) -> p k n", k=KO)
        Pr = PP[:, 0:D].rearrange("p (a n) -> p a n", a=2)
        PrT = PP[:, D:2 * D].rearrange("p (a n) -> p a n", a=2)
        maskA = GF[:, 0:4 * P]
        maskB = GF[:, 4 * P:6 * P]
        rope = GF[:, 768:768 + ALL * 2 * HD].rearrange("p (t c d) -> p t c d", t=ALL, c=2)
        sbias = GF[0:DEC * HB, 1408:2048]
        WQ0 = 3
        wq0 = [arena[:, a:a + 2 * D].rearrange("p (k n) -> p k n", k=KO) for a in (3 * ZW + D, 3 * ZW + 3 * D, 0)]
        gffn, gfin = GF[:, 0:D], GF[:, D:2 * D]
        KVW = 3 * WA + 2 * WK
        SA = WR[:, 8 * D:16 * D]
        kv = [SA[:, i * KVW:(i + 1) * KVW] for i in range(2)]
        values_at = [WR[:, i * 2 * D:i * 2 * D + KVW] for i in range(4)]
        values_at = kv + values_at + kv
        s0 = 2 * KVW
        prod = SA[:, s0:s0 + 3 * WA]
        qbc = [SA[:, s0 + 3 * WA + i * D:s0 + 3 * WA + (i + 1) * D] for i in range(2)]
        s1 = s0 + 3 * WA + 2 * D
        sS = SA[:, s1:s1 + 5 * 64].rearrange("p (c n) -> p c n", c=5)
        sP = SA[0:64, s1 + 320:s1 + 320 + 640]
        sPT = SA[:, s0:s0 + 320].rearrange("p (c n) -> p c n", c=5)
        qpT = XS[:, 0:4 * P].rearrange("p (b c n) -> p b c n", b=2, c=2)
        Ssc = XS[:, 4 * P:8 * P].rearrange("p (b c n) -> p b c n", b=2, c=2)
        hnT = XS[:, 4 * D:5 * D].rearrange("p (k n) -> p k n", k=KO)
        hnF = PP[:, 0:D]
        topv = PP[:, D:D + 256].rearrange("p (h c k) -> p h c k", h=PH, c=2)
        topi = PP[:, D + 256:D + 512].bitcast(u32).rearrange("p (h c k) -> p h c k", h=PH, c=2)
        best = PP[:, D + 512:D + 640].rearrange("p (h k) -> p h k", h=PH)
        bpos = PP[:, D + 640:D + 768].bitcast(u32).rearrange("p (h k) -> p h k", h=PH)
        bposf = PP[:, D + 768:D + 896].rearrange("p (h k) -> p h k", h=PH)
        eF = PP[:, D + 896:D + 1024]
        U = [arena[:, j * D:(j + 1) * D] for j in range(UR)]
        V = [arena[:, (UR + j) * D:(UR + j + 1) * D] for j in range(VR)]
        c0 = (UR + VR) * D
        diag = arena[:, c0:c0 + 8 * P].rearrange("p (j n) -> p j n", j=8)
        cs = arena[:, c0 + D:c0 + D + PH * CAND].rearrange("p (h c) -> p h c", h=PH)
        ce = arena[:, c0 + D + PH * CAND:c0 + D + 2 * PH * CAND].rearrange("p (h c) -> p h c", h=PH)
        gexp = arena[:, c0 + 2 * D - 160:c0 + 2 * D - 32].rearrange("p (h k) -> p h k", h=PH)
        topif = arena[:, c0 + 2 * D - 160:c0 + 2 * D + 96].rearrange("p (h c k) -> p h c k", h=PH, c=2)
        eq = XS[:, D:D + TOPK * CAND].rearrange("p (k c) -> p k c", k=TOPK)
        hbc = [XS[:, j * D:(j + 1) * D] for j in range(4)]
        ss, std, rstd = stats[:, 0:5], stats[:, 5:10], stats[:, 10:15]
        nm, den, rden, es = stats[:, 16:32], stats[:, 32:48], stats[:, 48:64], stats[:, 64:72]
        hss, hstd, hrstd = stats[:, 72:73], stats[:, 73:74], stats[:, 74:75]
        yss, ysum, ystd, yrstd = stats[:, 76:78], stats[:, 78:79], stats[:, 79:80], stats[:, 80:81]
        gsum = stats[:, 82:90]
        epsc = stats[:, 90:91]
        zero_col = sb("zero_col", [1, P])
        oTs = sb("oTs", [P, KO, DEC])
        assert D + 2 * PH * CAND <= 2 * D - 160
        assert 3 * ZW + 5 * D <= c0
        idxT = sb("idxT", [P, DEC], u32)
        gateT = sb("gateT", [P, DEC])
        sdots = sb("sdots", [P, 3, DEC])
        WM = sb("WM", [P, DEC, DEC])

        bank = [ctx.enter_context(nc.psum_tensor(f"bank{i}", [P, CHUNK], f32)) for i in range(8)]

        names = {}

        def sem(name):
            if name not in names:
                names[name] = ctx.enter_context(nc.semaphore(name))
            return names[name]

        full = [sem(f"full{i}") for i in range(8)]
        free = [sem(f"free{i}") for i in range(8)]
        for n in ("x_in", "const_in", "w_in0", "w_in1", "wab_in", "wout_in", "wq_in", "gf_in", "x_zero", "copies",
                  "stat", "std", "rstd", "xs", "rot", "stores", "probs", "pt", "pv", "onorm", "merged", "x_again",
                  "h", "dve", "kvzero", "q_out", "kv_in0", "kv_in1", "q_in0", "q_in1", "qk", "sP", "sE", "sW", "sO",
                  "sT", "hn", "hn_kept", "u_used", "v_used", "gelu", "w", "diag", "residual", "acc_full", "acc_free",
                  "ystat", "ysum", "ystd", "yrstd", "y_out", "idx", "gexp_in", "gexp", "chosen", "y_ready", "act",
                  "hn_out", "wq0_in0", "wq0_in1", "wq0_in2", "listed", "gated", "id_in", "rot_s", "hb_in0", "hb_in1", "hb_in2", "hb_in3", "esink", "sd", "sg", "swm", "tT", "kd", "v_in2", "v_in3", "v_in4", "v_in5", "oT_zero", "eps"):
            sem(n)
        S = names
        u_landed = [sem(f"u_landed{j}") for j in range(UR)]
        v_landed = [sem(f"v_landed{j}") for j in range(VR)]

        block = ctx.enter_context(nc.Block())

        w_in_v = w_in.rearrange("(k p) n -> p k n", p=P)
        w_a_v = w_a.rearrange("(k p) n -> p k n", p=P)
        w_b_v = w_b.rearrange("(k p) n -> p k n", p=P)
        w_o_v = w_o.rearrange("(k p) n -> p k n", p=P)
        w_pq_v = w_pq.rearrange("(k p) n -> p k n", p=P)
        PAIR_AT = [0, 2 * CHUNK, ZW, ZW + 2 * CHUNK]
        XLOADS, CONSTS = 16 * ALL, 16 * 14


        @block.sync
        def _(sp):
            L = Ledger()
            for t in range(TILES):
                sp.dma_start(GT[:, t, 0:D], x_p[t * P:(t + 1) * P, :]).then_inc(S["x_in"], 16)
            sp.wait_ge(S["x_zero"], 1)
            sp.dma_start(GT[0:DEC, SAMPLE, 0:D], x_s).then_inc(S["x_in"], 16)
            sp.dma_start(ident[:, :], ident_d).then_inc(S["id_in"], 16)
            sp.dma_start(gmix[:, :], g_mix.rearrange("(k p) -> p k", p=P), allow_slow_non_contiguous=True).then_inc(S["id_in"], 16)
            sp.dma_start(ring[1][:, :, 0:2 * WK], w_in_v[:, :, KB:KB + 2 * WK]).then_inc(S["w_in1"], 16)
            sp.dma_start(ring[0], w_in_v[:, :, 0:CHUNK]).then_inc(S["w_in0"], 16)
            sp.dma_start(GF[:, 0:768], masks_d).then_inc(S["const_in"], 16)
            sp.dma_start(GF[:, 768:1408], rope_d).then_inc(S["const_in"], 16)
            sp.dma_start(sbias, sbias_d).then_inc(S["const_in"], 16)
            sp.dma_start(iota[:, :], iota_d.partition_broadcast(P)).then_inc(S["const_in"], 16)
            sp.dma_start(nsink[:, :], sink.partition_broadcast(P)).then_inc(S["const_in"], 16)
            for b in range(DEC):
                sp.dma_start(nsink_bh[b * HB:(b + 1) * HB, :], sink.rearrange("(h o) -> h o", o=1)).then_inc(S["const_in"], 16)
            sp.dma_start(skT[:, :, :], subk.rearrange("c n d -> n c d")).then_inc(S["const_in"], 16)

            copies = [(c[b], o[b]) for b in range(DEC) for c, o in ((cak, aks), (cav, avs))]

            def copy_a():
                src, dst = copies.pop(0)
                n = (PAST - DEC_NEW) * WA // 64
                sp.dma_start(dst[0:PAST - 1, :].rearrange("s n -> (s n)").rearrange("(a n) -> a n", n=n),
                             src[1:PAST, :].rearrange("s n -> (s n)").rearrange("(a n) -> a n", n=n)).then_inc(S["copies"], 16)

            DEC_NEW = 1
            sp.dma_start(bks[:, 0:P - 1, :], cbk[:, 1:P, :]).then_inc(S["copies"], 16)
            sp.dma_start(bvs[:, 0:P - 1, :], cbv[:, 1:P, :]).then_inc(S["copies"], 16)

            def chunk(p, c):
                if p or c:
                    sp.wait_ge(full[6], 2 * p + c)
                    sp.dma_start(ring[c], w_in_v[:, :, PAIR_AT[p] + c * CHUNK:PAIR_AT[p] + (c + 1) * CHUNK])\
                        .then_inc(S[f"w_in{c}"], 16)
                copy_a()

            for p in range(3):
                for c in range(2):
                    chunk(p, c)
            sp.wait_ge(S["rot_s"], 1)
            sp.dma_start(aks[:, PAST - 1, :], Z[0:DEC, SAMPLE, KA:KA + WA]).then_inc(S["q_out"], 16)
            sp.dma_start(avs[:, PAST - 1, :], Z[0:DEC, SAMPLE, VA:VA + WA]).then_inc(S["q_out"], 16)
            sp.dma_start(bks[:, P - 1, :], Z[0:DEC, SAMPLE, KB:KB + WK]).then_inc(S["q_out"], 16)
            sp.dma_start(bvs[:, P - 1, :], Z[0:DEC, SAMPLE, VB:VB + WK]).then_inc(S["q_out"], 16)
            sp.dma_start(q_scratch[:, 0:WA], Z[0:DEC, SAMPLE, QA:QA + WA]).then_inc(S["q_out"], 16)
            sp.dma_start(q_scratch[:, WA:WA + WB], Z[0:DEC, SAMPLE, QB:QB + WB]).then_inc(S["q_out"], 16)
            sp.wait_ge(S["q_out"], 96)
            sp.wait_ge(S["kvzero"], 2)
            def store(t):
                sp.wait_ge(S["rot"], t + 1)
                rows = slice(t * P, (t + 1) * P)
                sp.dma_start(akp[rows, :], Z[:, t, KA:KA + WA]).then_inc(S["stores"], 16)
                sp.dma_start(avp[rows, :], Z[:, t, VA:VA + WA]).then_inc(S["stores"], 16)
                if t == TILES - 1:
                    sp.dma_start(bkp, Z[:, t, KB:KB + WK]).then_inc(S["stores"], 16)
                    sp.dma_start(bvp, Z[:, t, VB:VB + WK]).then_inc(S["stores"], 16)

            for i in range(2 * DEC):
                if i in (3, 6):
                    chunk(3, i // 6)
                b, r = i % DEC, i % 2
                ca, cb, na, nb = (cak, cbk, aks, bks) if i < DEC else (cav, cbv, avs, bvs)
                k, sem_kv = kv[r], S[f"kv_in{r}"]
                if 2 <= i <= DEC + 1:
                    sp.wait_ge(S["qk"], i - 1)
                elif DEC < i and b < 6:
                    sp.wait_ge(full[6], 9)
                    k, sem_kv = values_at[b], S[f"v_in{b}"]
                elif DEC < i:
                    sp.wait_ge(S["sO"], b - 5)
                sp.dma_start(k[:, 0:WA], ca[b, PAST - P:PAST, :]).then_inc(sem_kv, 16)
                sp.dma_start(k[0:FAR, WA:2 * WA], ca[b, PAST - CHUNK:PAST - P:4, :]).then_inc(sem_kv, 16)
                sp.dma_start(k[FAR:FAR + 1, WA:2 * WA], na[b, PAST - 1:PAST, :]).then_inc(sem_kv, 16)
                sp.dma_start(k[0:FAR, 2 * WA:3 * WA], ca[b, 0:PAST - CHUNK:16, :]).then_inc(sem_kv, 16)
                sp.dma_start(k[:, 3 * WA:3 * WA + WK], cb[b, :, :]).then_inc(sem_kv, 16)
                sp.dma_start(k[0:1, 3 * WA + WK:KVW], nb[b, P - 1:P, :]).then_inc(sem_kv, 16)
                if i < DEC:
                    sp.dma_start(qbc[r], q_scratch[b, :].partition_broadcast(P)).then_inc(S[f"q_in{r}"], 16)
                if i in (3, 5, 7, 9):
                    store((i - 3) // 2)
            sp.wait_ge(S["sO"], DEC)
            sp.dma_start(w_ab[:, 0:4, :], w_a_v).then_inc(S["wab_in"], 16)
            sp.dma_start(w_ab[:, 4:8, :], w_b_v).then_inc(S["wab_in"], 16)
            sp.dma_start(w_out, w_o_v).then_inc(S["wout_in"], 16)
            for t in range(TILES):
                copy_a()

            def x_again(t):
                sp.wait_ge(S["merged"], 2 * (t + 1))
                n = P if t < TILES else DEC
                sp.dma_start(GT[0:n, t, D:2 * D], x_p[t * P:(t + 1) * P, :] if t < TILES else x_s).then_inc(S["x_again"], 16)

            def head_weights(h):
                if h >= WQ0:
                    sp.wait_ge(S["listed"], h - WQ0 + 1)
                sp.dma_start(wq0[h % WQ0], w_pq_v[:, :, 2 * h * P:(2 * h + 2) * P]).then_inc(S[f"wq0_in{h % WQ0}"], 16)

            sp.wait_ge(S["onorm"], 2 * TILES)
            sp.dma_start(gffn, g_ffn.partition_broadcast(P)).then_inc(S["gf_in"], 16)
            head_weights(0)
            head_weights(1)
            x_again(0)
            head_weights(2)
            copy_a()
            x_again(1)
            for t in range(1, TILES):
                head_weights(2 * t + 1)
                copy_a()
                if t < TILES - 1:
                    head_weights(2 * t + 2)
                x_again(t + 1)
            sp.wait_ge(S["h"], 2 * ALL)
            for c in range(4):
                sp.dma_start(w_q[:, :, c * CHUNK:(c + 1) * CHUNK], w_pq_v[:, :, c * CHUNK:(c + 1) * CHUNK]).then_inc(S["wq_in"], 16)
            sp.dma_start(gfin, g_fin.partition_broadcast(P)).then_inc(S["gf_in"], 16)
            while copies:
                copy_a()
            with L.loop(sp, TILES - 1, PER_TILE) as t:
                sp.wait_ge(S["y_ready"], L.up("y_ready"))
                sp.dma_start(y_p[ds(t * P, P), :], GTf[:, ds(t * (2 * D) + D, D)]).then_inc(S["y_out"], 16)
            sp.wait_ge(S["hn_kept"], ALL)
            sp.dma_start(hn_scratch, GT[0:DEC, SAMPLE, 0:D]).then_inc(S["hn_out"], 16)
            sp.wait_ge(S["hn_out"], 16)
            sp.wait_ge(S["gated"], ALL)
            for b in range(DEC):
                if b >= 4:
                    sp.wait_ge(S["u_used"], UR + PROMPT_SLOTS + b - 3)
                sp.dma_start(hbc[b % 4], hn_scratch[b, :].partition_broadcast(P)).then_inc(S[f"hb_in{b % 4}"], 16)
            sp.wait_ge(S["y_ready"], TILES)
            sp.dma_start(y_p[SEQ - P:SEQ, :], GT[:, TILES - 1, D:2 * D]).then_inc(S["y_out"], 16)
            sp.wait_ge(S["y_ready"], ALL)
            sp.dma_start(y_s, GT[0:DEC, SAMPLE, D:2 * D]).then_inc(S["y_out"], 16)
            sp.wait_ge(S["y_out"], 16 * ALL)
            sp.wait_ge(S["stores"], 16 * (2 * TILES + 2))
            sp.wait_ge(S["copies"], 16 * 18)

        @block.gpsimd
        def _(pool):
            L = Ledger()
            nc.gpsimd.memset(GT[:, SAMPLE, 0:D], 0.0).then_inc(S["x_zero"], 1)
            nc.gpsimd.memset(epsc, EPS).then_inc(S["eps"], 1)
            nc.gpsimd.memset(WM[:, :, :], 0.0).then_inc(S["eps"], 1)
            nc.gpsimd.memset(kv[0], 0.0).then_inc(S["kvzero"], 1)
            nc.gpsimd.memset(kv[1], 0.0).then_inc(S["kvzero"], 1)

            pool.wait_ge(S["h"], 2 * ALL)
            pool.wait_ge(S["listed"], PH)

            def gather(dst, table, idx, landed):
                nc.gpsimd.indirect_dma_start(dst, None, table, bass.IndirectOffsetOnAxis(ap=idx, axis=0))\
                    .then_inc(landed, 16)

            experts = e_all[:, :, :].rearrange("p t n -> p (t n)")
            with L.loop(pool, TILES, PER_TILE) as t:
                for s in range(SLOTS):
                    if s % TOPK == 0:
                        pool.wait_ge(S["chosen"], L.up("chosen"))
                        pool.nop(nofuse=True)
                    if s % QUAD == 0:
                        q = s // QUAD % 4
                        nc.gpsimd.tensor_copy(idxq[:, q, :], experts[:, ds(t * SLOTS + s, QUAD)]).then_inc(S["idx"], 1)
                        pool.wait_ge(S["idx"], L.up("idx"))
                        pool.nop(nofuse=True)
                    pool.wait_ge(S["u_used"], L.up("u_used"))
                    pool.nop(nofuse=True)
                    gather(U[s % UR], pu, idxq[:, q, s % QUAD:s % QUAD + 1], u_landed[s % UR])
                    pool.wait_ge(S["v_used"], L.up("v_used"))
                    pool.nop(nofuse=True)
                    gather(V[s % VR], pv, idxq[:, q, s % QUAD:s % QUAD + 1], v_landed[s % VR])
            pool.wait_ge(S["tT"], 2)
            for b in range(DEC):
                pool.wait_ge(S["u_used"], L.up("u_used"))
                gather(U[b % UR], pu, idxT[:, b:b + 1], u_landed[b % UR])
                pool.wait_ge(S["v_used"], L.up("v_used"))
                gather(V[b], pv, idxT[:, b:b + 1], v_landed[b])

        @block.scalar
        def _(act):
            L = Ledger()
            act.wait_ge(S["x_in"], XLOADS)
            act.wait_ge(S["eps"], 1)
            for t in range(ALL):
                nc.scalar.activation(GT[:, t, D:2 * D], GT[:, t, 0:D], ACT.Square, accum_out=ss[:, t:t + 1])\
                    .then_inc(S["stat"], 1)
            act.wait_ge(S["stat"], ALL)
            nc.scalar.activation(std, ss, ACT.Sqrt, bias=epsc, scale=1.0 / D).then_inc(S["std"], 1)

            for m in range(ALL):
                act.wait_ge(full[2 + m], 1)
                nc.scalar.activation(Z[:, m, KB:KB + 2 * WK], bank[2 + m][:, 0:2 * WK], ACT.Copy).then_inc(free[2 + m], 1)
            zf = arena[:, 0:ALL * ZW]
            with act.Fori(0, 2) as p:
                for c in range(2):
                    for m in range(ALL):
                        act.wait_ge(full[2 + m], p * 2 + (c + 2))
                        nc.scalar.activation(zf[:, ds(p * (2 * CHUNK) + (m * ZW + c * CHUNK), CHUNK)], bank[2 + m][:, :],
                                             ACT.Copy).then_inc(free[2 + m], 1)
            gf = GT[:, :, :].rearrange("p t n -> p (t n)")
            with act.Fori(0, 2) as p:
                for c in range(2):
                    for m in range(ALL):
                        act.wait_ge(full[2 + m], p * 2 + (c + 6))
                        nc.scalar.activation(gf[:, ds(p * D + (m * 2 * D + c * CHUNK), CHUNK)], bank[2 + m][:, :],
                                             ACT.Sigmoid).then_inc(free[2 + m], 1)
            for m in range(ALL):
                L.n[f"full{2 + m}"] = 9
            misc = [0]

            def evac(dst, width=CHUNK, cols=P):
                i = 4 + misc[0] % 2
                misc[0] += 1
                act.wait_ge(full[i], L.up(f"full{i}"))
                nc.scalar.activation(dst, bank[i][:, 0:width].rearrange("p (k n) -> p k n", n=P)[:, :, 0:cols], ACT.Copy)\
                    .then_inc(free[i], 1)

            def skip(n):
                for _ in range(n):
                    L.up(f"full{4 + misc[0] % 2}")
                    misc[0] += 1

            def mix(t, part):
                n = P if t < TILES else DEC
                if part == 0:
                    skip(4)
                else:
                    evac(mT[:, 0:4, 0:n], cols=n)
                    evac(mT[:, 4:8, 0:n], cols=n)
                    skip(2)

            def turned(t):
                cols = slice(t * P, (t + 1) * P)
                evac(qT[:, 0:4, :])
                evac(KT[:, :, cols])
                evac(qT[:, 4:8, :])
                evac(KBT[:, :, cols], 2 * P)

            act.wait_ge(S["sP"], 2)
            nc.scalar.activation(sP[:, 0:384], sP[:, 0:384], ACT.Exp, bias=nm[0:64, 0:1], scale=-1.0,
                                 accum_out=den[0:64, 0:1]).then_inc(S["sE"], 1)
            nc.scalar.activation(sP[:, 384:640], sP[:, 384:640], ACT.Exp, bias=nm[0:64, 1:2], scale=-1.0,
                                 accum_out=den[0:64, 1:2]).then_inc(S["sE"], 1)
            act.wait_ge(S["esink"], 1)
            nc.scalar.activation(es[0:64, 0:1], es[0:64, 0:1], ACT.Exp).then_inc(S["esink"], 1)
            skip(2)
            turned(0)
            for t in range(TILES):
                for hd in range(HA + HB):
                    n = (t + 1) * P if hd < HA else min(t + 1, 2) * P
                    act.wait_ge(free[hd % 2], ALL + 8 * t + hd // 2 + 1)
                    nc.scalar.activation(Pr[:, hd % 2, 0:n], Pr[:, hd % 2, 0:n], ACT.Exp, bias=nm[:, hd:hd + 1], scale=-1.0,
                                         accum_out=den[:, hd:hd + 1]).then_inc(S["probs"], 1)
                    if t == 0 and hd == 2:
                        i = 4 + misc[0] % 2
                        misc[0] += 1
                        act.wait_ge(full[i], L.up(f"full{i}"))
                        nc.scalar.activation(sPT, bank[i][:, 0:320].rearrange("p (c n) -> p c n", c=5), ACT.Copy)\
                            .then_inc(free[i], 1)
                        skip(1)
                act.wait_ge(S["esink"], 2 * t + 3)
                nc.scalar.activation(es, es, ACT.Exp).then_inc(S["esink"], 1)
                if t + 1 < TILES:
                    turned(t + 1)
                if t == 0:
                    act.wait_ge(S["stores"], 16 * (2 * TILES + 2))
                evac(oT[t][:, 0:4, :])
                evac(oT[t][:, 4:8, :])

            def choose(t, step):
                if step == 0:
                    nc.scalar.activation(hnF, row(t, D, 2 * D), ACT.Square, accum_out=hss).then_inc(S["stat"], 1)
                    act.wait_ge(S["stat"], L.up("stat"))
                    nc.scalar.activation(hstd, hss, ACT.Sqrt, bias=epsc, scale=1.0 / D).then_inc(S["std"], 1)
                if step == 1:
                    act.wait_ge(S["hn"], L.up("hn"))
                    nc.scalar.activation(row(t, 0, D), hnF, ACT.Copy).then_inc(S["hn_kept"], 1)
                if step == 2:
                    evac(hnT[:, 0:4, :])
                    evac(hnT[:, 4:8, :])
                if (h := HEAD(step, 2)) is not None:
                    evac(qpT[:, h % 2, :, :], 2 * P)
                if (h := HEAD(step, 4)) is not None:
                    n = L.at("listed")
                    if not (isinstance(n, int) and n < 2):
                        act.wait_ge(S["listed"], n - 1)
                    L.up("listed")
                    evac(Ssc[:, h % 2, :, :], 2 * P)
                if step == STEPS - 1:
                    act.wait_ge(S["gexp_in"], L.up("gexp_in"))
                    nc.scalar.activation(gexp, gexp, ACT.Exp).then_inc(S["gexp"], 1)

            L.n["stat"], L.n["hn"] = ALL, 0
            mix(0, 0)
            mix(0, 1)
            act.wait_ge(S["h"], 2)
            for step in range(STEPS):
                choose(0, step)
                if (h := HEAD(step, 2)) is not None:
                    mix(h // 2 + 1, h % 2)
            act.wait_ge(S["h"], 2 * ALL)

            L.n["u_used"] = UR
            L.n["v_used"] = VR

            with L.loop(act, TILES, PER_TILE) as t:
                for q in range(STEPS):
                    act.wait_ge(S["u_used"], L.up("u_used", QUAD))
                    nc.scalar.activation(gelus[:, q % 2, :], dots[:, q % 2, :], ACT.Gelu).then_inc(S["gelu"], 1)
                    act.wait_ge(S["w"], L.up("w"))
                    act.wait_ge(S["v_used"], L.up("v_used", QUAD) - 2 * QUAD)
                    for j in range(QUAD):
                        nc.scalar.activation(diag[:, QUAD * (q % 2) + j, :], ident[:, :], ACT.Copy,
                                             scale=wq[:, q % 2, j:j + 1]).then_inc(S["diag"], 1)
                    choose(t + 1, q)
                act.wait_ge(S["acc_full"], L.up("acc_full"))
                for c in range(2):
                    nc.scalar.activation(PP[:, 0:CHUNK], bank[6 + c][:, :], ACT.Square, accum_out=yss[:, c:c + 1])\
                        .then_inc(S["ystat"], 1)
                    act.wait_ge(S["ystat"], L.up("ystat"))
                act.wait_ge(S["ysum"], L.up("ysum"))
                nc.scalar.activation(ystd, ysum, ACT.Sqrt, bias=epsc, scale=1.0 / D).then_inc(S["ystd"], 1)
            act.wait_ge(S["u_used"], UR + PROMPT_SLOTS + DEC)
            nc.scalar.activation(sdots[:, 1, :], sdots[:, 0, :], ACT.Gelu).then_inc(S["sg"], 1)
            act.wait_ge(S["acc_full"], L.up("acc_full"))
            for c in range(2):
                nc.scalar.activation(PP[0:DEC, 0:CHUNK], bank[6 + c][0:DEC, :], ACT.Square, accum_out=yss[0:DEC, c:c + 1])\
                    .then_inc(S["ystat"], 1)
                act.wait_ge(S["ystat"], L.up("ystat"))
            act.wait_ge(S["ysum"], L.up("ysum"))
            nc.scalar.activation(ystd[0:DEC, :], ysum[0:DEC, :], ACT.Sqrt, bias=epsc[0:DEC, :], scale=1.0 / D)\
                .then_inc(S["ystd"], 1)

        @block.tensor
        def _(pe):
            L = Ledger()

            def claim(i):
                n = L.at(f"free{i}")
                if not (isinstance(n, int) and n == 0):
                    pe.wait_ge(free[i], n)
                L.up(f"free{i}")

            pe.wait_ge(S["id_in"], 32)
            misc = [0]
            item = {}

            def next_bank():
                i = 4 + misc[0] % 2
                misc[0] += 1
                claim(i)
                return i

            def transpose_x(m):
                pe.wait_ge(S["xs"], m + 1)
                for half in range(2):
                    claim(half)
                    for k in range(4):
                        col = D + (4 * half + k) * P
                        last = nc.tensor.transpose(bank[half][:, k * P:(k + 1) * P], GT[:, m, col:col + P], ident[:, :])
                    last.then_inc(full[half], 1)

            transpose_x(0)
            for m in range(ALL):
                if m + 1 < ALL:
                    transpose_x(m + 1)
                pe.wait_ge(free[0], m + 1)
                pe.wait_ge(free[1], m + 1)
                pe.wait_ge(S["w_in1"], 16)
                for k in range(KO):
                    last = nc.tensor.matmul(bank[2 + m][:, 0:2 * WK], xT[:, k, m * P:(m + 1) * P], ring[1][:, k, 0:2 * WK],
                                            start=(k == 0), stop=(k == KO - 1))
                last.then_inc(full[2 + m], 1)
            with pe.Fori(0, 4) as p:
                for c in range(2):
                    pe.wait_ge(S[f"w_in{c}"], p * 16 + (16 if c == 0 else 32))
                    for m in range(ALL):
                        pe.wait_ge(free[2 + m], p * 2 + (1 + c))
                        for k in range(KO):
                            last = nc.tensor.matmul(bank[2 + m][:, :], xT[:, k, m * P:(m + 1) * P], ring[c][:, k, :],
                                                    start=(k == 0), stop=(k == KO - 1))
                        last.then_inc(full[2 + m], 1)
            for m in range(ALL):
                L.n[f"free{2 + m}"] = 9

            def transposes(src, blocks):
                i = next_bank()
                for k in range(blocks):
                    last = nc.tensor.transpose(bank[i][:, k * P:(k + 1) * P], src[:, k * P:(k + 1) * P], ident[:, :])
                last.then_inc(full[i], 1)
                return i

            def mix(t, part):
                n = P if t < TILES else DEC
                if part == 0:
                    pe.wait_ge(S["wab_in"], 32)
                    if t == SAMPLE:
                        pe.wait_ge(S["sT"], 1)
                    outs = oT[t] if t < TILES else oTs
                    for c in range(2):
                        for br in range(2):
                            i = next_bank()
                            for k in range(4):
                                last = nc.tensor.matmul(bank[i][0:n, :], outs[:, 4 * br + k, :],
                                                        w_ab[:, 4 * br + k, c * CHUNK:(c + 1) * CHUNK],
                                                        start=(k == 0), stop=(k == 3))
                            last.then_inc(full[i], 1)
                    return
                pe.wait_ge(S["merged"], 2 * t + 2)
                for half in range(2):
                    i = next_bank()
                    for k in range(4):
                        col = (4 * half + k) * P
                        last = nc.tensor.transpose(bank[i][:, k * P:k * P + n], GT[0:n, t, col:col + P], ident[0:n, 0:n])
                    last.then_inc(full[i], 1)
                pe.wait_ge(S["wout_in"], 16)
                pe.wait_ge(free[4], L.at("free4"))
                pe.wait_ge(free[5], L.at("free5"))
                for c in range(2):
                    i = next_bank()
                    for k in range(KO):
                        last = nc.tensor.matmul(bank[i][0:n, :], mT[:, k, 0:n], w_out[:, k, c * CHUNK:(c + 1) * CHUNK],
                                                start=(k == 0), stop=(k == KO - 1))
                    last.then_inc(full[i], 1)

            pe.wait_ge(S["qk"], DEC)
            pe.wait_ge(S["const_in"], CONSTS)
            for tiles in ((0, 3), (3, 5)):
                i = next_bank()
                for c in range(*tiles):
                    last = nc.tensor.transpose(bank[i][0:64, (c - tiles[0]) * P:(c - tiles[0] + 1) * P], sS[:, c, :], ident[:, :])
                if tiles[0]:
                    for c in range(2):
                        last = nc.tensor.transpose(bank[i][:, (2 + c) * P:(3 + c) * P], skT[:, c, :], ident[:, :])
                last.then_inc(full[i], 1)

            def sampled(b):
                if b == 0:
                    pe.wait_ge(free[4], L.at("free4"))
                    item["s"] = next_bank()
                i = item["s"]
                v = values_at[b]
                if 2 <= b < 6:
                    pe.wait_ge(S[f"v_in{b}"], 96)
                else:
                    pe.wait_ge(S[f"kv_in{b % 2}"], 96 * (DEC // 2 + b // 6 + 1))
                for pair in range(4):
                    for c in range(3):
                        nc.tensor.matmul(bank[i][:, pair * 64 + b * 8:pair * 64 + b * 8 + 8],
                                         v[:, c * WA + pair * P:c * WA + (pair + 1) * P],
                                         sPT[:, c, b * 8:b * 8 + 8], start=(c == 0), stop=(c == 2))
                for c in range(2):
                    last = nc.tensor.matmul(bank[i][:, 256 + b * 8:256 + b * 8 + 8], v[:, 3 * WA + c * WK:3 * WA + (c + 1) * WK],
                                            sPT[:, 3 + c, b * 8:b * 8 + 8], start=(c == 0), stop=(c == 1))
                last.then_inc(S["sO"], 1)
                if b == DEC - 1:
                    pe.wait_ge(S["sO"], DEC)
                    pe.sem_inc(full[i], 1)

            def turned(t):
                pe.wait_ge(S["rot"], t + 1)
                pe.wait_ge(S["kd"], 2)
                transposes(Z[:, t, QA:QA + WA], 4)
                transposes(Z[:, t, KA:KA + WA], 4)
                transposes(Z[:, t, QB:QB + WB], 4)
                transposes(KD[:, t, :, :, :].rearrange("p g c d -> p (g c d)"), 2)

            turned(0)
            for t in range(TILES):
                pe.wait_ge(free[4], L.at("free4"))
                pe.wait_ge(free[5], L.at("free5"))

                def span(hd):
                    return (0, t + 1) if hd < HA else (max(t - 1, 0), t + 1)

                def score(hd):
                    lo, hi = span(hd)
                    h = hd % 8
                    r = slice(HD * (h % 2), HD * (h % 2) + HD)
                    claim(hd % 2)
                    keys = KT[r, h // 2, lo * P:hi * P] if hd < HA else KBT[r, h // 4, lo * P:hi * P]
                    nc.tensor.matmul(bank[hd % 2][:, 0:(hi - lo) * P], qT[r, (hd // 8) * 4 + h // 2, :], keys,
                                     start=True, stop=True).then_inc(full[hd % 2], 1)

                def turn(hd):
                    lo, hi = span(hd)
                    pe.wait_ge(S["probs"], t * 16 + hd + 1)
                    claim(2 + hd % 2)
                    for k in range(hi - lo):
                        last = nc.tensor.transpose(bank[2 + hd % 2][:, k * P:(k + 1) * P], Pr[:, hd % 2, k * P:(k + 1) * P], ident[:, :])
                    last.then_inc(full[2 + hd % 2], 1)

                def values(hd):
                    lo, hi = span(hd)
                    h = hd % 8
                    if h == 0:
                        claim(6 + hd // 8)
                    pe.wait_ge(free[2 + hd % 2], 9 * (2 + hd % 2 >= 2) + 8 * t + hd // 2 + 1)
                    at = VA + h * HD if hd < HA else VB + (h // 4) * HD
                    for k in range(hi - lo):
                        last = nc.tensor.matmul(bank[6 + hd // 8][:, h * HD:(h + 1) * HD], PrT[:, hd % 2, k * P:(k + 1) * P],
                                                Z[:, lo + k, at:at + HD], start=(k == 0), stop=(k == hi - lo - 1))
                    last.then_inc(S["pv"], 1)

                NH = HA + HB
                score(0)
                for hd in range(NH):
                    if hd + 1 < NH:
                        score(hd + 1)
                    turn(hd)
                    if hd:
                        values(hd - 1)
                    if t == 0 and hd == 2:
                        pe.wait_ge(S["sW"], 2)
                        i = next_bank()
                        for c in range(5):
                            last = nc.tensor.transpose(bank[i][:, c * 64:(c + 1) * 64], sP[:, c * P:(c + 1) * P], ident[0:64, 0:64])
                        last.then_inc(full[i], 1)
                    if t == 0 and hd >= NH - DEC:
                        sampled(hd - (NH - DEC))
                values(NH - 1)
                if t + 1 < TILES:
                    turned(t + 1)
                pe.wait_ge(S["onorm"], 2 * t + 2)
                transposes(O[:, 0:CHUNK], 4)
                transposes(O[:, CHUNK:D], 4)
            pe.wait_ge(free[4], L.at("free4"))
            pe.wait_ge(free[5], L.at("free5"))
            mix(0, 0)
            mix(0, 1)

            def choose(t, step):
                if step == 1:
                    pe.wait_ge(S["hn"], L.up("hn"))
                    transposes(hnF[:, 0:CHUNK], 4)
                    transposes(hnF[:, CHUNK:D], 4)
                if (h := HEAD(step, 3)) is not None:
                    pe.wait_ge(free[item["q"]], L.at(f"free{item['q']}"))
                    i = next_bank()
                    for c in range(2):
                        last = nc.tensor.matmul(bank[i][:, c * P:(c + 1) * P], qpT[:, h % 2, c, :], skT[:, c, :],
                                                start=True, stop=True)
                    last.then_inc(full[i], 1)
                for c in range(2):
                    if (h := HEAD(step, c)) is not None:
                        if h == 0 and c == 0:
                            pe.wait_ge(free[4], L.at("free4"))
                            pe.wait_ge(free[5], L.at("free5"))
                        if c == 0:
                            item["q"] = next_bank()
                        i = item["q"]
                        if isinstance(t, int):
                            pe.wait_ge(S[f"wq0_in{h % WQ0}"], 16 * (h // WQ0 + 1))
                        elif h == 0 and c == 0:
                            pe.wait_ge(S["wq_in"], 64)
                        for k in range(KO):
                            weights = wq0[h % WQ0][:, k, c * P:(c + 1) * P] if isinstance(t, int) else \
                                w_q[:, k, (2 * h + c) * P:(2 * h + c + 1) * P]
                            last = nc.tensor.matmul(bank[i][:, c * P:(c + 1) * P], weights,
                                                    hnT[:, k, :], start=(k == 0), stop=(k == KO - 1))
                        if c:
                            last.then_inc(full[i], 1)

            for step in range(STEPS):
                choose(0, step)
                if (h := HEAD(step, 2)) is not None:
                    mix(h // 2 + 1, h % 2)
            pe.wait_ge(S["h"], 2 * ALL)
            with L.loop(pe, TILES, PER_TILE) as t:
                pe.wait_ge(S["acc_free"], L.up("acc_free"))
                for c in range(2):
                    nc.tensor.matmul(bank[6 + c][:, :], ident[:, :],
                                     row(t, D + c * CHUNK, D + (c + 1) * CHUNK),
                                     start=True, stop=False, skip_group_check=True)
                for s in range(SLOTS):
                    j = s % VR
                    pe.wait_ge(v_landed[j], L.up(f"v_landed{j}", 16))
                    pe.wait_ge(S["diag"], L.up("diag"))
                    for c in range(2):
                        last = nc.tensor.matmul(bank[6 + c][:, :], diag[:, j, :], V[j][:, c * CHUNK:(c + 1) * CHUNK],
                                                start=False, stop=False, skip_group_check=True)
                    last.then_inc(S["v_used"], 1)
                    if s % QUAD == QUAD - 1:
                        choose(t + 1, s // QUAD)
                for c in range(2):
                    last = nc.tensor.matmul(bank[6 + c][:, :], zero_col[0:1, :], gffn[0:1, 0:CHUNK],
                                            start=False, stop=True, skip_group_check=True)
                last.then_inc(S["acc_full"], 1)

            pe.wait_ge(S["gated"], ALL)
            for src in (eF, gate_all[:, SAMPLE, :]):
                i = next_bank()
                nc.tensor.transpose(bank[i][:, 0:P], src, ident[:, :]).then_inc(full[i], 1)
            pe.wait_ge(S["acc_free"], L.up("acc_free"))
            for c in range(2):
                nc.tensor.matmul(bank[6 + c][0:DEC, :], ident[0:DEC, 0:DEC], GT[0:DEC, SAMPLE, D + c * CHUNK:D + (c + 1) * CHUNK],
                                 start=True, stop=False, skip_group_check=True)
            pe.wait_ge(S["swm"], 1)
            for b in range(DEC):
                pe.wait_ge(v_landed[b], L.up(f"v_landed{b}", 16))
                for c in range(2):
                    last = nc.tensor.matmul(bank[6 + c][0:DEC, :], WM[:, b, :], V[b][:, c * CHUNK:(c + 1) * CHUNK],
                                            start=False, stop=(b == DEC - 1), skip_group_check=True)
            last.then_inc(S["acc_full"], 1)

        @block.vector
        def _(dve):
            L = Ledger()

            def mark(ins):
                ins.then_inc(S["dve"], 1)
                L.up("dve")

            def settle():
                dve.wait_ge(S["dve"], L.at("dve"))
            V_ = nc.vector
            mark(V_.memset(zero_col[0:1, :], 0.0))
            dve.sem_inc(S["u_used"], UR)
            dve.sem_inc(S["v_used"], VR)
            dve.sem_inc(S["acc_free"], 1)
            dve.wait_ge(S["std"], 1)
            V_.reciprocal(rstd, std).then_inc(S["rstd"], 1)
            dve.wait_ge(S["rstd"], 1)
            for t in range(ALL):
                V_.tensor_scalar(GT[:, t, D:2 * D], GT[:, t, 0:D], rstd[:, t:t + 1], None, ALU.mult).then_inc(S["xs"], 1)
            dve.wait_ge(S["id_in"], 32)
            for m in range(ALL):
                for half in range(2):
                    dve.wait_ge(full[half], m + 1)
                    V_.tensor_tensor(xT[:, 4 * half:4 * half + 4, m * P:(m + 1) * P],
                                     bank[half][:, :].rearrange("p (k n) -> p k n", k=4),
                                     gmix[:, 4 * half:4 * half + 4].unsqueeze(2).to_broadcast([P, 4, P]), ALU.mult)\
                        .then_inc(free[half], 1)
            L.n["full4"] = L.n["full5"] = 9
            misc = [0]

            def skip(n):
                for _ in range(n):
                    L.up(f"full{4 + misc[0] % 2}")
                    misc[0] += 1

            def arrived():
                i = 4 + misc[0] % 2
                misc[0] += 1
                dve.wait_ge(full[i], L.up(f"full{i}"))
                return i

            def rotate(t):
                for src, heads in ((QA, 2 * HA), (QB, HB + KVB)):
                    z = Z[:, t, src:src + heads * HD].rearrange("p (h d) -> p h d", d=HD)
                    a = PP[:, 0:heads * HD].rearrange("p (h d) -> p h d", d=HD)
                    b = PP[:, D:D + heads * HD].rearrange("p (h d) -> p h d", d=HD)
                    H = HD // 2
                    settle()
                    mark(V_.tensor_tensor(a, z, rope[:, t, 0:1, :].to_broadcast([P, heads, HD]), ALU.mult))
                    mark(V_.tensor_tensor(b[:, :, 0:H], z[:, :, H:HD], rope[:, t, 1:2, 0:H].to_broadcast([P, heads, H]), ALU.mult))
                    mark(V_.tensor_tensor(b[:, :, H:HD], z[:, :, 0:H], rope[:, t, 1:2, H:HD].to_broadcast([P, heads, H]), ALU.mult))
                    settle()
                    mark(V_.tensor_tensor(z, a, b, ALU.add))
                settle()
                dve.sem_inc(S["rot_s" if t == SAMPLE else "rot"], 1)

            def mix(t, part):
                n = P if t < TILES else DEC
                if part == 0:
                    for c in range(2):
                        ga, gb = (GT[0:n, t, br * D + c * CHUNK:br * D + (c + 1) * CHUNK] for br in range(2))
                        for g in (ga, gb):
                            i = arrived()
                            V_.tensor_tensor(g, g, bank[i][0:n, :], ALU.mult).then_inc(free[i], 1)
                        dve.wait_ge(free[4], L.at("full4"))
                        dve.wait_ge(free[5], L.at("full5"))
                        V_.tensor_tensor(ga, ga, gb, ALU.add).then_inc(S["merged"], 1)
                    return
                skip(2)
                dve.wait_ge(S["x_again"], 16 * (t + 1))
                for c in range(2):
                    i = arrived()
                    h = GT[0:n, t, D + c * CHUNK:D + (c + 1) * CHUNK]
                    V_.tensor_tensor(h, h, bank[i][0:n, :], ALU.add).then_inc(free[i], 1)
                dve.wait_ge(free[4], L.at("full4"))
                dve.wait_ge(free[5], L.at("full5"))
                dve.sem_inc(S["h"], 2)

            dve.wait_ge(free[2 + SAMPLE], 5)
            dve.wait_ge(S["const_in"], CONSTS)
            mark(V_.tensor_scalar(nsink[:, :], nsink[:, :], -1.0, None, ALU.mult))
            mark(V_.tensor_scalar(nsink_bh[:, :], nsink_bh[:, :], -1.0, None, ALU.mult))
            rotate(SAMPLE)
            for b in range(DEC):
                k, q = kv[b % 2], qbc[b % 2]
                dve.wait_ge(S[f"kv_in{b % 2}"], 96 * (b // 2 + 1))
                dve.wait_ge(S[f"q_in{b % 2}"], 16 * (b // 2 + 1))
                settle()
                mark(V_.tensor_tensor(prod.rearrange("p (c n) -> p c n", c=3), k[:, 0:3 * WA].rearrange("p (c n) -> p c n", c=3),
                                      q[:, 0:WA].unsqueeze(1).to_broadcast([P, 3, WA]), ALU.mult))
                settle()
                mark(V_.tensor_reduce(sS[:, 0:3, b * 8:b * 8 + 8], prod.rearrange("p (c h d) -> p c h d", c=3, d=HD), AX.X, ALU.add))
                settle()
                for c in range(2):
                    mark(V_.tensor_tensor(prod[:, c * WB:(c + 1) * WB].rearrange("p (g r d) -> p g r d", g=KVB, d=HD),
                                          k[:, 3 * WA + c * WK:3 * WA + (c + 1) * WK].rearrange("p (g d) -> p g d", g=KVB)
                                          .unsqueeze(2).to_broadcast([P, KVB, HB // KVB, HD]),
                                          q[:, WA:WA + WB].rearrange("p (g r d) -> p g r d", g=KVB, d=HD), ALU.mult))
                settle()
                V_.tensor_reduce(sS[:, 3:5, b * 8:b * 8 + 8], prod[:, 0:2 * WB].rearrange("p (c h d) -> p c h d", c=2, d=HD),
                                 AX.X, ALU.add).then_inc(S["qk"], 1)
                dve.wait_ge(S["qk"], b + 1)
                if b % 2 == 0:
                    dve.wait_ge(free[2 + b // 2], 5)
                    rotate(b // 2)
            dve.wait_ge(full[6], 9)
            for c in range(2):
                V_.tensor_copy(KD[:, :, :, c, :], Z[:, 0:TILES, KB:KB + WK].rearrange("p t (g d) -> p t g d", g=KVB))\
                    .then_inc(S["kd"], 1)
            i = arrived()
            V_.tensor_tensor_reduce(out=sP[:, 0:384], in0=bank[i][0:64, 0:384], in1=sbias[:, 0:384], scale=-SCALE, scalar=3e38,
                                    op0=ALU.add, op1=ALU.min, accum_out=nm[0:64, 0:1]).then_inc(S["sP"], 1)
            j = arrived()
            V_.tensor_tensor_reduce(out=sP[:, 384:640], in0=bank[j][0:64, 0:256], in1=sbias[:, 384:640], scale=-SCALE,
                                    scalar=nsink_bh[:, 0:1], op0=ALU.add, op1=ALU.min, accum_out=nm[0:64, 1:2])\
                .then_inc(S["sP"], 1)
            mark(V_.tensor_copy(skT[:, :, :], bank[j][:, 2 * P:4 * P].rearrange("p (c n) -> p c n", c=2)))
            settle()
            dve.wait_ge(S["sP"], 2)
            dve.sem_inc(free[i], 1)
            dve.sem_inc(free[j], 1)
            mark(V_.tensor_tensor(es[0:64, 0:1], nm[0:64, 1:2], nsink_bh[:, :], ALU.subtract))
            settle()
            dve.sem_inc(S["esink"], 1)
            dve.wait_ge(S["esink"], 2)
            mark(V_.tensor_tensor(den[0:64, 1:2], den[0:64, 1:2], es[0:64, 0:1], ALU.add))
            settle()
            mark(V_.reciprocal(rden[0:64, 0:2], den[0:64, 0:2]))
            settle()
            V_.tensor_scalar(sP[:, 0:384], sP[:, 0:384], rden[0:64, 0:1], None, ALU.mult).then_inc(S["sW"], 1)
            V_.tensor_scalar(sP[:, 384:640], sP[:, 384:640], rden[0:64, 1:2], None, ALU.mult).then_inc(S["sW"], 1)
            for m in range(ALL):
                dve.wait_ge(free[2 + m], 9)

            def own():
                skip(1)
                i = arrived()
                for r in range(2):
                    rows = slice(HD * r, HD * r + HD)
                    src = bank[i][rows, 0:4 * 66].rearrange("p (c x) -> p c x", x=66)[:, :, r:r + 57:8]
                    mark(V_.tensor_copy(oTs[rows, 0:4, :], src))
                    for g in range(KVB):
                        src = bank[i][g * HD:(g + 1) * HD, 256:320].rearrange("p (b h) -> p h b", h=HB)[:, 4 * g + r:4 * g + r + 3:2, :]
                        mark(V_.tensor_copy(oTs[rows, 4 + 2 * g:6 + 2 * g, :], src))
                settle()
                dve.sem_inc(S["sT"], 1)
                dve.sem_inc(free[i], 1)

            skip(4)
            for t in range(TILES):

                def scored(hd):
                    lo, hi = (0, t + 1) if hd < HA else (max(t - 1, 0), t + 1)
                    n = (hi - lo) * P
                    mask = maskA[:, 4 * P - n:4 * P] if hd < HA else maskB[:, 2 * P - n:2 * P]
                    dve.wait_ge(full[hd % 2], ALL + 8 * t + hd // 2 + 1)
                    if hd >= 2 or t:
                        dve.wait_ge(full[2 + hd % 2], 9 + 8 * t + hd // 2)
                    V_.tensor_tensor_reduce(out=Pr[:, hd % 2, 0:n], in0=bank[hd % 2][:, 0:n], in1=mask, scale=-SCALE,
                                            scalar=3e38 if hd < HA else nsink[:, hd - HA:hd - HA + 1],
                                            op0=ALU.add, op1=ALU.min, accum_out=nm[:, hd:hd + 1]).then_inc(free[hd % 2], 1)

                def turned(hd):
                    n = (t + 1) * P if hd < HA else min(t + 1, 2) * P
                    dve.wait_ge(full[2 + hd % 2], 9 + 8 * t + hd // 2 + 1)
                    if hd >= 2 or t:
                        dve.wait_ge(S["pv"], 16 * t + hd - 1)
                    V_.tensor_copy(PrT[:, hd % 2, 0:n], bank[2 + hd % 2][:, 0:n]).then_inc(free[2 + hd % 2], 1)

                def normalise(br):
                    hs = slice(8 * br, 8 * br + 8)
                    if br:
                        mark(V_.tensor_tensor(es, nm[:, 8:16], nsink[:, :], ALU.subtract))
                        settle()
                        dve.sem_inc(S["esink"], 1)
                        dve.wait_ge(S["esink"], 2 * t + 4)
                        mark(V_.tensor_tensor(den[:, 8:16], den[:, 8:16], es, ALU.add))
                        settle()
                    else:
                        dve.wait_ge(S["probs"], 16 * t + 8)
                    mark(V_.reciprocal(rden[:, hs], den[:, hs]))
                    settle()
                    dve.wait_ge(S["pv"], 16 * t + 8 * br + 8)
                    V_.tensor_tensor(O[:, br * CHUNK:(br + 1) * CHUNK].rearrange("p (h d) -> p h d", d=HD),
                                     bank[6 + br][:, :].rearrange("p (h d) -> p h d", d=HD),
                                     rden[:, hs].unsqueeze(2).to_broadcast([P, 8, HD]), ALU.mult).then_inc(S["onorm"], 1)
                    dve.wait_ge(S["onorm"], 2 * t + br + 1)
                    dve.sem_inc(free[6 + br], 1)

                scored(0)
                for hd in range(16):
                    if hd + 1 < 16:
                        scored(hd + 1)
                    turned(hd)
                    if hd == 9:
                        normalise(0)
                normalise(1)
                if t == 0:
                    own()
                skip(4 if t + 1 < TILES else 0)
                skip(2)
            mix(0, 0)
            mix(0, 1)

            def best16(lists):
                dve.nop(nofuse=True)
                for src, val, pos in lists:
                    mark(V_.max(val[:, 0:8], src))
                settle()
                dve.nop(nofuse=True)
                for src, val, pos in lists:
                    mark(V_.max_index(pos[:, 0:8], val[:, 0:8], src))
                settle()
                dve.nop(nofuse=True)
                for src, val, pos in lists:
                    mark(V_.match_replace(src, val[:, 0:8], src, LOW))
                settle()
                dve.nop(nofuse=True)
                for src, val, pos in lists:
                    mark(V_.max(val[:, 8:16], src))
                settle()
                dve.nop(nofuse=True)
                for src, val, pos in lists:
                    mark(V_.max_index(pos[:, 8:16], val[:, 8:16], src))
                settle()
                dve.nop(nofuse=True)

            scores_out = [0]

            def choose(t, step):
                if step == 0:
                    dve.wait_ge(S["std"], L.up("std"))
                    mark(V_.reciprocal(hrstd, hstd))
                    settle()
                    V_.scalar_tensor_tensor(hnF, row(t, D, 2 * D), hrstd, gffn, ALU.mult, ALU.mult).then_inc(S["hn"], 1)
                    skip(2)
                if HEAD(step, 2) is not None:
                    skip(1)
                if HEAD(step, 4) is not None:
                    skip(1)
                    scores_out[0] = L.at("full5")
                if (h := HEAD(step, 5)) is not None:
                    dve.wait_ge(free[5], scores_out[0])
                    best16([(Ssc[:, h % 2, c, :], topv[:, h, c, :], topi[:, h, c, :]) for c in range(2)])
                    V_.tensor_copy(topif[:, h, :, :], topi[:, h, :, :]).then_inc(S["listed"], 1)
                    top = topv[:, h, :, :]
                    for a, na, nb, at in RECTS_AT:
                        mark(V_.tensor_tensor(cs[:, h, at:at + na * nb].rearrange("p (a b) -> p a b", a=na),
                                              top[:, 0, a:a + na].unsqueeze(2).to_broadcast([P, na, nb]),
                                              top[:, 1:2, 0:nb].to_broadcast([P, na, nb]), ALU.add))
                    dve.wait_ge(S["listed"], L.up("listed"))
                    dve.nop(nofuse=True)
                    mark(V_.tensor_scalar(topif[:, h, 0, :], topif[:, h, 0, :], float(NK), None, ALU.mult))
                    settle()
                    top = topif[:, h, :, :]
                    for a, na, nb, at in RECTS_AT:
                        mark(V_.tensor_tensor(ce[:, h, at:at + na * nb].rearrange("p (a b) -> p a b", a=na),
                                              top[:, 0, a:a + na].unsqueeze(2).to_broadcast([P, na, nb]),
                                              top[:, 1:2, 0:nb].to_broadcast([P, na, nb]), ALU.add))
                    settle()
                if (h := HEAD(step, 6)) is not None:
                    best16([(cs[:, h, :], best[:, h, :], bpos[:, h, :])])
                    mark(V_.tensor_copy(bposf[:, h, :], bpos[:, h, :]))
                    settle()
                    mark(V_.tensor_tensor(eq, iota[:, :].unsqueeze(1).to_broadcast([P, TOPK, CAND]),
                                          bposf[:, h, :].unsqueeze(2).to_broadcast([P, TOPK, CAND]), ALU.is_equal))
                    settle()
                    mark(V_.tensor_tensor(eq, eq, ce[:, h:h + 1, :].to_broadcast([P, TOPK, CAND]), ALU.mult))
                    settle()
                    mark(V_.tensor_reduce(eF[:, h * TOPK:(h + 1) * TOPK], eq, AX.X, ALU.add))
                    settle()
                    V_.tensor_copy(e_all[:, :, :].rearrange("p t n -> p (t n)")[:, ds(t * SLOTS + h * TOPK, TOPK)],
                                   eF[:, h * TOPK:(h + 1) * TOPK]).then_inc(S["chosen"], 1)
                if step == STEPS - 1:
                    V_.tensor_tensor(gexp, best, best[:, :, 0:1].to_broadcast([P, PH, TOPK]), ALU.subtract)\
                        .then_inc(S["gexp_in"], 1)
                    dve.wait_ge(S["gexp"], L.up("gexp"))
                    mark(V_.tensor_reduce(gsum, gexp, AX.X, ALU.add))
                    settle()
                    mark(V_.reciprocal(gsum, gsum))
                    settle()
                    out = slots(gate_all, t).rearrange("p (h k) -> p h k", h=PH)
                    V_.tensor_tensor(out, gexp, gsum.unsqueeze(2).to_broadcast([P, PH, TOPK]), ALU.mult).then_inc(S["gated"], 1)
                    dve.wait_ge(S["gated"], L.up("gated"))

            dve.wait_ge(S["gf_in"], 16)
            L.n["std"], L.n["rstd"] = 1, 1
            for step in range(STEPS):
                choose(0, step)
                if (h := HEAD(step, 2)) is not None:
                    mix(h // 2 + 1, h % 2)
            dve.wait_ge(S["gf_in"], 32)
            gates = gate_all[:, :, :].rearrange("p t n -> p (t n)")

            def finish(rows, out):
                dve.wait_ge(S["ystat"], L.up("ystat", 2))
                V_.tensor_tensor(ysum[0:rows, :], yss[0:rows, 0:1], yss[0:rows, 1:2], ALU.add).then_inc(S["ysum"], 1)
                dve.wait_ge(S["ystd"], L.up("ystd"))
                mark(V_.reciprocal(yrstd[0:rows, :], ystd[0:rows, :]))
                settle()
                for c in range(2):
                    ins = V_.scalar_tensor_tensor(out[c], bank[6 + c][0:rows, :], yrstd[0:rows, :],
                                                  gfin[0:rows, c * CHUNK:(c + 1) * CHUNK], ALU.mult, ALU.mult)
                    ins.then_inc(S["y_ready"], 1) if c else mark(ins)
                dve.wait_ge(S["y_ready"], L.up("y_ready"))
                dve.sem_inc(S["acc_free"], 1)

            with L.loop(dve, TILES, PER_TILE) as t:
                for q in range(STEPS):
                    for j in range(QUAD):
                        dve.wait_ge(u_landed[j], L.up(f"u_landed{j}", 16))
                        V_.scalar_tensor_tensor(U[j], U[j], 1.0, row(t, 0, D), ALU.mult, ALU.mult,
                                                accum_out=dots[:, q % 2, j:j + 1]).then_inc(S["u_used"], 1)
                    dve.wait_ge(S["gelu"], L.up("gelu"))
                    V_.tensor_tensor(wq[:, q % 2, :], gelus[:, q % 2, :], gates[:, ds(t * SLOTS + q * QUAD, QUAD)], ALU.mult)\
                        .then_inc(S["w"], 1)
                    choose(t + 1, q)
                dve.wait_ge(S["acc_full"], L.up("acc_full"))
                finish(P, [row(t, D + c * CHUNK, D + (c + 1) * CHUNK) for c in range(2)])
            i = arrived()
            V_.tensor_copy(idxT[:, :], bank[i][:, 0:DEC]).then_inc(S["tT"], 1)
            j = arrived()
            V_.tensor_copy(gateT[:, :], bank[j][:, 0:DEC]).then_inc(S["tT"], 1)
            for b in range(DEC):
                dve.wait_ge(u_landed[b % UR], L.up(f"u_landed{b % UR}", 16))
                dve.wait_ge(S[f"hb_in{b % 4}"], 16 * (b // 4 + 1))
                V_.scalar_tensor_tensor(U[b % UR], U[b % UR], 1.0, hbc[b % 4], ALU.mult, ALU.mult,
                                        accum_out=sdots[:, 0, b:b + 1]).then_inc(S["u_used"], 1)
            dve.wait_ge(S["sg"], 1)
            dve.wait_ge(S["tT"], 2)
            V_.tensor_tensor(WM[:, :, :].rearrange("p a b -> p (a b)")[:, 0:64:9], sdots[:, 1, :], gateT[:, :], ALU.mult)\
                .then_inc(S["swm"], 1)
            dve.wait_ge(S["acc_full"], L.up("acc_full"))
            finish(DEC, [GT[0:DEC, SAMPLE, D + c * CHUNK:D + (c + 1) * CHUNK] for c in range(2)])


_INS = ['x_prompt', 'x_sample', 'cache_a_k', 'cache_a_v', 'cache_b_k', 'cache_b_v', 'norm_mix', 'w_in', 'w_branch_a',
        'w_branch_b', 'w_out', 'sink_b', 'norm_ffn', 'w_peer_q', 'peer_sub_keys', 'peer_u', 'peer_v', 'norm_final']
_OUTS = [(1, SEQ, D), (DEC, 1, D), (1, 1, SEQ, HA, HD), (1, 1, SEQ, HA, HD), (1, 1, P, KVB, HD), (1, 1, P, KVB, HD),
         (1, DEC, PAST, HA, HD), (1, DEC, PAST, HA, HD), (1, DEC, P, KVB, HD), (1, DEC, P, KVB, HD)]


def _tables():
    t, s = np.arange(P)[:, None], np.arange(P)[None, :]

    def count_a(off, near):
        n = (near & (off <= 128)).astype(int) + (off % 4 == 0) + (off % 16 == 0)
        return np.where(off >= 0, n, 0)

    def bias(n):
        return np.where(n > 0, np.log(np.maximum(n, 1)) / SCALE, NEG)

    a = [bias(count_a(t - s + P * d, True)) for d in (3, 2, 1, 0)]
    b = [bias(((t - s + P * d >= 0) & (t - s + P * d <= 128)).astype(int)) for d in (1, 0)]
    masks = np.concatenate(a + b, 1).astype(np.float32)
    inv = (10000.0 ** (-np.arange(0, HD, 2, dtype=np.float32) / HD)).astype(np.float32)
    pos = np.stack([np.arange(P) + P * i for i in range(TILES)] + [np.full(P, PAST)], 1).astype(np.float32)
    ang = (pos[:, :, None] * inv).astype(np.float32).astype(np.float64)
    c, sn = np.cos(ang), np.sin(ang)
    rope = np.stack([np.concatenate([c, c], -1), np.concatenate([-sn, sn], -1)], 2).astype(np.float32)
    near = np.arange(PAST - P, PAST)
    mid = np.arange(PAST - CHUNK, PAST - P, 4)
    n = np.zeros((3, P), int)
    n[0] = 1 + (near % 4 == 0) + (near % 16 == 0)
    n[1, :FAR] = 1 + (mid % 16 == 0)
    n[1, FAR] = 3
    n[2, :FAR] = 1
    m = np.zeros((2, P), int)
    m[0] = 1
    m[1, 0] = 1
    sb = np.concatenate([bias(n).reshape(-1), bias(m).reshape(-1)])
    sb = np.tile(sb.astype(np.float32), (DEC * HB, 1))
    return {"masks": masks, "rope": rope.reshape(P, -1), "sbias": sb, "ident": np.eye(P, dtype=np.float32),
            "iota": np.arange(CAND, dtype=np.float32)}


def kernel(**inputs):
    import concourse.bacc as _bacc
    from concourse import mybir as _mybir
    from concourse.bass_utils import run_bass_kernel_spmd as _run

    nc = _bacc.Bacc("TRN2", target_bir_lowering=False, num_devices=1)
    arrays, args = {}, []
    named = [(n, np.ascontiguousarray(inputs[n])) for n in _INS] + list(_tables().items())
    for name, a in named:
        arrays[f"in_{name}_dram"] = a
        args.append(nc.dram_tensor(f"in_{name}_dram", a.shape, _mybir.dt.from_np(a.dtype), kind="ExternalInput").ap())
    for i, shape in enumerate(_OUTS):
        args.append(nc.dram_tensor(f"out_{i}_dram", shape, _mybir.dt.float32, kind="ExternalOutput").ap())
    ways = ["o s d -> (o s) d", "b o d -> (b o) d"] + ["o b s h d -> (o b) s (h d)"] * 4
    ways += ["o d -> (o d)"] + ["o k n -> (o k) n"] * 4 + ["o h -> (o h)", "o d -> (o d)", "o k n -> (o k) n",
                                                        "o c n d -> (o c) n d", "o e d -> (o e) d", "o e d -> (o e) d"]
    ways += [None] * 6
    ways += ["o s d -> (o s) d", "b o d -> (b o) d"] + ["o b s h d -> (o b s) (h d)"] * 4 + ["o b s h d -> (o b) s (h d)"] * 4
    assert len(ways) == len(args)
    hybrid_step_kernel(nc, *[a if w is None else a.rearrange(w) for a, w in zip(args, ways)])
    r = _run(nc, [arrays], core_ids=[0])
    return tuple(r.results[0][f"out_{i}_dram"] for i in range(len(_OUTS)))
```
